# Optimizing a Trainium2 kernel written in Bass

```python
import math
import jax, jax.numpy as jnp
from jax import lax
import numpy as np

D_MODEL = 1024
BATCH = 1
SEQ = 2048
DEPTH = 1
DEC_BATCH = 8
DEC_SEQ = 1
PAST_LEN = 8192
PAGE_SIZE = 128

HEAD_DIM = 64
BLOCK = 128
POOL_WINDOWS = (2, 4, 8, 16)
N_POOL_GROUPS = 4
POOL_GROUP = D_MODEL // 16
W_POOL = N_POOL_GROUPS * POOL_GROUP
POOL_BUF = 15
DIL_CONFIGS = ((128, 1), (512, 4), (2048, 16))
DIL_MAX = 2048
N_HEADS_DIL = 6
W_DIL = N_HEADS_DIL * HEAD_DIM
W_CONV = D_MODEL // 4
CONV_WIDTH = 3
CONV_BUF = CONV_WIDTH - 1
N_HEADS_SWA = 4
N_KV_SWA = 2
GQA_GROUP = N_HEADS_SWA // N_KV_SWA
W_SWA = N_HEADS_SWA * HEAD_DIM
W_SWA_KV = N_KV_SWA * HEAD_DIM
SWA_WINDOW = 128
D_MIX = W_POOL + W_DIL + W_CONV + W_SWA
PROJ_SIZES = (W_POOL, W_POOL,
              W_DIL, W_DIL, W_DIL, W_DIL,
              W_CONV, W_CONV, W_CONV, W_CONV,
              W_SWA, W_SWA_KV, W_SWA_KV, W_SWA)
D_PROJ = 2 * W_POOL + 4 * W_DIL + 4 * W_CONV + 2 * W_SWA + 2 * W_SWA_KV
RMS_EPS = 1e-6

kernel_name = "hymba_pool_dilated_conv_swa_step"

def _split_proj(z):
    out, off = [], 0
    for n in PROJ_SIZES:
        out.append(z[..., off:off + n])
        off += n
    return out

def _rmsnorm(x, g):
    xf = x.astype(jnp.float32)
    y = xf * lax.rsqrt(jnp.mean(xf * xf, axis=-1, keepdims=True) + RMS_EPS)
    return y.astype(x.dtype) * g

def _alibi_slopes(n):
    return jnp.exp2(-8.0 * jnp.arange(1, n + 1, dtype=jnp.float32) / n)

def _band_attention(q, k, v, slopes, dist_scale, sink=None):
    n, l, hk, g, dh = q.shape
    nb = -(-l // BLOCK)
    pad = nb * BLOCK - l
    qb = jnp.pad(q, ((0, 0), (0, pad), (0, 0), (0, 0), (0, 0))).reshape(n, nb, BLOCK, hk, g, dh)
    kp = jnp.pad(k, ((0, 0), (BLOCK, pad), (0, 0), (0, 0))).reshape(n, nb + 1, BLOCK, hk, dh)
    vp = jnp.pad(v, ((0, 0), (BLOCK, pad), (0, 0), (0, 0))).reshape(n, nb + 1, BLOCK, hk, dh)
    kw = jnp.concatenate([kp[:, :-1], kp[:, 1:]], axis=2)
    vw = jnp.concatenate([vp[:, :-1], vp[:, 1:]], axis=2)
    s = jnp.einsum("nbqhgd,nbkhd->nbhgqk", qb, kw,
                   preferred_element_type=jnp.float32) * (1.0 / math.sqrt(dh))
    qi = jnp.arange(BLOCK)[:, None]
    kj = jnp.arange(2 * BLOCK)[None, :] - BLOCK
    off = qi - kj
    kpos = (jnp.arange(nb) * BLOCK)[:, None, None] + kj[None]
    valid = (off >= 0) & (off <= BLOCK) & (kpos >= 0)
    bias = -(slopes * dist_scale)[:, :, None, None] * off.astype(jnp.float32)
    s = jnp.where(valid[None, :, None, None], s + bias, -jnp.inf)
    m = jnp.max(s, axis=-1)
    if sink is not None:
        m = jnp.maximum(m, sink[:, :, None])
    p = jnp.exp(s - m[..., None])
    den = jnp.sum(p, axis=-1)
    if sink is not None:
        den = den + jnp.exp(sink[:, :, None] - m)
    o = jnp.einsum("nbhgqk,nbkhd->nbqhgd", p.astype(v.dtype), vw,
                   preferred_element_type=jnp.float32)
    o = o / jnp.moveaxis(den, -1, 2)[..., None]
    lse = jnp.moveaxis(m + jnp.log(den), -1, 2)
    o = o.reshape(n, nb * BLOCK, hk, g, dh)[:, :l].astype(q.dtype)
    lse = lse.reshape(n, nb * BLOCK, hk, g)[:, :l]
    return o, lse

def _gather_attention(q, kc, vc, dists, slopes, sink=None):
    n, t, hk, g, dh = q.shape
    r = kc.shape[1]
    idx = (r - t + jnp.arange(t))[:, None] - dists[None, :]
    valid = idx >= 0
    idx = jnp.clip(idx, 0, r - 1)
    kg = kc[:, idx]
    vg = vc[:, idx]
    s = jnp.einsum("nthgd,ntjhd->nthgj", q, kg,
                   preferred_element_type=jnp.float32) * (1.0 / math.sqrt(dh))
    s = s - slopes[:, :, None] * dists.astype(jnp.float32)
    s = jnp.where(valid[None, :, None, None, :], s, -jnp.inf)
    m = jnp.max(s, axis=-1)
    if sink is not None:
        m = jnp.maximum(m, sink)
    p = jnp.exp(s - m[..., None])
    den = jnp.sum(p, axis=-1)
    if sink is not None:
        den = den + jnp.exp(sink - m)
    o = jnp.einsum("nthgj,ntjhd->nthgd", p.astype(vc.dtype), vg,
                   preferred_element_type=jnp.float32) / den[..., None]
    return o.astype(q.dtype), m + jnp.log(den)

def _mix_dilations(outs, lses):
    w = jax.nn.softmax(jnp.stack(lses, axis=0), axis=0)
    return jnp.einsum("cnlh,cnlhd->nlhd", w, jnp.stack(outs, axis=0).astype(jnp.float32))

def _fold(a, d):
    n, l, h, dh = a.shape
    return a.reshape(n, l // d, d, h, dh).transpose(0, 2, 1, 3, 4).reshape(n * d, l // d, h, dh)

def _dilated_prompt(q, k, v, slopes):
    n, l, h, dh = q.shape
    outs, lses = [], []
    for window, d in DIL_CONFIGS:
        o, lse = _band_attention(_fold(q, d)[:, :, :, None], _fold(k, d), _fold(v, d),
                                 slopes[:, None], d)
        outs.append(o[:, :, :, 0].reshape(n, d, l // d, h, dh).transpose(0, 2, 1, 3, 4)
                    .reshape(n, l, h, dh))
        lses.append(lse[..., 0].reshape(n, d, l // d, h).transpose(0, 2, 1, 3).reshape(n, l, h))
    return _mix_dilations(outs, lses)

def _dilated_decode(q, kc, vc, slopes):
    outs, lses = [], []
    for window, d in DIL_CONFIGS:
        dists = d * jnp.arange(window // d + 1)
        o, lse = _gather_attention(q[:, :, :, None], kc, vc, dists, slopes[:, None])
        outs.append(o[:, :, :, 0])
        lses.append(lse[..., 0])
    return _mix_dilations(outs, lses)

def _pool_mix(u_ext, t, w_pool, pool_scale):
    n, r, _ = u_ext.shape
    uf = u_ext.astype(jnp.float32).reshape(n, r, N_POOL_GROUPS, POOL_GROUP)
    cs = jnp.concatenate([jnp.zeros_like(uf[:, :1]), jnp.cumsum(uf, axis=1)], axis=1)
    i = jnp.arange(r - t, r)
    means = []
    for gi, w in enumerate(POOL_WINDOWS):
        csg = cs[:, :, gi]
        s = csg[:, i + 1] - csg[:, jnp.maximum(i + 1 - w, 0)]
        means.append(s / jnp.minimum(i + 1, w).astype(jnp.float32)[None, :, None])
    diff = (jnp.stack(means, axis=2) - uf[:, r - t:]).astype(u_ext.dtype)
    y = jnp.einsum("ntgc,gce->ntge", diff, w_pool).reshape(n, t, W_POOL)
    return y * pool_scale

def _short_conv(z_ext, t, conv_w):
    acc = conv_w[0] * z_ext[:, 0:t]
    for j in range(1, CONV_WIDTH):
        acc = acc + conv_w[j] * z_ext[:, j:j + t]
    return acc

def _pre(x, c, norm_g, w_ada, b_ada, w_in):
    mod = jnp.einsum("nd,de->ne", jax.nn.silu(c), w_ada) + b_ada
    shift, scale, gate = jnp.split(mod[:, None, :], 3, axis=-1)
    h = _rmsnorm(x, norm_g) * (1.0 + scale) + shift
    z = jnp.einsum("nld,de->nle", h, w_in)
    return _split_proj(z), gate

def _post(x, gate, branches, gate_paths, w_out):
    y = jnp.concatenate([b.astype(x.dtype) * jax.nn.silu(gp)
                         for b, gp in zip(branches, gate_paths)], axis=-1)
    return x + gate * jnp.einsum("nle,ed->nld", y, w_out)

def setup_inputs(seed: int = 0) -> dict:
    key = jax.random.key(seed)
    ks = jax.random.split(key, 24)
    f32 = jnp.float32
    wb = min(DIL_MAX, PAST_LEN)
    wd = min(SWA_WINDOW, PAST_LEN)
    nrm = lambda k, shape, s=1.0: jax.random.normal(k, shape, f32) * s
    return {
        "x_prompt": nrm(ks[0], (BATCH, SEQ, D_MODEL)),
        "x_sample": nrm(ks[1], (DEC_BATCH, DEC_SEQ, D_MODEL)),
        "c_prompt": nrm(ks[2], (BATCH, D_MODEL)),
        "c_sample": nrm(ks[3], (DEC_BATCH, D_MODEL)),
        "state_pool": nrm(ks[4], (DEPTH, DEC_BATCH, POOL_BUF, W_POOL)),
        "cache_dil_k": nrm(ks[5], (DEPTH, DEC_BATCH, wb, N_HEADS_DIL, HEAD_DIM)),
        "cache_dil_v": nrm(ks[6], (DEPTH, DEC_BATCH, wb, N_HEADS_DIL, HEAD_DIM)),
        "state_conv": nrm(ks[7], (DEPTH, DEC_BATCH, CONV_BUF, W_CONV)),
        "cache_swa_k": nrm(ks[8], (DEPTH, DEC_BATCH, wd, N_KV_SWA, HEAD_DIM)),
        "cache_swa_v": nrm(ks[9], (DEPTH, DEC_BATCH, wd, N_KV_SWA, HEAD_DIM)),
        "norm_g": 1.0 + nrm(ks[10], (DEPTH, D_MODEL), 0.02),
        "w_ada": nrm(ks[11], (DEPTH, D_MODEL, 3 * D_MODEL), 0.5 * D_MODEL ** -0.5),
        "b_ada": nrm(ks[12], (DEPTH, 3 * D_MODEL), 0.02),
        "w_in": nrm(ks[13], (DEPTH, D_MODEL, D_PROJ), D_MODEL ** -0.5),
        "w_pool": nrm(ks[14], (DEPTH, N_POOL_GROUPS, POOL_GROUP, POOL_GROUP), POOL_GROUP ** -0.5),
        "pool_scale": 1.0 + nrm(ks[15], (DEPTH, W_POOL), 0.1),
        "conv_w": nrm(ks[16], (DEPTH, CONV_WIDTH, W_CONV), CONV_WIDTH ** -0.5),
        "swa_sink": nrm(ks[17], (DEPTH, N_HEADS_SWA), 0.5),
        "w_out": nrm(ks[18], (DEPTH, D_MIX, D_MODEL), D_MIX ** -0.5),
        "final_g": 1.0 + nrm(ks[19], (D_MODEL,), 0.02),
    }

def reference(x_prompt, x_sample, c_prompt, c_sample, state_pool, cache_dil_k, cache_dil_v,
              state_conv, cache_swa_k, cache_swa_v, norm_g, w_ada, b_ada, w_in, w_pool,
              pool_scale, conv_w, swa_sink, w_out, final_g):
    dil_slopes = _alibi_slopes(N_HEADS_DIL)
    swa_slopes = _alibi_slopes(N_HEADS_SWA).reshape(N_KV_SWA, GQA_GROUP)
    swa_dists = jnp.arange(SWA_WINDOW + 1)
    xp, xs = x_prompt, x_sample
    pool_p, pool_s, dkp, dvp, dks, dvs = [], [], [], [], [], []
    conv_p, conv_s, skp, svp, sks, svs = [], [], [], [], [], []
    for i in range(DEPTH):
        sink = swa_sink[i].astype(jnp.float32).reshape(N_KV_SWA, GQA_GROUP)

        (pu, pg, dq, dk, dv, dg, ch, cb, cc, cg, sq, sk, sv, sg), gate = _pre(
            xp, c_prompt, norm_g[i], w_ada[i], b_ada[i], w_in[i])
        n, l = xp.shape[:2]
        a_out = _pool_mix(pu, l, w_pool[i], pool_scale[i])
        dk4 = dk.reshape(n, l, N_HEADS_DIL, HEAD_DIM)
        dv4 = dv.reshape(n, l, N_HEADS_DIL, HEAD_DIM)
        b_out = _dilated_prompt(dq.reshape(n, l, N_HEADS_DIL, HEAD_DIM), dk4, dv4,
                                dil_slopes).reshape(n, l, W_DIL)
        zc = cc * ch
        c_out = cb * _short_conv(jnp.pad(zc, ((0, 0), (CONV_BUF, 0), (0, 0))), l, conv_w[i])
        sk4 = sk.reshape(n, l, N_KV_SWA, HEAD_DIM)
        sv4 = sv.reshape(n, l, N_KV_SWA, HEAD_DIM)
        so, _ = _band_attention(sq.reshape(n, l, N_KV_SWA, GQA_GROUP, HEAD_DIM), sk4, sv4,
                                swa_slopes, 1, sink)
        d_out = so.reshape(n, l, W_SWA)
        xp = _post(xp, gate, (a_out, b_out, c_out, d_out), (pg, dg, cg, sg), w_out[i])
        pool_p.append(pu[:, -POOL_BUF:])
        dkp.append(dk4[:, -min(DIL_MAX, l):])
        dvp.append(dv4[:, -min(DIL_MAX, l):])
        conv_p.append(zc[:, -CONV_BUF:])
        skp.append(sk4[:, -min(SWA_WINDOW, l):])
        svp.append(sv4[:, -min(SWA_WINDOW, l):])

        (pu, pg, dq, dk, dv, dg, ch, cb, cc, cg, sq, sk, sv, sg), gate = _pre(
            xs, c_sample, norm_g[i], w_ada[i], b_ada[i], w_in[i])
        n, t = xs.shape[:2]
        u_ext = jnp.concatenate([state_pool[i], pu], axis=1)
        a_out = _pool_mix(u_ext, t, w_pool[i], pool_scale[i])
        dk4 = dk.reshape(n, t, N_HEADS_DIL, HEAD_DIM)
        dv4 = dv.reshape(n, t, N_HEADS_DIL, HEAD_DIM)
        b_out = _dilated_decode(dq.reshape(n, t, N_HEADS_DIL, HEAD_DIM),
                                jnp.concatenate([cache_dil_k[i], dk4], axis=1),
                                jnp.concatenate([cache_dil_v[i], dv4], axis=1),
                                dil_slopes).reshape(n, t, W_DIL)
        z_ext = jnp.concatenate([state_conv[i], cc * ch], axis=1)
        c_out = cb * _short_conv(z_ext, t, conv_w[i])
        sk4 = sk.reshape(n, t, N_KV_SWA, HEAD_DIM)
        sv4 = sv.reshape(n, t, N_KV_SWA, HEAD_DIM)
        so, _ = _gather_attention(sq.reshape(n, t, N_KV_SWA, GQA_GROUP, HEAD_DIM),
                                  jnp.concatenate([cache_swa_k[i], sk4], axis=1),
                                  jnp.concatenate([cache_swa_v[i], sv4], axis=1),
                                  swa_dists, swa_slopes, sink)
        d_out = so.reshape(n, t, W_SWA)
        xs = _post(xs, gate, (a_out, b_out, c_out, d_out), (pg, dg, cg, sg), w_out[i])
        pool_s.append(u_ext[:, -POOL_BUF:])
        dks.append(dk4)
        dvs.append(dv4)
        conv_s.append(z_ext[:, -CONV_BUF:])
        sks.append(sk4)
        svs.append(sv4)

    y_prompt = _rmsnorm(xp, final_g)
    y_sample = _rmsnorm(xs, final_g)
    return (y_prompt, y_sample,
            jnp.stack(pool_p), jnp.stack(pool_s),
            jnp.stack(dkp), jnp.stack(dvp), jnp.stack(dks), jnp.stack(dvs),
            jnp.stack(conv_p), jnp.stack(conv_s),
            jnp.stack(skp), jnp.stack(svp), jnp.stack(sks), jnp.stack(svs))


_drawn_inputs = setup_inputs


def setup_inputs(seed=0):
    import zlib

    import numpy as np

    out = dict(_drawn_inputs(seed))
    spreads = {}
    factors = {'cache_swa_k': 3.026, 'pool_scale': 6.838, 'swa_sink': 8.0, 'final_g': 2.839}
    for name, (base, spread) in spreads.items():
        noise = np.random.default_rng([zlib.crc32(name.encode()), seed]).standard_normal(out[name].shape)
        drawn = base * np.exp(spread * noise) if base else spread * noise
        out[name] = __import__('jax').numpy.asarray(drawn.astype(out[name].dtype))
    for name, factor in factors.items():
        out[name] = (out[name] * factor).astype(out[name].dtype)
    return out
```

```python
import math
from contextlib import ExitStack

import numpy as np

import concourse.bass as bass
from concourse import mybir
from concourse.alu_op_type import AluOpType as ALU

F32 = mybir.dt.float32
F32R = mybir.dt.float32r
ACT = mybir.ActivationFunctionType
AX = mybir.AxisListType

P = 128
D = 1024
KD = D // P
T = 2048
NS = 8
TT = T + NS
GROUP = 416
GROUPS = [(g * GROUP, min(TT, (g + 1) * GROUP)) for g in range(5)]
NT = 30
PLAIN0, GATE0, V0, Q0, K0 = 0, 8, 17, 21, 26
Y = 9
EPS = 1e-6
BIG = 1.0e30
NHD, NHS = 6, 4
SLOPE_D = [2.0 ** (-8.0 * (h + 1) / NHD) for h in range(NHD)]
SLOPE_S = [2.0 ** (-8.0 * (h + 1) / NHS) for h in range(NHS)]
DILATIONS = (1, 4, 16)
CH = 256
HALO = 16

C_ID, C_OFF, C_SELP, C_SLD, C_SLS, C_INVW, C_RCF, C_DB, C_SB, C_NEW, C_END = np.cumsum(
    [0, 128, 256, 128, 6, 4, 2, 32, 18, 4, 8]).tolist()


def constants():
    c = np.zeros((P, C_END), np.float32)
    p = np.arange(P)
    c[:, C_ID:C_ID + P] = np.eye(P)
    off = p[:, None] - np.arange(256)[None, :] + 128.0
    c[:, C_OFF:C_OFF + 256] = np.where((off >= 0) & (off <= 128), off, BIG)
    c[NS, C_SELP:C_SELP + P] = 1.0
    c[:, C_SLD:C_SLD + 6] = np.array(SLOPE_D)
    c[:, C_SLS:C_SLS + 4] = np.array(SLOPE_S)
    for t in range(2):
        for half in range(2):
            w = (2, 4, 8, 16)[2 * t + half]
            rows = slice(64 * half, 64 * half + 64)
            c[rows, C_INVW + t] = 1.0 / w
            c[rows, C_RCF + 16 * t:C_RCF + 16 * t + 16] = 1.0 / np.minimum(np.arange(16) + 1, w)
    for i, d in enumerate(DILATIONS):
        for h in range(NHD):
            c[:, C_DB + 6 * i + h] = -np.float32(SLOPE_D[h]) * d * (128 - p)
    for h in range(NHS):
        c[:, C_SB + h] = -np.float32(SLOPE_S[h]) * (128 - p)
    c[:, C_NEW:C_NEW + NS] = np.where(p[:, None] % NS == np.arange(NS)[None], 0.0, -BIG)
    return c


def build_program(nc, x_prompt, x_sample, c_t, w_ada, b_ada, norm_g, w_tiles, const, pool_w, pool_scale,
                  conv_w, sink, sink_rows, w_out, final_g, dil_kc, dil_vc, swa_kc, swa_vc, pool_state,
                  conv_state, pool_rows, conv_rows,
                  y_prompt, y_sample, pool_p, pool_s, dil_k_p, dil_v_p, dil_k_s, dil_v_s,
                  conv_p, conv_s, swa_k_p, swa_v_p, swa_k_s, swa_v_s):
    with ExitStack() as ctx:
        base = (nc.sbuf_base + 63) // 64 * 64
        arena_bytes = nc.sbuf_usable_end - base - 64
        ctx.enter_context(nc.sbuf_tensor("arena", [P, arena_bytes // 4], F32, align_bytes=64))

        class Plan:
            def __init__(self, at):
                self.at = at

            def put(self, name, shape, dtype=F32):
                size = int(np.prod(shape[1:])) * 4
                t = nc.alloc_sbuf_tensor_at(name, shape, dtype, offset=self.at)
                self.at = (self.at + size + 31) // 32 * 32
                assert self.at <= base + arena_bytes, name
                return t

        def sem(name):
            return ctx.enter_context(nc.semaphore(name))

        def scratch(name, shape, dtype=F32):
            return nc.dram_tensor(name, shape, dtype, kind="Internal").ap()

        plain_dram = scratch("plain_dram", [8, P, T])
        gate_dram = scratch("gate_dram", [Y, P, T])
        kv_dram = scratch("kv_dram", [8, P, T])
        qk_hi_dram = scratch("qk_hi_dram", [9, P, T])
        qk_lo_dram = scratch("qk_lo_dram", [9, P, T])
        yac_dram = scratch("yac_dram", [4, P, T])
        swa_v_dram = scratch("swa_v_dram", [T, P])
        mix_dram = scratch("mix_dram", [3, T, 3, 132])
        swa_mix_dram = scratch("swa_mix_dram", [T, 2, 132])
        zs_dram = scratch("zs_dram", [NS, 19 * P])

        keep = Plan(base)
        consts = keep.put("consts", [P, C_END])
        mod_gate = keep.put("mod_gate", [NS + 1, D])
        zs_t = keep.put("zs_t", [P, NT, NS])
        mod_scale = keep.put("mod_scale", [P, KD, NS + 1])
        mod_shift = keep.put("mod_shift", [P, KD, NS + 1])
        c_sb = keep.put("c_sb", [P, KD, NS + 1])
        c_silu = keep.put("c_silu", [P, KD, NS + 1])
        g_t = keep.put("g_t", [P, KD])
        small = keep.put("small", [P, 64])
        pool_scale_t = keep.put("pool_scale_t", [P, 2])
        conv_w_t = keep.put("conv_w_t", [P, 2, 3])
        pool_w_sb = keep.put("pool_w_sb", [P, 2, P])
        tail_u = keep.put("tail_u", [P, 2, 15])
        tail_z = keep.put("tail_z", [P, 2, 2])
        zc_s = keep.put("zc_s", [NS, 256])
        neg_sink = keep.put("neg_sink", [P, NHS])
        b_gate = keep.put("b_gate", [NS + 1, D])
        ident = consts[:, C_ID:C_ID + P]

        h_at = keep.at
        h_bytes = KD * TT * 4
        w_at = h_at + 2 * h_bytes
        slot_at = w_at + 6 * D * 4
        SLOT = TT * 4
        assert slot_at + 5 * SLOT <= base + arena_bytes

        h_hi = Plan(h_at).put("h_hi", [P, KD, TT], F32R)
        h_lo = Plan(h_at + h_bytes).put("h_lo", [P, KD, TT], F32R)
        h_f32 = Plan(h_at + h_bytes).put("h_f32", [P, KD, TT])
        wp = Plan(w_at)
        w_raw = [wp.put(f"w_raw{b}", [P, KD, P]) for b in range(2)]
        w_hi = [wp.put(f"w_hi{b}", [P, KD, P], F32R) for b in range(2)]
        w_lo = [wp.put(f"w_lo{b}", [P, KD, P], F32R) for b in range(2)]
        main = [Plan(slot_at + b * SLOT).put(f"main{b}", [P, TT]) for b in range(2)]
        main_hi = [Plan(slot_at + b * SLOT).put(f"main_hi{b}", [P, TT], F32R) for b in range(2)]
        main_lo = [Plan(slot_at + (2 + b) * SLOT).put(f"main_lo{b}", [P, TT], F32R) for b in range(2)]
        k_nat = Plan(slot_at + 4 * SLOT).put("k_nat", [P, TT])
        ada_w = Plan(h_at).put("ada_w", [P, 4, KD, 512])
        xp_ = Plan(slot_at)
        x_in = [xp_.put(f"x_in{i}", [P, D]) for i in range(4)]
        junk = Plan(slot_at + 2 * SLOT).put("junk", [P, D])
        b_mod = Plan(slot_at + 3 * SLOT).put("b_mod", [NS + 1, 2 * D])
        mod_sb = Plan(slot_at + 4 * SLOT).put("mod_sb", [NS + 1, 2 * D])
        gate_w = [Plan(slot_at + (2 + b) * SLOT).put(f"gate_w{b}", [P, KD, 256]) for b in range(2)]
        cp = Plan(slot_at + 2 * SLOT)
        u_in = cp.put("u_in", [P, 2, HALO + CH])
        sum_a = cp.put("sum_a", [P, 2, HALO + CH])
        sum_b = cp.put("sum_b", [P, 2, HALO + CH])
        diff = cp.put("diff", [P, 2, CH])
        ch_in = cp.put("ch_in", [P, 2, 2 + CH])
        cc_in = cp.put("cc_in", [P, 2, 2 + CH])
        cb_in = cp.put("cb_in", [P, 2, CH])
        gate_in = cp.put("gate_in", [P, 4, CH])
        yac = cp.put("yac", [P, 4, CH])
        assert cp.at <= slot_at + 5 * SLOT
        np_ = Plan(w_at)
        kv_in = [np_.put(f"kv_in{b}", [P, 8, P]) for b in range(2)]
        kv_nat = [np_.put(f"kv_nat{b}", [P, 8, P]) for b in range(2)]
        ap_ = Plan(h_at)
        q_st = [[ap_.put(f"q_st{j}{h}", [P, T], F32R) for h in range(2)] for j in range(2)]
        kh_st = [[ap_.put(f"kh_st0{h}", [P, T], F32R) for h in range(2)], [ap_.put("kh_st1", [P, T], F32R)] * 2]
        kl_st = [[ap_.put(f"kl_st0{h}", [P, T], F32R) for h in range(2)], [ap_.put("kl_st1", [P, T], F32R)] * 2]
        v_dil = [ap_.put(f"v_dil{c}", [P, 16, P]) for c in range(3)]
        v_swa = ap_.put("v_swa", [P, 16, 64])
        logits_at = ap_.at
        xs_ = [ap_.put(f"logits{b}", [P, 2, 256]) for b in range(2)]
        probs = [ap_.put(f"probs{b}", [P, 2, 256]) for b in range(4)]
        probs_t = [ap_.put(f"probs_t{b}", [P, 4, P]) for b in range(2)]
        o_t = ap_.put("o_t", [P, 4, P])
        assert ap_.at <= w_at
        ZN_TILES = list(range(0, 6)) + list(range(V0, NT))
        ZN = {"pu": (0, 256), "ch": (256, 512), "cc": (512, 768), "dv": (768, 1152), "sv": (1152, 1280),
              "dq": (1280, 1664), "sq": (1664, 1920), "dk": (1920, 2304), "sk": (2304, 2432)}
        zp = Plan(logits_at)
        zn = zp.put("zn", [NS, len(ZN_TILES) * P])
        tail_rows = zp.put("tail_rows", [15, 512])
        assert zp.at <= logits_at + 3 * 4096
        bp = Plan(slot_at)
        bias_dil = bp.put("bias_dil", [P, 3, 2, 256])
        bias_swa = bp.put("bias_swa", [P, 2, 256])
        o_st = [bp.put(f"o_st{b}", [P, 4, 132]) for b in range(4)]
        sink_now = bp.put("sink_now", [P, 2])
        op = Plan(h_at)
        wo_hi = op.put("wo_hi", [P, Y, D], F32R)
        wo_lo = op.put("wo_lo", [P, Y, D], F32R)
        ys_hi = op.put("ys_hi", [P, Y, NS], F32R)
        ys_lo = op.put("ys_lo", [P, Y, NS], F32R)
        y_place = op.at
        y_hi = [op.put(f"y_hi{b}", [P, Y, P], F32R) for b in range(2)]
        y_lo = [op.put(f"y_lo{b}", [P, Y, P], F32R) for b in range(2)]
        mix_in = [op.put(f"mix_in{b}", [P, 3, 3, 132]) for b in range(2)]
        swa_in = [op.put(f"swa_in{b}", [P, 2, 132]) for b in range(2)]
        x_res = [op.put(f"x_res{b}", [P, D]) for b in range(2)]
        gates = [op.put(f"gates{b}", [P, 5, P]) for b in range(2)]
        o_mix = op.put("o_mix", [P, 640])
        assert op.at <= w_at
        op = Plan(w_at)
        wo_raw = [op.put(f"wo_raw{b}", [P, D]) for b in range(2)]
        resid = [op.put(f"resid{b}", [P, D]) for b in range(2)]
        gate_all = op.put("gate_all", [P, D])
        assert op.at <= slot_at
        op = Plan(slot_at)
        y_t = [op.put(f"y_t{b}", [P, Y, P]) for b in range(2)]
        y_out = [op.put(f"y_out{b}", [P, D]) for b in range(2)]
        final_g_sb = op.put("final_g_sb", [P, D])
        junk_o = op.put("junk_o", [P, D])
        o_part = op.put("o_part", [P, 384])
        fac = op.put("fac", [P, 64])
        fin = op.put("fin", [P, 8])

        psum = ctx.enter_context(nc.psum_tensor("psum", [P, 8, 512], F32))

        const_loaded = sem("const_loaded")
        x_loaded = [sem(f"x_loaded{i}") for i in range(4)]
        xs_loaded = sem("xs_loaded")
        ada_loaded = [sem(f"ada_loaded{i}") for i in range(4)]
        gate_loaded = [sem(f"gate_loaded{i}") for i in range(2)]
        c_ready = sem("c_ready")
        sumsq = sem("sumsq")
        var_ready = sem("var_ready")
        std_ready = sem("std_ready")
        rstd_ready = sem("rstd_ready")
        xn_ready = sem("xn_ready")
        xt_ready = sem("xt_ready")
        xt_copied = [sem(f"xt_copied{i}") for i in range(2)]
        ada_more = sem("ada_more")
        dve_link = sem("dve_link")
        mod_mm = sem("mod_mm")
        mod_added = sem("mod_added")
        mod_t = sem("mod_t")
        mod_done = sem("mod_done")
        h_aff = sem("h_aff")
        h_hi_ready = sem("h_hi_ready")
        h_ready = sem("h_ready")
        w_loaded = [sem(f"w_loaded{b}") for b in range(2)]
        w_hi_ready = sem("w_hi_ready")
        w_ready = sem("w_ready")
        group_done = sem("group_done")
        bank_free = [sem(f"bank_free{g}") for g in range(5)]
        act_evac = sem("act_evac")
        main_stored = [sem(f"main_stored{b}") for b in range(2)]
        lo_stored = [sem(f"lo_stored{b}") for b in range(2)]
        knat_stored = sem("knat_stored")
        gate_mm = sem("gate_mm")
        gate_added = sem("gate_added")
        chunk_loaded = sem("chunk_loaded")
        diff_ready = sem("diff_ready")
        pool_mm = sem("pool_mm")
        yac_ready = sem("yac_ready")
        yac_stored = sem("yac_stored")
        tail_t = sem("tail_t")
        tail_copied = sem("tail_copied")
        kv_loaded = [sem(f"kv_loaded{b}") for b in range(2)]
        kv_t = sem("kv_t")
        nat_a = sem("nat_a")
        nat_v = sem("nat_v")
        nat_stored = [sem(f"nat_stored{b}") for b in range(2)]
        out_stored = sem("out_stored")
        qkv_loaded = [sem(f"qkv_loaded{j}") for j in range(2)]
        s_done = sem("s_done")
        x_ready = sem("x_ready")
        bias_ready = sem("bias_ready")
        p_ready = sem("p_ready")
        pt_done = sem("pt_done")
        pt_copied = sem("pt_copied")
        pv_done = sem("pv_done")
        ot_copied = sem("ot_copied")
        o_turned = sem("o_turned")
        o_copied = sem("o_copied")
        mix_stored = [sem(f"mix_stored{b}") for b in range(4)]
        wo_loaded = [sem(f"wo_loaded{b}") for b in range(2)]
        wo_hi_ready = sem("wo_hi_ready")
        wo_split = sem("wo_split")
        fg_loaded = sem("fg_loaded")
        tile_in = [sem(f"tile_in{b}") for b in range(2)]
        x_again = [sem(f"x_again{b}") for b in range(2)]
        gate_bc = sem("gate_bc")
        arg_ready = sem("arg_ready")
        exp_ready = sem("exp_ready")
        mixed = sem("mixed")
        mix_t = sem("mix_t")
        yt_ready = sem("yt_ready")
        yh_ready = sem("yh_ready")
        y_split = sem("y_split")
        out_mm = sem("out_mm")
        res_gated = sem("res_gated")
        res_ready = sem("res_ready")
        sq_ready = sem("sq_ready")
        fvar_ready = sem("fvar_ready")
        fstd_ready = sem("fstd_ready")
        y_ready = sem("y_ready")
        y_stored = [sem(f"y_stored{b}") for b in range(2)]
        out_link = sem("out_link")
        sink_negated = sem("sink_negated")
        unit_open = sem("unit_open")
        store_open = sem("store_open")
        zs_t_done = sem("zs_t_done")
        zs_copied = sem("zs_copied")
        zc_ready = sem("zc_ready")
        zs_stored = sem("zs_stored")
        dec_loaded = sem("dec_loaded")
        dec_k_loaded = [sem(f"dec_k_loaded{b}") for b in range(2)]
        dec_v_loaded = sem("dec_v_loaded")
        dec_k_used = sem("dec_k_used")
        dec_s_ready = sem("dec_s_ready")
        dec_st = sem("dec_st")
        dec_neg = sem("dec_neg")
        dec_exp = sem("dec_exp")
        dec_pn = sem("dec_pn")
        dec_pt_done = sem("dec_pt_done")
        dec_pt_ready = sem("dec_pt_ready")
        dec_o_done = sem("dec_o_done")
        dec_diff = sem("dec_diff")
        dec_pool = sem("dec_pool")
        dec_gate = sem("dec_gate")
        dec_y_full = sem("dec_y_full")
        dec_y_ready = sem("dec_y_ready")
        dec_mm = sem("dec_mm")
        dec_res = sem("dec_res")
        dec_sq_ready = sem("dec_sq_ready")
        dec_var = sem("dec_var")
        dec_std = sem("dec_std")
        dec_out = sem("dec_out")
        rec_ready = sem("rec_ready")
        gate_bc_read = sem("gate_bc_read")

        PAIR_GROUPS = 4

        def walk(eng, body):
            for t in (0, 1):
                body(t, t // 2, t, "plain")
            with eng.Fori(0, 3) as i:
                for b in range(2):
                    body(2 + 2 * i + b, 1 + i, 2 + b, "plain")
            with eng.Fori(0, 2) as i:
                for b in range(2):
                    body(8 + 2 * i + b, 4 + i, 8 + b, "gate")
            for t in range(12, Q0):
                body(t, t // 2, t, "gate" if t < V0 else "plain")
            for t in range(Q0, K0):
                body(t, t // 2, t, "q")
            for t in range(K0, NT):
                body(t, t // 2, t, "k")

        CHUNK0 = 12
        NCH = T // CH

        UNITS = 2 * 64 + 48

        def attention_qk(eng, kind, p):
            qt, kt = (p, 5 + p) if kind == 0 else (3 + p, 8)
            up, down = slice(0, 64), slice(64, 128)
            for h in range(2):
                r = slice(64 * h, 64 * h + 64)
                for half, src in ((up, qk_hi_dram), (down, qk_lo_dram)):
                    eng.dma_start(q_st[kind][h][half, :].bitcast(F32), src[qt, r, :]).then_inc(qkv_loaded[kind], 16)
            for h in range(2 if kind == 0 else 1):
                r = slice(64 * h, 64 * h + 64) if kind == 0 else slice(64 * p, 64 * p + 64)
                for half in (up, down):
                    eng.dma_start(kh_st[kind][h][half, :].bitcast(F32), qk_hi_dram[kt, r, :]).then_inc(
                        qkv_loaded[kind], 16)
                    eng.dma_start(kl_st[kind][h][half, :].bitcast(F32), qk_lo_dram[kt, r, :]).then_inc(
                        qkv_loaded[kind], 16)

        def attention_v(eng, kind, p):
            if kind == 1:
                eng.dma_start(v_swa[:], swa_v_dram[:, 64 * p:64 * p + 64].rearrange("(b q) c -> q b c", q=P)).then_inc(
                    qkv_loaded[1], 16)
                return
            v = dil_v_p[:, P * p:P * p + P]
            eng.dma_start(v_dil[0][:], v.rearrange("(b q) c -> q b c", q=P)).then_inc(qkv_loaded[0], 16)
            for r in range(4):
                eng.dma_start(v_dil[1][:, 4 * r:4 * r + 4, :],
                              v.rearrange("(b q r) c -> r q b c", q=P, r=4)[r]).then_inc(qkv_loaded[0], 16)
            eng.dma_start(v_dil[2][:], v.rearrange("(q r) c -> q r c", r=16)).then_inc(qkv_loaded[0], 16)

        QKV_DMAS = (18, 9)

        ZS_STORES = 11
        DEC_LOADS = 2 + 6 + 2 * (2 + 4) + 5

        class Unit:
            def __init__(self, kind, c, i):
                self.kind, self.c, self.i = kind, c, i
                d = 1 if kind else DILATIONS[c]
                self.r, self.b = (0, i) if d == 1 else (i // 4, i % 4) if d == 4 else (i, 0)
                self.d = d
                self.full = self.b > 0
                self.own = P if self.full or (d == 16 and self.r % 2) else 0

            def view(self, t):
                return t[:].rearrange("p (t r) -> p r t", r=self.d)

            def q(self, h):
                return self.view(q_st[self.kind][h])[:, self.r, P * self.b:P * self.b + P]

            def keys(self, stack, h):
                v = self.view(stack[self.kind][h])
                if self.d == 16:
                    r0 = self.r - self.r % 2
                    return v[:, r0:r0 + 2, :]
                c0 = P * (self.b - 1) if self.full else 0
                return v[:, self.r, c0:c0 + 256]

            def v(self, h, back):
                if self.kind:
                    return v_swa[:, self.i - back, :]
                return v_dil[self.c][:, self.i - back, 64 * h:64 * h + 64]

            def bias(self, h):
                t = bias_swa[:, h, :] if self.kind else bias_dil[:, self.c, h, :]
                return t if self.full else t[:, P:256]

            def cols(self):
                return slice(0, 256) if self.full else slice(self.own, self.own + P)

            def halves(self):
                return ((0, 1), (P, 0)) if self.full else ((self.own, 0),)

        units = [Unit(0, c, i) for c in range(3) for i in range(16)] + [Unit(1, 0, i) for i in range(16)]

        def rounds(eng, body):
            with eng.Fori(0, 2) as i:
                body(i, units)
            body(2, units[:48])

        S_BANK, PT_BANK, OT_BANK, ON_BANK = 0, 2, 4, 6

        def out_load(eng, j, b):
            rows = bass.ds(P * j, P)
            eng.dma_start(mix_in[b][:], mix_dram[:, rows, :, :].rearrange("c q j w -> q c j w")).then_inc(tile_in[b], 16)
            eng.dma_start(swa_in[b][:], swa_mix_dram[rows, :, :]).then_inc(tile_in[b], 16)
            eng.dma_start(gates[b][:], gate_dram[4:Y, :, rows].rearrange("m p t -> p m t")).then_inc(tile_in[b], 16)
            eng.dma_start(y_t[b][:, 0:4, :], yac_dram[:, :, rows].rearrange("m p t -> p m t")).then_inc(tile_in[b], 16)

        def res_load(eng, j, b):
            eng.dma_start(x_res[b][:], x_prompt[bass.ds(P * j, P), :]).then_inc(x_again[b], 16)

        def out_walk(eng, step):
            step(0, 0, 0, True)
            step(1, 0, 1, True)
            with eng.Fori(1, 8) as i:
                for b in range(2):
                    step(2 * i + b, i, b, False)

        dp = Plan(y_place)
        dec_v = dp.put("dec_v", [P, NS, 3, 384])
        dec_q = dp.put("dec_q", [P, NS, 384])
        dec_k4 = dp.put("dec_k4", [24, 384])
        dec_v4 = dp.put("dec_v4", [24, 384])
        dec_state = dp.put("dec_state", [P, 2, NS, 15])
        dec_conv = dp.put("dec_conv", [P, 2, NS, 2])
        assert dp.at <= w_at
        dp = Plan(w_at)
        dec_k = [dp.put(f"dec_k{b}", [P, 3, 384]) for b in range(2)]
        dec_prod = dp.put("dec_prod", [P, NS * 384])
        dec_sq = dp.put("dec_sq", [P, NS * 256])
        dec_sk = dp.put("dec_sk", [P, NS, 2, 2, 64])
        dec_sv = dp.put("dec_sv", [P, NS, 2, 2, 64])
        dec_sk4 = dp.put("dec_sk4", [NS, 2, 2, 64])
        dec_sv4 = dp.put("dec_sv4", [NS, 2, 2, 64])
        dec_s = dp.put("dec_s", [P, 3, 48])
        dec_s4 = dp.put("dec_s4", [24, 48])
        dec_ss = dp.put("dec_ss", [P, 32])
        dec_ss4 = dp.put("dec_ss4", [NS, 32])
        dec_p = dp.put("dec_p", [48, 408])
        dec_ps = dp.put("dec_ps", [32, 136])
        dec_pt = dp.put("dec_pt", [P, 3, 48])
        dec_pt4 = dp.put("dec_pt4", [24, 48])
        dec_pst = dp.put("dec_pst", [P, 32])
        dec_pst4 = dp.put("dec_pst4", [NS, 32])
        dec_g = dp.put("dec_g", [P, Y, NS])
        dec_y = dp.put("dec_y", [P, Y, NS])
        dec_a = dp.put("dec_a", [P, 2, NS])
        dec_b = dp.put("dec_b", [P, 2, NS])
        sink_col = dp.put("sink_col", [32, 1])
        dec_small = dp.put("dec_small", [P, 16])
        dec_x = dp.put("dec_x", [NS, D])
        dec_r = dp.put("dec_r", [NS, D])
        dec_fg = dp.put("dec_fg", [NS, D])
        assert dp.at <= slot_at + 5 * SLOT
        block = ctx.enter_context(nc.Block())
        wv = w_ada.rearrange("(k p) e -> p k e", p=P)

        def bank(b, n=512):
            return psum[:, b, 0:n]

        @block.sync
        def _(sp):
            for dst, src in ((c_sb[:], c_t), (consts[:], const), (g_t[:], norm_g), (b_mod[:], b_ada[:, 0:2 * D]),
                             (b_gate[:], b_ada[:, 2 * D:]), (pool_scale_t[:], pool_scale), (conv_w_t[:], conv_w),
                             (pool_w_sb[:], pool_w), (neg_sink[:], sink)):
                sp.dma_start(dst, src).then_inc(const_loaded, 16)

            def x_round(j, first):
                for i in range(4):
                    if not first:
                        sp.wait_ge(xt_ready, 4 * j - 3 + i)
                    sp.dma_start(x_in[i][:], x_prompt[bass.ds(512 * j + P * i, P), :]).then_inc(x_loaded[i], 16)

            x_round(0, True)
            with sp.Fori(1, 4) as j:
                x_round(j, False)
            sp.wait_ge(xt_ready, 13)
            sp.dma_start(x_in[0][0:NS, :], x_sample).then_inc(xs_loaded, 16)

            sp.wait_ge(sumsq, 17)
            sp.wait_ge(mod_added, 4)
            sp.wait_ge(mod_mm, 4)
            for q in range(2):
                sp.dma_start(gate_w[q][:], wv[:, :, 2 * D + 256 * q:2 * D + 256 * q + 256]).then_inc(gate_loaded[q], 16)

            def store(t, half, ts, kind):
                b = ts % 2
                one = lambda a, i: a[bass.ds(i, 1), :, :].rearrange("a p t -> p (a t)")
                sp.wait_ge(bank_free[4], t + 1)
                if kind == "plain":
                    dst = one(plain_dram, t) if ts < GATE0 else one(kv_dram, t - 13)
                    sp.dma_start(dst, main[b][:, 0:T]).then_inc(main_stored[b], 16)
                elif kind == "gate":
                    sp.dma_start(one(gate_dram, t - GATE0), main[b][:, 0:T]).then_inc(main_stored[b], 16)
                else:
                    sp.dma_start(one(qk_hi_dram, t - Q0), main_hi[b][:, 0:T].bitcast(F32)).then_inc(main_stored[b], 16)
                    sp.dma_start(one(qk_lo_dram, t - Q0), main_lo[b][:, 0:T].bitcast(F32)).then_inc(lo_stored[b], 16)
                    if kind == "k":
                        sp.dma_start(one(kv_dram, t - K0), k_nat[:, 0:T]).then_inc(knat_stored, 16)
                if 0 <= ts - CHUNK0 < NCH:
                    n = ts - CHUNK0
                    sp.wait_ge(yac_ready, n + 1)
                    sp.dma_start(yac_dram[:, :, CH * n:CH * n + CH].rearrange("m p t -> p m t"), yac[:]).then_inc(
                        yac_stored, 16)
                if ts == 1:
                    for q in range(2):
                        sp.wait_ge(gate_mm, q + 1)
                        sp.dma_start(gate_w[q][:], wv[:, :, 2 * D + 512 + 256 * q:2 * D + 768 + 256 * q]).then_inc(
                            gate_loaded[q], 16)

            walk(sp, store)

            for b in range(2):
                sp.wait_ge(main_stored[b], 16 * 15)
            sp.wait_ge(knat_stored, 16 * 4)
            sp.wait_ge(group_done, 5 * NT)

            def kv_load(j, b):
                sp.dma_start(kv_in[b][:], kv_dram[:, :, bass.ds(P * j, P)].rearrange("m p t -> p m t")).then_inc(
                    kv_loaded[b], 16)

            def kv_store(j, b):
                rows = bass.ds(P * j, P)
                sp.dma_start(dil_k_p[rows, :], kv_nat[b][:, 0:3, :].rearrange("p m c -> p (m c)")).then_inc(
                    nat_stored[b], 16)
                sp.dma_start(dil_v_p[rows, :], kv_nat[b][:, 4:7, :].rearrange("p m c -> p (m c)")).then_inc(
                    nat_stored[b], 16)
                sp.dma_start(swa_v_dram[rows, :], kv_nat[b][:, 7, :]).then_inc(nat_stored[b], 16)

            def kv_stores(j, b):
                sp.wait_ge(nat_a, j + 1)
                sp.wait_ge(nat_v, j + 1)
                kv_store(j, b)

            for b in range(2):
                kv_load(b, b)
            sp.wait_ge(zs_copied, 6)
            sp.wait_ge(zc_ready, 1)
            zcol = lambda n: zn[:, ZN[n][0]:ZN[n][1]]
            sp.dma_start(zs_dram, zn[:]).then_inc(zs_stored, 16)
            for dst, src in ((dil_k_s, zcol("dk")), (dil_v_s, zcol("dv")), (swa_k_s, zcol("sk")), (swa_v_s, zcol("sv")),
                             (pool_s[:, 14, :], zcol("pu")), (pool_s[:, 0:14, :], pool_rows[:, 1:15, :]),
                             (conv_s[:, 1, :], zc_s[:]), (conv_s[:, 0, :], conv_rows[:, 1, :]),
                             (pool_p, tail_rows[:, 0:256]), (conv_p, tail_rows[0:2, 256:512])):
                sp.dma_start(dst, src).then_inc(zs_stored, 16)
            with sp.Fori(0, 7) as i:
                for b in range(2):
                    sp.wait_ge(kv_t, 2 * i + b + 1)
                    kv_load(2 * i + 2 + b, b)
                    kv_stores(2 * i + b, b)
            for b in range(2):
                kv_stores(14 + b, b)
            sp.dma_start(swa_k_p, kv_nat[1][:, 3, :]).then_inc(out_stored, 16)
            sp.dma_start(swa_v_p, kv_nat[1][:, 7, :]).then_inc(out_stored, 16)
            for b in range(2):
                sp.wait_ge(nat_stored[b], 3 * 16 * 8)
            sp.wait_ge(out_stored, 16 * 2)
            attention_v(sp, 0, 0)
            attention_qk(sp, 1, 0)
            attention_v(sp, 1, 0)
            for kind, p, used in ((0, 1, 48), (1, 1, 64), (0, 2, 64 + 48)):
                sp.wait_ge(pv_done, used)
                attention_qk(sp, kind, p)
                attention_v(sp, kind, p)

            sp.wait_ge(pv_done, UNITS)
            sp.wait_ge(o_turned, UNITS // 4)
            for k in range(Y):
                if k >= 2:
                    sp.wait_ge(wo_split, k - 1)
                sp.dma_start(wo_raw[k % 2][:], w_out[:, k, :]).then_inc(wo_loaded[k % 2], 16)
                if k == 0:
                    for b in range(4):
                        sp.wait_ge(mix_stored[b], 16 * (UNITS // 16))
                    sp.dma_start(final_g_sb[:], final_g).then_inc(fg_loaded, 16)
                    for b in range(2):
                        out_load(sp, b, b)
                        res_load(sp, b, b)

            def out_store(j, b):
                sp.wait_ge(y_ready, j + 1)
                sp.dma_start(y_prompt[bass.ds(P * j, P), :], y_out[b][:]).then_inc(y_stored[b], 16)

            with sp.Fori(1, 8) as i:
                for b in range(2):
                    sp.wait_ge(y_split, 2 * i + b - 1)
                    out_load(sp, 2 * i + b, b)
                    sp.wait_ge(res_ready, 2 * i + b - 1)
                    res_load(sp, 2 * i + b, b)
                    out_store(2 * i + b - 2, b)
            for b in range(2):
                out_store(14 + b, b)

            sp.wait_ge(out_mm, 16)
            sp.wait_ge(y_ready, 16)
            for b in range(2):
                sp.wait_ge(y_stored[b], 16 * 8)
            zrow = lambda n: zs_dram[:, ZN[n][0]:ZN[n][1]]

            def cache_rows(cache, b, c):
                d = DILATIONS[c]
                return cache[b, 2048 - P * d:2048, :].rearrange("(p r) e -> r p e", r=d)[0]

            sp.dma_start(dec_q[:], zrow("dq").partition_broadcast(P)).then_inc(dec_loaded, 16)
            sp.dma_start(dec_sq[:].rearrange("p (s e) -> p s e", s=NS), zrow("sq").partition_broadcast(P)).then_inc(
                dec_loaded, 16)
            for n in range(3):
                sp.dma_start(dec_k4[NS * n:NS * n + NS, :], zrow("dk")).then_inc(dec_loaded, 16)
                sp.dma_start(dec_v4[NS * n:NS * n + NS, :], zrow("dv")).then_inc(dec_loaded, 16)
            for x in range(2):
                for dst, src in ((dec_sk4, zrow("sk")), (dec_sv4, zrow("sv"))):
                    sp.dma_start(dst[:, :, x, :], src.rearrange("s (g e) -> s g e", g=2)).then_inc(dec_loaded, 16)
                for dst, src in ((dec_sk, swa_kc), (dec_sv, swa_vc)):
                    for g in range(2):
                        sp.dma_start(dst[:, :, g, x, :], src.rearrange("s p (g e) -> p s g e", g=2)[:, :, g, :]).then_inc(
                            dec_loaded, 16)
            sp.dma_start(dec_state[:], pool_state).then_inc(dec_loaded, 16)
            sp.dma_start(dec_conv[:], conv_state).then_inc(dec_loaded, 16)
            sp.dma_start(dec_x[:], x_sample).then_inc(dec_loaded, 16)
            sp.dma_start(dec_fg[:], final_g[0:NS, :]).then_inc(dec_loaded, 16)
            sp.dma_start(sink_col[:], sink_rows).then_inc(dec_loaded, 16)
            for b in range(NS):
                if b >= 2:
                    sp.wait_ge(dec_k_used, b - 1)
                for c in range(3):
                    sp.dma_start(dec_k[b % 2][:, c, :], cache_rows(dil_kc, b, c)).then_inc(dec_k_loaded[b % 2], 16)
            for b in range(NS):
                for c in range(3):
                    sp.dma_start(dec_v[:, b, c, :], cache_rows(dil_vc, b, c)).then_inc(dec_v_loaded, 16)
            sp.wait_ge(dec_out, 1)
            sp.dma_start(y_sample, dec_r[:]).then_inc(out_stored, 16)
            sp.wait_ge(out_stored, 48)

        @block.gpsimd
        def _(pool):
            for b in range(2):
                pool.dma_start(w_raw[b][:], w_tiles[b]).then_inc(w_loaded[b], 16)

            def load(t, half, ts, kind):
                b = ts % 2
                if ts < NT - 2:
                    pool.wait_ge(w_ready, t + 1)
                    pool.dma_start(w_raw[b][:], w_tiles[bass.ds(t + 2, 1), :, :, :].rearrange(
                        "a p k c -> p (a k) c")).then_inc(w_loaded[b], 16)
                n = ts - CHUNK0
                if 0 <= n < NCH:
                    chunk_load(n)

            def chunk_load(n):
                c0 = CH * n
                if n == 0:
                    for b in range(2):
                        pool.wait_ge(main_stored[b], 16 * 6)
                else:
                    pool.wait_ge(yac_ready, n)
                h = HALO if n else 0
                h2 = 2 if n else 0
                def rows(a, c, left, dst):
                    pool.dma_start(dst, a[:, :, c - left:c + CH].rearrange("m p t -> p m t")).then_inc(chunk_loaded, 16)
                rows(plain_dram[0:2], c0, h, u_in[:, :, HALO - h:])
                rows(plain_dram[2:4], c0, h2, ch_in[:, :, 2 - h2:])
                rows(plain_dram[4:6], c0, h2, cc_in[:, :, 2 - h2:])
                rows(plain_dram[6:8], c0, 0, cb_in[:])
                rows(gate_dram[0:4], c0, 0, gate_in[:])

            walk(pool, load)

            def mixes(i, us):
                for g in range(len(us) // 4):
                    u = us[4 * g]
                    pool.wait_ge(o_copied, 16 * i + g + 1)
                    if u.kind:
                        dst = swa_mix_dram[:, bass.ds(i, 1), :].rearrange("t a w -> t (a w)")
                    else:
                        dst = mix_dram[u.c, :, bass.ds(i, 1), :].rearrange("t a w -> t (a w)")
                    if u.d == 1:
                        dst = dst[P * u.b:P * u.b + 512].rearrange("(b q) w -> q b w", q=P)
                    elif u.d == 4:
                        dst = dst.rearrange("(b q r) w -> r q b w", q=P, r=4)[u.r]
                    else:
                        dst = dst.rearrange("(q r) w -> q r w", r=16)[:, u.r:u.r + 4, :]
                    pool.sem_inc(store_open, 1)
                    pool.dma_start(dst, o_st[g % 4][:]).then_inc(mix_stored[g % 4], 16)

            rounds(pool, mixes)

            def residual(j, half, b, first):
                pool.wait_ge(x_again[b], 16 * (half + 1))
                pool.wait_ge(res_gated, j + 1)
                nc.gpsimd.tensor_tensor(resid[b][:], resid[b][:], x_res[b][:], ALU.add).then_inc(res_ready, 1)

            out_walk(pool, residual)

        @block.tensor
        def _(pe):
            def x_tile(j, i, first):
                pe.wait_ge(xn_ready, 4 * j + i + 1)
                if not (first and i < 2):
                    pe.wait_ge(xt_copied[i % 2], 2 * j + i // 2)
                for k in range(KD):
                    m = pe.transpose(psum[:, 2 * (i % 2) + k // 4, (k % 4) * P:(k % 4 + 1) * P],
                                     x_in[i][:, k * P:(k + 1) * P], ident)
                m.then_inc(xt_ready, 1)

            def mod_chunk(j, first):
                if first:
                    pe.wait_ge(c_ready, 1)
                else:
                    pe.wait_ge(mod_added, j)
                for k in range(KD):
                    m = pe.matmul(psum[0:NS + 1, 4, :], c_silu[:, k, :],
                                  ada_w[:, bass.ds(j, 1), k, :].rearrange("p a e -> p (a e)"),
                                  start=(k == 0), stop=(k == KD - 1))
                m.then_inc(mod_mm, 1)

            pe.wait_ge(const_loaded, 16 * 9)
            for i in range(4):
                x_tile(0, i, True)
            pe.wait_ge(ada_loaded[0], 16)
            mod_chunk(0, True)
            with pe.Fori(1, 4) as j:
                for i in range(4):
                    x_tile(j, i, False)
                if True:
                    pe.wait_ge(ada_more, 16 * 3)
                    mod_chunk(j, False)
            pe.wait_ge(xn_ready, 17)
            pe.wait_ge(xt_copied[0], 8)
            for k in range(KD):
                m = pe.transpose(psum[:, 0, NS * k:NS * k + NS], x_in[0][0:NS, k * P:(k + 1) * P], ident[0:NS, 0:NS])
            m.then_inc(xt_ready, 1)
            pe.wait_ge(mod_added, 4)
            for e in range(2 * KD):
                m = pe.transpose(psum[:, 5, (NS + 1) * e:(NS + 1) * (e + 1)], mod_sb[:, e * P:(e + 1) * P],
                                 ident[0:NS + 1, 0:NS + 1])
            m.then_inc(mod_t, 1)

            def three(out, hi, lo, mhi, mlo, start, stop):
                pe.matmul(out, hi, mhi, start=start, stop=False)
                pe.matmul(out, hi, mlo, start=False, stop=False)
                return pe.matmul(out, lo, mhi, start=False, stop=stop)

            def gate_columns(q):
                b = q % 2
                pe.wait_ge(gate_loaded[b], 16 * (q // 2 + 1))
                if q:
                    pe.wait_ge(gate_added, q)
                for k in range(KD):
                    m = pe.matmul(psum[0:NS + 1, 5, 0:256], c_silu[:, k, :], gate_w[b][:, k, :],
                                  start=(k == 0), stop=(k == KD - 1))
                m.then_inc(gate_mm, 1)

            def pool_matmul(n):
                pe.wait_ge(diff_ready, n + 1)
                for m in range(2):
                    mm = pe.matmul(psum[:, 5, CH * m:CH * m + CH], pool_w_sb[:, m, :], diff[:, m, :],
                                   start=True, stop=True)
                mm.then_inc(pool_mm, 1)

            def project(t, b, ts, chunk=None):
                pe.wait_ge(w_ready, t + 1)
                if ts == 0:
                    for k in range(KD):
                        pe.wait_ge(h_ready, k + 1)
                        for g, (c0, c1) in enumerate(GROUPS):
                            m = three(bank(g, c1 - c0), w_hi[b][:, k, :], w_lo[b][:, k, :],
                                      h_hi[:, k, c0:c1], h_lo[:, k, c0:c1], k == 0, k == KD - 1)
                            if k == KD - 1:
                                m.then_inc(group_done, 1)
                    return
                for g, (c0, c1) in enumerate(GROUPS):
                    pe.wait_ge(bank_free[g], t)
                    for k in range(KD):
                        m = three(bank(g, c1 - c0), w_hi[b][:, k, :], w_lo[b][:, k, :],
                                  h_hi[:, k, c0:c1], h_lo[:, k, c0:c1], k == 0, k == KD - 1)
                    m.then_inc(group_done, 1)
                    if g == 2 and chunk is not None:
                        pool_matmul(chunk)

            project(0, 0, 0)
            project(1, 1, 1)
            for q in range(4):
                gate_columns(q)
            with pe.Fori(1, 6) as i:
                for b in range(2):
                    project(2 * i + b, b, 2)
            project(12, 0, 12)
            with pe.Fori(0, NCH // 2) as i:
                for b in range(2):
                    project(CHUNK0 + 1 + 2 * i + b, 1 - b, 13, chunk=2 * i + b)
            project(21, 1, 21)
            with pe.Fori(11, 15) as i:
                for b in range(2):
                    project(2 * i + b, b, 22)

            pe.wait_ge(tail_copied, 1)
            for m in range(2):
                pe.transpose(psum[0:15, 5, P * m:P * m + P], tail_u[:, m, :], ident)
                last = pe.transpose(psum[0:2, 5, 256 + P * m:256 + P * m + P], tail_z[:, m, :], ident)
            last.then_inc(tail_t, 1)

            pe.wait_ge(bank_free[4], NT)
            for x in range(0, len(ZN_TILES), 4):
                if x >= 12:
                    pe.wait_ge(zs_copied, x // 4 - 2)
                for y, t in enumerate(ZN_TILES[x:x + 4]):
                    m = pe.transpose(psum[0:NS, (6, 7, 4)[x // 4 % 3], P * y:P * y + P], zs_t[:, t, :], ident)
                m.then_inc(zs_t_done, 1)

            for g in range(4):
                pe.wait_ge(bank_free[g], NT)

            def kv_turn(j, b, half, first):
                pe.wait_ge(kv_loaded[b], 16 * (half + 1))
                if not first:
                    pe.wait_ge(nat_a, j - 1)
                    pe.wait_ge(nat_v, j - 1)
                for m in range(8):
                    mm = pe.transpose(psum[:, 2 * b + m // 4, (m % 4) * P:(m % 4 + 1) * P], kv_in[b][:, m, :], ident)
                mm.then_inc(kv_t, 1)

            for b in range(2):
                kv_turn(b, b, 0, True)
            with pe.Fori(1, 8) as i:
                for b in range(2):
                    kv_turn(2 * i + b, b, i, False)

            pe.wait_ge(nat_a, 16)
            pe.wait_ge(nat_v, 16)

            def scores(base, n, u, i):
                if u.i == 0 and u.c == 0:
                    pe.wait_ge(qkv_loaded[u.kind], 16 * QKV_DMAS[u.kind] * (i + 1))
                if n >= 2:
                    pe.wait_ge(x_ready, base + n - 1)
                for h in range(2):
                    out = psum[:, S_BANK + n % 2, 256 * h:256 * h + 256]
                    pe.matmul(out, u.q(h), u.keys(kh_st, h), start=True, stop=False)
                    m = pe.matmul(out, u.q(h), u.keys(kl_st, h), start=False, stop=True)
                m.then_inc(s_done, 1)

            def turn_probs(base, n, u):
                pe.wait_ge(p_ready, base + n + 1)
                if n >= 2:
                    pe.wait_ge(pt_copied, base + n - 1)
                for h in range(2):
                    for c, _ in u.halves():
                        k = 2 * h + (c // P if u.full else 0)
                        m = pe.transpose(psum[:, PT_BANK + n % 2, P * k:P * k + P], probs[n % 4][:, h, c:c + P], ident)
                m.then_inc(pt_done, 1)

            def weigh_values(base, gbase, n, u):
                g = n // 4
                pe.wait_ge(pt_copied, base + n + 1)
                if n % 4 == 0 and g >= 2:
                    pe.wait_ge(ot_copied, gbase + g - 1)
                for h in range(2):
                    hs = u.halves()
                    for x, (c, back) in enumerate(hs):
                        k = 2 * h + x
                        m = pe.matmul(psum[64 * h:64 * h + 64, OT_BANK + g % 2, P * (n % 4):P * (n % 4) + P],
                                      u.v(h, back), probs_t[n % 2][:, k, :], start=(x == 0), stop=(x == len(hs) - 1))
                m.then_inc(pv_done, 1)

            def turn_out(gbase, g):
                pe.wait_ge(ot_copied, gbase + g + 1)
                if g:
                    pe.wait_ge(o_copied, gbase + g)
                for x in range(4):
                    m = pe.transpose(psum[:, ON_BANK, P * x:P * x + P], o_t[:, x, :], ident)
                m.then_inc(o_turned, 1)

            def attend(i, us):
                base, gbase, n = 64 * i, 16 * i, len(us)
                for s in range(n + 6):
                    if s < n:
                        scores(base, s, us[s], i)
                    if 2 <= s < n + 2:
                        turn_probs(base, s - 2, us[s - 2])
                    if 3 <= s < n + 3:
                        weigh_values(base, gbase, s - 3, us[s - 3])
                    if s >= 8 and s % 4 == 0:
                        turn_out(gbase, (s - 8) // 4)

            rounds(pe, attend)

            pe.wait_ge(o_copied, UNITS // 4)
            for n in range(2):
                m = pe.matmul(bank(n), consts[0:NS + 1, C_SELP:C_SELP + P], mod_gate[:, 512 * n:512 * n + 512],
                              start=True, stop=True)
            m.then_inc(gate_bc, 1)

            def turn_mix(j):
                pe.wait_ge(mixed, j + 1)
                for m in range(5):
                    mm = pe.transpose(psum[:, 4 + m // 4, (m % 4) * P:(m % 4 + 1) * P], o_mix[:, m * P:m * P + P], ident)
                mm.then_inc(mix_t, 1)

            def out_half(b, n):
                for k in range(Y):
                    c = slice(512 * n, 512 * n + 512)
                    m = three(bank(2 * b + n), y_hi[b][:, k, :], y_lo[b][:, k, :], wo_hi[:, k, c], wo_lo[:, k, c],
                              k == 0, k == Y - 1)
                return m

            def out_step(j, b, turn, first):
                pe.wait_ge(y_split, j + 1)
                if not first:
                    pe.wait_ge(res_gated, j - 1)
                out_half(b, 0)
                if turn:
                    turn_mix(j + 1)
                out_half(b, 1).then_inc(out_mm, 1)

            turn_mix(0)
            pe.wait_ge(wo_split, Y)
            pe.wait_ge(gate_bc_read, 1)
            out_step(0, 0, True, True)
            out_step(1, 1, True, True)
            with pe.Fori(1, 7) as i:
                for b in range(2):
                    out_step(2 * i + b, b, True, False)
            out_step(14, 0, True, False)
            out_step(15, 1, False, False)

            pe.wait_ge(dec_s_ready, 1)
            pe.wait_ge(res_gated, 16)
            for c in range(3):
                pe.transpose(psum[0:48, 6, P * c:P * c + P], dec_s[:, c, :], ident)
            pe.transpose(psum[0:48, 6, 384:408], dec_s4[:], ident[0:24, 0:24])
            pe.transpose(psum[0:32, 7, 0:P], dec_ss[:], ident)
            pe.transpose(psum[0:32, 7, P:136], dec_ss4[:], ident[0:NS, 0:NS]).then_inc(dec_st, 1)
            pe.wait_ge(dec_diff, 1)
            for m in range(2):
                mm = pe.matmul(psum[:, 4, NS * m:NS * m + NS], pool_w_sb[:, m, :], dec_a[:, m, :], start=True, stop=True)
            mm.then_inc(dec_pool, 1)
            pe.wait_ge(dec_pn, 2)
            for c in range(3):
                pe.transpose(psum[:, 6, 48 * c:48 * c + 48], dec_p[:, P * c:P * c + P], ident[0:48, 0:48])
            pe.transpose(psum[0:24, 6, 144:192], dec_p[:, 384:408], ident[0:48, 0:48])
            pe.transpose(psum[:, 7, 0:32], dec_ps[:, 0:P], ident[0:32, 0:32])
            pe.transpose(psum[0:NS, 7, 32:64], dec_ps[:, P:136], ident[0:32, 0:32]).then_inc(dec_pt_done, 1)
            pe.wait_ge(dec_pt_ready, 1)
            pe.wait_ge(dec_v_loaded, 16 * 24)
            for b in range(NS):
                for j in range(3):
                    hs = slice(6 * b + 2 * j, 6 * b + 2 * j + 2)
                    out = psum[:, 0, 6 * b + 2 * j:6 * b + 2 * j + 2]
                    for c in range(3):
                        pe.matmul(out, dec_v[:, b, c, P * j:P * j + P], dec_pt[:, c, hs], start=(c == 0), stop=False)
                    pe.matmul(out, dec_v4[:, P * j:P * j + P], dec_pt4[:, hs], start=False, stop=True)
                for g in range(2):
                    hs = slice(4 * b + 2 * g, 4 * b + 2 * g + 2)
                    out = psum[:, 1, 4 * b + 2 * g:4 * b + 2 * g + 2]
                    pe.matmul(out, dec_sv[:, b, g, :, :], dec_pst[:, hs], start=True, stop=False)
                    mm = pe.matmul(out, dec_sv4[:, g, :, :], dec_pst4[:, hs], start=False, stop=True)
            mm.then_inc(dec_o_done, 1)
            pe.wait_ge(dec_y_ready, 2)
            for n in range(2):
                for k in range(Y):
                    c = slice(512 * n, 512 * n + 512)
                    m = three(psum[0:NS, 2 + n, :], ys_hi[:, k, :], ys_lo[:, k, :], wo_hi[:, k, c], wo_lo[:, k, c], k == 0, k == Y - 1)
            m.then_inc(dec_mm, 1)

        @block.scalar
        def _(act):
            for i in range(4):
                act.dma_start(ada_w[:, i, :, :], wv[:, :, 512 * i:512 * i + 512]).then_inc(
                    ada_loaded[0] if i == 0 else ada_more, 16)
            act.wait_ge(const_loaded, 16 * 9)
            nc.scalar.activation(c_silu[:], c_sb[:], ACT.Silu).then_inc(c_ready, 1)

            def x_round(j, first):
                for i in range(4):
                    act.wait_ge(x_loaded[i], 16 * (j + 1))
                    if not (first and i == 0):
                        act.wait_ge(sumsq, 4 * j + i)
                    nc.scalar.activation(junk[:], x_in[i][:], ACT.Square, accum_out=small[:, i:i + 1]).then_inc(sumsq, 1)
                act.wait_ge(var_ready, j + 1)
                nc.scalar.activation(small[:, 8:12], small[:, 4:8], ACT.Sqrt).then_inc(std_ready, 1)
                for i in (0, 2):
                    act.wait_ge(xt_ready, 4 * j + i + 1)
                    nc.scalar.copy(h_f32[:, :, bass.ds(512 * j + P * i, P)],
                                   psum[:, 0:2, :].rearrange("p b (k t) -> p (b k) t", t=P)).then_inc(xt_copied[0], 1)

            x_round(0, True)
            with act.Fori(1, 4) as j:
                x_round(j, False)
            act.wait_ge(xs_loaded, 16)
            act.wait_ge(sumsq, 16)
            nc.scalar.activation(junk[0:NS, :], x_in[0][0:NS, :], ACT.Square, accum_out=small[0:NS, 0:1]).then_inc(sumsq, 1)
            act.wait_ge(var_ready, 5)
            nc.scalar.activation(small[0:NS, 8:9], small[0:NS, 4:5], ACT.Sqrt).then_inc(std_ready, 1)
            act.wait_ge(xt_ready, 17)
            nc.scalar.copy(h_f32[:, :, T:TT], psum[:, 0, 0:NS * KD].rearrange("p (k s) -> p k s", s=NS)).then_inc(
                xt_copied[0], 1)

            def split_w(t, half, ts):
                b = ts % 2
                act.wait_ge(w_loaded[b], 16 * (half + 1))
                if ts >= 2:
                    act.wait_ge(group_done, 5 * (t - 1))
                nc.scalar.copy(w_hi[b][:], w_raw[b][:]).then_inc(w_hi_ready, 1)

            split_w(0, 0, 0)
            for k in range(KD):
                act.wait_ge(h_aff, k + 2)
                nc.scalar.copy(h_hi[:, k, :], h_f32[:, k, :]).then_inc(h_hi_ready, 1)

            def evac(t, half, ts, kind):
                b = ts % 2
                if ts + 1 < NT:
                    split_w(t + 1, half + ts % 2, ts + 1)
                if kind == "plain":
                    return
                if ts >= 2:
                    act.wait_ge(main_stored[b], 16 * half)
                for g, (c0, c1) in enumerate(GROUPS):
                    n = min(c1, T) - c0
                    act.wait_ge(group_done, 5 * t + g + 1)
                    if kind == "gate":
                        m = nc.scalar.activation(main[b][:, c0:c0 + n], bank(g, n), ACT.Silu)
                        m.then_inc(act_evac if g == 4 else bank_free[g], 1)
                    else:
                        nc.scalar.activation(main_hi[b][:, c0:c0 + n], bank(g, n), ACT.Copy,
                                             scale=-0.125 if kind == "q" else 1.0).then_inc(act_evac, 1)

            walk(act, evac)

            def nat(i, b, first):
                act.wait_ge(kv_t, 2 * i + b + 1)
                if not first:
                    act.wait_ge(nat_stored[b], 48 * i)
                nc.scalar.copy(kv_nat[b][:, 0:4, :], bank(2 * b).rearrange("p (m c) -> p m c", c=P)).then_inc(nat_a, 1)

            for b in range(2):
                act.wait_ge(main_stored[b], 16 * 15)
                act.wait_ge(lo_stored[b], 16 * (4 + b))
            act.wait_ge(group_done, 5 * NT)
            attention_qk(act, 0, 0)
            for b in range(2):
                nat(0, b, True)
            with act.Fori(1, 8) as i:
                for b in range(2):
                    nat(i, b, False)

            def attend(i, us):
                base, gbase, n = 64 * i, 16 * i, len(us)
                for s in range(n + 7):
                    if s < n:
                        u = us[s]
                        act.wait_ge(x_ready, base + s + 1)
                        if s >= 4:
                            act.wait_ge(pt_done, base + s - 3)
                        for h in range(2):
                            st = o_st[s // 4 % 4]
                            m = nc.scalar.activation(probs[s % 4][:, h, u.cols()], xs_[s % 2][:, h, u.cols()], ACT.Exp,
                                                     scale=-1.0, bias=st[:, s % 4, 128 + 2 * h:129 + 2 * h],
                                                     accum_out=st[:, s % 4, 129 + 2 * h:130 + 2 * h])
                        m.then_inc(p_ready, 1)
                    if s >= 7 and (s - 7) % 4 == 0 and (s - 7) // 4 < n // 4:
                        copy_ot(base, gbase, (s - 7) // 4)
                    if s >= 9 and (s - 9) % 4 == 0 and (s - 9) // 4 < n // 4:
                        copy_o(gbase, (s - 9) // 4)

            def copy_ot(base, gbase, g):
                act.wait_ge(pv_done, base + 4 * g + 4)
                if g:
                    act.wait_ge(o_turned, gbase + g)
                nc.scalar.copy(o_t[:], bank(OT_BANK + g % 2).rearrange("p (x q) -> p x q", q=P)).then_inc(ot_copied, 1)

            def copy_o(gbase, g):
                act.wait_ge(o_turned, gbase + g + 1)
                nc.scalar.copy(o_st[g % 4][:, :, 0:P], bank(ON_BANK).rearrange("p (x q) -> p x q", q=P)).then_inc(
                    o_copied, 1)

            rounds(act, attend)

            act.wait_ge(o_turned, UNITS // 4)
            for k in range(Y):
                act.wait_ge(wo_loaded[k % 2], 16 * (k // 2 + 1))
                nc.scalar.copy(wo_hi[:, k, :], wo_raw[k % 2][:]).then_inc(wo_hi_ready, 1)

            def out_a(j, b):
                act.wait_ge(arg_ready, j + 1)
                nc.scalar.activation(fac[:, 0:22], fac[:, 0:22], ACT.Exp).then_inc(exp_ready, 1)

            def out_b(j, b, first):
                act.wait_ge(yt_ready, j + 1)
                if not first:
                    act.wait_ge(out_mm, j - 1)
                nc.scalar.copy(y_hi[b][:], y_t[b][:]).then_inc(yh_ready, 1)

            def out_c(j, b):
                act.wait_ge(res_ready, j + 1)
                nc.scalar.activation(junk_o[:], resid[b][:], ACT.Square, accum_out=fin[:, 0:1]).then_inc(sq_ready, 1)
                act.wait_ge(fvar_ready, j + 1)
                nc.scalar.activation(fin[:, 2:3], fin[:, 1:2], ACT.Sqrt).then_inc(fstd_ready, 1)

            out_a(0, 0)
            out_b(0, 0, True)
            out_a(1, 1)
            out_b(1, 1, True)
            with act.Fori(1, 8) as i:
                for b in range(2):
                    out_a(2 * i + b, b)
                    out_c(2 * i + b - 2, b)
                    out_b(2 * i + b, b, False)
            out_c(14, 0)
            out_c(15, 1)

            act.wait_ge(y_ready, 16)
            for b in range(2):
                act.wait_ge(y_stored[b], 16 * 8)
            nc.scalar.activation(dec_g[:], zs_t[:, GATE0:V0, :], ACT.Silu).then_inc(dec_gate, 1)
            act.wait_ge(dec_neg, 2)
            nc.scalar.activation(dec_p[:], psum[0:48, 6, 0:408], ACT.Exp, bias=dec_small[0:48, 0:1],
                                 accum_out=dec_small[0:48, 1:2]).then_inc(dec_exp, 1)
            nc.scalar.activation(dec_ps[:], psum[0:32, 7, 0:136], ACT.Exp, bias=dec_small[0:32, 4:5],
                                 accum_out=dec_small[0:32, 5:6]).then_inc(dec_exp, 1)
            nc.scalar.activation(dec_small[0:32, 6:7], sink_col[:], ACT.Exp, bias=dec_small[0:32, 4:5]).then_inc(dec_exp, 1)
            act.wait_ge(dec_y_full, 1)
            nc.scalar.copy(ys_hi[:], dec_y[:]).then_inc(dec_y_ready, 1)
            act.wait_ge(dec_res, 1)
            nc.scalar.activation(dec_prod[0:NS, 0:D], dec_r[:], ACT.Square, accum_out=dec_small[0:NS, 8:9]).then_inc(
                dec_sq_ready, 1)
            act.wait_ge(dec_var, 1)
            nc.scalar.activation(dec_small[0:NS, 10:11], dec_small[0:NS, 9:10], ACT.Sqrt).then_inc(dec_std, 1)

        @block.vector
        def _(dve):
            links = [0]

            def link(ins):
                links[0] += 1
                ins.then_inc(dve_link, 1)
                dve.wait_ge(dve_link, links[0])

            def x_round(j):
                dve.wait_ge(sumsq, 4 * j + 4)
                dve.tensor_scalar(small[:, 4:8], small[:, 0:4], 1.0 / D, EPS, ALU.mult, ALU.add).then_inc(var_ready, 1)
                dve.wait_ge(std_ready, j + 1)
                dve.reciprocal(small[:, 12:16], small[:, 8:12]).then_inc(rstd_ready, 1)
                dve.wait_ge(rstd_ready, j + 1)
                for i in range(4):
                    dve.tensor_scalar(x_in[i][:], x_in[i][:], small[:, 12 + i:13 + i], None, ALU.mult).then_inc(
                        xn_ready, 1)
                for i in (1, 3):
                    dve.wait_ge(xt_ready, 4 * j + i + 1)
                    dve.tensor_copy(h_f32[:, :, bass.ds(512 * j + P * i, P)],
                                    psum[:, 2:4, :].rearrange("p b (k t) -> p (b k) t", t=P)).then_inc(xt_copied[1], 1)

            def mod_add(j):
                dve.wait_ge(mod_mm, j + 1)
                dve.tensor_tensor(mod_sb[:, bass.ds(512 * j, 512)], psum[0:NS + 1, 4, :],
                                  b_mod[:, bass.ds(512 * j, 512)], ALU.add).then_inc(mod_added, 1)

            dve.wait_ge(const_loaded, 16 * 9)
            x_round(0)
            mod_add(0)
            with dve.Fori(1, 4) as j:
                x_round(j)
                mod_add(j)
            dve.wait_ge(sumsq, 17)
            dve.tensor_scalar(small[0:NS, 4:5], small[0:NS, 0:1], 1.0 / D, EPS, ALU.mult, ALU.add).then_inc(var_ready, 1)
            dve.wait_ge(std_ready, 5)
            link(dve.reciprocal(small[0:NS, 12:13], small[0:NS, 8:9]))
            dve.tensor_scalar(x_in[0][0:NS, :], x_in[0][0:NS, :], small[0:NS, 12:13], None, ALU.mult).then_inc(xn_ready, 1)
            dve.wait_ge(mod_t, 1)
            mod_ps = psum[:, 5, 0:2 * KD * (NS + 1)].rearrange("p (e n) -> p e n", n=NS + 1)
            dve.tensor_copy(mod_shift[:], mod_ps[:, 0:KD, :])
            link(dve.scalar_tensor_tensor(mod_scale[:], mod_ps[:, KD:2 * KD, :], 1.0,
                                          g_t[:].unsqueeze(2).broadcast_to([P, KD, NS + 1]), ALU.add, ALU.mult))
            dve.wait_ge(xt_copied[0], 9)
            dve.wait_ge(xt_copied[1], 8)
            dve_s = h_f32[:, :, T:TT]
            link(dve.tensor_tensor(dve_s, dve_s, mod_scale[:, :, 0:NS], ALU.mult))
            dve.tensor_tensor(dve_s, dve_s, mod_shift[:, :, 0:NS], ALU.add).then_inc(h_aff, 1)

            def split_w(t):
                b = t[1] % 2
                dve.wait_ge(w_hi_ready, t[0] + 1)
                dve.tensor_tensor(w_lo[b][:], w_raw[b][:], w_hi[b][:].bitcast(F32), ALU.subtract).then_inc(w_ready, 1)

            split_w((0, 0))
            def affine(k):
                dve.tensor_scalar(h_f32[:, k, 0:T], h_f32[:, k, 0:T], mod_scale[:, k, NS:NS + 1],
                                  mod_shift[:, k, NS:NS + 1], ALU.mult, ALU.add).then_inc(h_aff, 1)
            affine(0)
            for k in range(KD):
                if k + 1 < KD:
                    affine(k + 1)
                dve.wait_ge(h_hi_ready, k + 1)
                dve.tensor_tensor(h_lo[:, k, :], h_f32[:, k, :], h_hi[:, k, :].bitcast(F32), ALU.subtract).then_inc(
                    h_ready, 1)

            def chunk(n):
                if n == 0:
                    for t_, w in ((u_in, HALO), (ch_in, 2), (cc_in, 2)):
                        link(dve.memset(t_[:, :, 0:w], 0.0))
                dve.wait_ge(chunk_loaded, 80 * (n + 1))
                W = HALO + CH
                link(dve.tensor_tensor(sum_a[:, :, 1:W], u_in[:, :, 1:W], u_in[:, :, 0:W - 1], ALU.add))
                link(dve.tensor_tensor(sum_b[:, :, 3:W], sum_a[:, :, 3:W], sum_a[:, :, 1:W - 2], ALU.add))
                link(dve.tensor_tensor(sum_a[:, 1, 7:W], sum_b[:, 1, 7:W], sum_b[:, 1, 3:W - 4], ALU.add))
                link(dve.tensor_tensor(sum_b[:, 1, 15:W], sum_a[:, 1, 15:W], sum_a[:, 1, 7:W - 8], ALU.add))
                for m in range(2):
                    for half, s in ((0, sum_a), (1, sum_b)):
                        r = slice(64 * half, 64 * half + 64)
                        last = dve.scalar_tensor_tensor(diff[r, m, :], s[r, m, HALO:W], 1.0 / (2, 4, 8, 16)[2 * m + half],
                                                        u_in[r, m, HALO:W], ALU.mult, ALU.subtract)
                if n == 0:
                    link(last)
                    for half, s in ((0, sum_a), (1, sum_b)):
                        r = slice(64 * half, 64 * half + 64)
                        rc = consts[r, C_RCF:C_RCF + 32].rearrange("p (m t) -> p m t", m=2)
                        link(dve.tensor_tensor(s[r, :, 0:16], s[r, :, HALO:HALO + 16], rc, ALU.mult))
                        last = dve.tensor_tensor(diff[r, :, 0:16], s[r, :, 0:16], u_in[r, :, HALO:HALO + 16], ALU.subtract)
                last.then_inc(diff_ready, 1)
                link(dve.tensor_tensor(ch_in[:], ch_in[:], cc_in[:], ALU.mult))
                for m in range(2):
                    for j in range(3):
                        z = ch_in[:, m, j:j + CH]
                        wj = conv_w_t[:, m, j:j + 1]
                        acc = cc_in[:, m, 0:CH]
                        if j == 0:
                            ins = dve.tensor_scalar(acc, z, wj, None, ALU.mult)
                        else:
                            ins = dve.scalar_tensor_tensor(acc, z, wj, acc, ALU.mult, ALU.add)
                        link(ins)
                link(dve.tensor_tensor(cc_in[:, :, 0:CH], cc_in[:, :, 0:CH], cb_in[:], ALU.mult))
                if n:
                    dve.wait_ge(yac_stored, 16 * n)
                dve.tensor_tensor(yac[:, 2:4, :], cc_in[:, :, 0:CH], gate_in[:, 2:4, :], ALU.mult)
                if n == NCH - 1:
                    dve.tensor_copy(tail_u[:], u_in[:, :, HALO + CH - 15:HALO + CH])
                    dve.tensor_copy(tail_z[:], ch_in[:, :, CH:CH + 2]).then_inc(tail_copied, 1)
                dve.wait_ge(pool_mm, n + 1)
                for m in range(2):
                    last = dve.scalar_tensor_tensor(yac[:, m, :], psum[:, 5, CH * m:CH * m + CH], pool_scale_t[:, m:m + 1],
                                                    gate_in[:, m, :], ALU.mult, ALU.mult)
                last.then_inc(yac_ready, 1)

            def evac(t, half, ts, kind):
                b = ts % 2
                if ts + 1 < NT:
                    split_w((t + 1, ts + 1))
                if kind == "plain" and ts >= 2:
                    dve.wait_ge(main_stored[b], 16 * half)
                if ts == Q0:
                    dve.wait_ge(yac_stored, 16 * NCH)
                if ts >= Q0 + 2:
                    dve.wait_ge(lo_stored[b], 16 * ((ts - Q0) // 2))
                if ts > K0:
                    dve.wait_ge(knat_stored, 16 * (ts - K0))
                for g, (c0, c1) in enumerate(GROUPS):
                    n = min(c1, T) - c0
                    if kind == "plain":
                        dve.wait_ge(group_done, 5 * t + g + 1)
                        last = dve.tensor_copy(main[b][:, c0:c0 + n], bank(g, n))
                    elif kind == "gate":
                        if g < 4:
                            continue
                        dve.wait_ge(act_evac, t - GATE0 + 1)
                    else:
                        dve.wait_ge(act_evac, V0 - GATE0 + 5 * (ts - Q0) + g + 1)
                        last = dve.scalar_tensor_tensor(main_lo[b][:, c0:c0 + n], bank(g, n),
                                                        -0.125 if kind == "q" else 1.0,
                                                        main_hi[b][:, c0:c0 + n].bitcast(F32), ALU.mult, ALU.subtract)
                        if kind == "k":
                            last = dve.tensor_copy(k_nat[:, c0:c0 + n], bank(g, n))
                    if g == 4:
                        dve.tensor_copy(zs_t[:, bass.ds(t, 1), :].rearrange("p a s -> p (a s)"),
                                        psum[:, g, n:n + NS]).then_inc(bank_free[g], 1)
                    else:
                        last.then_inc(bank_free[g], 1)
                if 0 <= ts - CHUNK0 < NCH:
                    chunk(ts - CHUNK0)
                if ts == 1:
                    for q in range(4):
                        dve.wait_ge(gate_mm, q + 1)
                        dve.tensor_tensor(mod_gate[:, 256 * q:256 * q + 256], psum[0:NS + 1, 5, 0:256],
                                          b_gate[:, 256 * q:256 * q + 256], ALU.add).then_inc(gate_added, 1)

            walk(dve, evac)

            def nat(i, b, first):
                dve.wait_ge(kv_t, 2 * i + b + 1)
                if not first:
                    dve.wait_ge(nat_stored[b], 48 * i)
                dve.tensor_copy(kv_nat[b][:, 4:8, :], bank(2 * b + 1).rearrange("p (m c) -> p m c", c=P)).then_inc(
                    nat_v, 1)

            for x in range(0, len(ZN_TILES), 4):
                dve.wait_ge(zs_t_done, x // 4 + 1)
                n = P * min(4, len(ZN_TILES) - x)
                dve.tensor_copy(zn[:, P * x:P * x + n], psum[0:NS, (6, 7, 4)[x // 4 % 3], 0:n]).then_inc(zs_copied, 1)
            dve.wait_ge(tail_t, 1)
            dve.tensor_copy(tail_rows[:, 0:256], psum[0:15, 5, 0:256])
            dve.tensor_copy(tail_rows[0:2, 256:512], psum[0:2, 5, 256:512]).then_inc(zs_copied, 1)
            dve.wait_ge(zs_copied, 6)
            dve.tensor_tensor(zc_s[:], zn[:, 256:512], zn[:, 512:768], ALU.mult).then_inc(zc_ready, 1)

            for b in range(2):
                nat(0, b, True)
            with dve.Fori(1, 8) as i:
                for b in range(2):
                    nat(i, b, False)

            for b in range(2):
                dve.wait_ge(main_stored[b], 16 * 15)
                dve.wait_ge(lo_stored[b], 16 * (4 + b))
            dve.wait_ge(knat_stored, 16 * 4)
            dve.wait_ge(zs_stored, 16 * ZS_STORES)
            dve.tensor_scalar(neg_sink[:], neg_sink[:], -1.0, None, ALU.mult).then_inc(sink_negated, 1)
            dve.wait_ge(sink_negated, 1)

            def pair_tables(i, kind):
                off = consts[:, C_OFF:C_OFF + 256]
                for h in range(2):
                    if kind == 0:
                        slope = consts[:, bass.ds(C_SLD + 2 * i + h, 1)]
                        for c, d in enumerate(DILATIONS):
                            last = dve.tensor_scalar(bias_dil[:, c, h, :], off, slope, float(d), ALU.mult, ALU.mult)
                    else:
                        slope = consts[:, bass.ds(C_SLS + 2 * i + h, 1)]
                        last = dve.tensor_scalar(bias_swa[:, h, :], off, slope, None, ALU.mult)
                if kind:
                    last = dve.tensor_copy(sink_now[:], neg_sink[:, bass.ds(2 * i, 2)])
                last.then_inc(bias_ready, 1)
                dve.wait_ge(bias_ready, 2 * i + kind + 1)

            def attend(i, us):
                base, gbase, n = 64 * i, 16 * i, len(us)
                for s in range(n + 3):
                    if s >= 3:
                        u = us[s - 3]
                        dve.wait_ge(pt_done, base + s - 2)
                        if s >= 5:
                            dve.wait_ge(pv_done, base + s - 4)
                        src = bank(PT_BANK + (s - 3) % 2).rearrange("p (k q) -> p k q", q=P)
                        dst = probs_t[(s - 3) % 2]
                        if u.full:
                            dve.tensor_copy(dst[:], src).then_inc(pt_copied, 1)
                        else:
                            dve.tensor_copy(dst[:, 0:4:2, :], src[:, 0:4:2, :]).then_inc(pt_copied, 1)
                    if s < n:
                        u = us[s]
                        g = s // 4
                        if u.i == 0 and u.c == 0:
                            pair_tables(i, u.kind)
                        dve.wait_ge(s_done, base + s + 1)
                        if s >= 2:
                            dve.wait_ge(p_ready, base + s - 1)
                        if s % 4 == 0 and g >= 4:
                            dve.wait_ge(mix_stored[g % 4], 16 * (4 * i + g // 4))
                        dve.sem_inc(unit_open, 1)
                        for h in range(2):
                            c = u.cols()
                            m = dve.tensor_tensor_reduce(
                                out=xs_[s % 2][:, h, c], in0=psum[:, S_BANK + s % 2, 256 * h + c.start:256 * h + c.stop],
                                in1=u.bias(h), scale=1.0, scalar=sink_now[:, h:h + 1] if u.kind else 3.0e38,
                                op0=ALU.add, op1=ALU.min,
                                accum_out=o_st[g % 4][:, s % 4, 128 + 2 * h:129 + 2 * h])
                        m.then_inc(x_ready, 1)
                for b in range(4):
                    dve.wait_ge(mix_stored[b], 16 * (4 * i + len(us) // 16))

            rounds(dve, attend)

            dve.wait_ge(gate_bc, 1)
            dve.tensor_copy(gate_all[:], psum[:, 0:2, :].rearrange("p a b -> p (a b)")).then_inc(gate_bc_read, 1)
            for k in range(Y):
                dve.wait_ge(wo_hi_ready, k + 1)
                dve.tensor_tensor(wo_lo[:, k, :], wo_raw[k % 2][:], wo_hi[:, k, :].bitcast(F32), ALU.subtract).then_inc(
                    wo_split, 1)
            dve.wait_ge(fg_loaded, 16)

            LINKS = 10

            def combine(j, half, b, first):
                n = [0]

                def olink(ins):
                    n[0] += 1
                    ins.then_inc(out_link, 1)
                    dve.wait_ge(out_link, LINKS * j + n[0])

                dve.wait_ge(tile_in[b], 64 * (half + 1))
                st = mix_in[b][:, :, :, P:132].rearrange("p c j (h s) -> p c j h s", s=2)
                ss = swa_in[b][:, :, P:132].rearrange("p j (h s) -> p j h s", s=2)
                v6 = lambda a: fac[:, a:a + 6].rearrange("p (j h) -> p j h", h=2)
                v4 = lambda a: fac[:, a:a + 4].rearrange("p (j h) -> p j h", h=2)
                olink(dve.tensor_tensor(v6(24), st[:, 0, :, :, 0], st[:, 1, :, :, 0], ALU.min))
                olink(dve.tensor_tensor(v6(24), v6(24), st[:, 2, :, :, 0], ALU.min))
                for c in range(3):
                    dve.tensor_tensor(v6(6 * c), v6(24), st[:, c, :, :, 0], ALU.subtract)
                sinks = neg_sink[:].rearrange("p (j h) -> p j h", h=2)
                dve.tensor_tensor(v4(18), ss[:, :, :, 0], sinks, ALU.subtract).then_inc(arg_ready, 1)
                dve.wait_ge(exp_ready, j + 1)
                for c in range(3):
                    last = dve.tensor_tensor(v6(30 + 6 * c), v6(6 * c), st[:, c, :, :, 1], ALU.mult)
                olink(last)
                olink(dve.tensor_tensor(v6(48), v6(30), v6(36), ALU.add))
                dve.tensor_tensor(v6(48), v6(48), v6(42), ALU.add)
                olink(dve.tensor_tensor(v4(54), v4(18), ss[:, :, :, 1], ALU.add))
                olink(dve.reciprocal(fac[:, 48:58], fac[:, 48:58]))
                olink(dve.tensor_tensor(fac[:, 0:18].rearrange("p (c x) -> p c x", c=3),
                                        fac[:, 0:18].rearrange("p (c x) -> p c x", c=3),
                                        fac[:, 48:54].unsqueeze(1).broadcast_to([P, 3, 6]), ALU.mult))
                if not (first and b == 0):
                    dve.wait_ge(mix_t, j)
                src = lambda c: mix_in[b][:, c, :, 0:P].rearrange("p j (h e) -> p j h e", e=64)
                f = lambda a: fac[:, a:a + 6].rearrange("p (j h) -> p j h", h=2).unsqueeze(3).broadcast_to([P, 3, 2, 64])
                om = o_mix[:, 0:384].rearrange("p (j h e) -> p j h e", h=2, e=64)
                op_ = o_part[:].rearrange("p (j h e) -> p j h e", h=2, e=64)
                dve.tensor_tensor(om, src(0), f(0), ALU.mult)
                dve.tensor_tensor(o_mix[:, 384:640].rearrange("p (j h e) -> p j h e", h=2, e=64),
                                  swa_in[b][:, :, 0:P].rearrange("p j (h e) -> p j h e", e=64),
                                  fac[:, 54:58].rearrange("p (j h) -> p j h", h=2).unsqueeze(3).broadcast_to([P, 2, 2, 64]),
                                  ALU.mult)
                olink(dve.tensor_tensor(op_, src(1), f(6), ALU.mult))
                olink(dve.tensor_tensor(o_mix[:, 0:384], o_mix[:, 0:384], o_part[:], ALU.add))
                olink(dve.tensor_tensor(op_, src(2), f(12), ALU.mult))
                dve.tensor_tensor(o_mix[:, 0:384], o_mix[:, 0:384], o_part[:], ALU.add).then_inc(mixed, 1)
                assert n[0] == LINKS, n[0]

            def gate_mix(j, b):
                dve.wait_ge(mix_t, j + 1)
                dve.tensor_tensor(y_t[b][:, 4:8, :], bank(4).rearrange("p (m t) -> p m t", t=P), gates[b][:, 0:4, :], ALU.mult)
                dve.tensor_tensor(y_t[b][:, 8, :], bank(5, P), gates[b][:, 4, :], ALU.mult).then_inc(yt_ready, 1)

            def split_y(j, b):
                dve.wait_ge(yh_ready, j + 1)
                dve.tensor_tensor(y_lo[b][:], y_t[b][:], y_hi[b][:].bitcast(F32), ALU.subtract).then_inc(y_split, 1)

            def gate_out(j, b):
                dve.wait_ge(out_mm, j + 1)
                dve.tensor_tensor(resid[b][:], psum[:, 2 * b:2 * b + 2, :].rearrange("p a c -> p (a c)"), gate_all[:],
                                  ALU.mult).then_inc(res_gated, 1)

            def final_norm(j, half, b, first):
                dve.wait_ge(sq_ready, j + 1)
                dve.tensor_scalar(fin[:, 1:2], fin[:, 0:1], 1.0 / D, EPS, ALU.mult, ALU.add).then_inc(fvar_ready, 1)
                dve.wait_ge(fstd_ready, j + 1)
                dve.reciprocal(fin[:, 3:4], fin[:, 2:3]).then_inc(rec_ready, 1)
                dve.wait_ge(rec_ready, j + 1)
                if not first:
                    dve.wait_ge(y_stored[b], 16 * half)
                dve.scalar_tensor_tensor(y_out[b][:], resid[b][:], fin[:, 3:4], final_g_sb[:], ALU.mult, ALU.mult).then_inc(
                    y_ready, 1)

            for b in range(2):
                combine(b, 0, b, True)
                gate_mix(b, b)
                split_y(b, b)
            for b in range(2):
                gate_out(b, b)
                combine(2 + b, 1, b, False)
                final_norm(b, 0, b, True)
                gate_mix(2 + b, b)
                split_y(2 + b, b)
            with dve.Fori(2, 8) as i:
                for b in range(2):
                    gate_out(2 * i + b - 2, b)
                    combine(2 * i + b, i, b, False)
                    final_norm(2 * i + b - 2, i - 1, b, False)
                    gate_mix(2 * i + b, b)
                    split_y(2 * i + b, b)
            for b in range(2):
                gate_out(14 + b, b)
                final_norm(14 + b, 7, b, False)

            dve.wait_ge(y_ready, 16)
            dve.wait_ge(out_mm, 16)
            for b in range(2):
                dve.wait_ge(y_stored[b], 16 * 8)
            dve.wait_ge(dec_loaded, 16 * DEC_LOADS)
            for b in range(NS):
                dve.wait_ge(dec_k_loaded[b % 2], 48 * (b // 2 + 1))
                prod = dec_prod[:, 0:1152].rearrange("p (c e) -> p c e", c=3)
                link(dve.tensor_tensor(prod, dec_k[b % 2][:], dec_q[:, b, :].unsqueeze(1).broadcast_to([P, 3, 384]), ALU.mult))
                link(dve.tensor_reduce(dec_s[:, :, 6 * b:6 * b + 6], prod.rearrange("p c (h e) -> p c h e", e=64), AX.X, ALU.add))
                dve.sem_inc(dec_k_used, 1)
            p4 = dec_prod[0:24, :]
            link(dve.tensor_tensor(p4.rearrange("p (s e) -> p s e", s=NS), dec_q[0:24],
                                   dec_k4[:].unsqueeze(1).broadcast_to([24, NS, 384]), ALU.mult))
            link(dve.tensor_reduce(dec_s4[:], p4.rearrange("p (x e) -> p x e", e=64), AX.X, ALU.add))
            pz = dec_prod[:, 0:2048]
            link(dve.tensor_tensor(pz, dec_sq[:], dec_sk[:].rearrange("p s g x e -> p (s g x e)"), ALU.mult))
            link(dve.tensor_reduce(dec_ss[:], pz.rearrange("p (x e) -> p x e", e=64), AX.X, ALU.add))
            p8 = dec_prod[0:NS, 0:2048]
            link(dve.tensor_tensor(p8.rearrange("p (s e) -> p s e", s=NS), dec_sq[0:NS].rearrange("p (s e) -> p s e", s=NS),
                                   dec_sk4[:].rearrange("p g x e -> p (g x e)").unsqueeze(1).broadcast_to([NS, NS, 256]),
                                   ALU.mult))
            link(dve.tensor_reduce(dec_ss4[:], p8.rearrange("p (x e) -> p x e", e=64), AX.X, ALU.add))
            heads = lambda ap, n: ap.rearrange("p (s h) -> p s h", h=n)
            for c in range(3):
                bias = consts[:, C_DB + 6 * c:C_DB + 6 * c + 6].unsqueeze(1).broadcast_to([P, NS, 6])
                v = heads(dec_s[:, c, :], 6)
                dve.scalar_tensor_tensor(v, v, 0.125, bias, ALU.mult, ALU.add)
            v = heads(dec_s4[:], 6)
            dve.scalar_tensor_tensor(v, v, 0.125, consts[0:24, C_NEW:C_NEW + NS].unsqueeze(2).broadcast_to([24, NS, 6]),
                                     ALU.mult, ALU.add)
            v = heads(dec_ss[:], 4)
            dve.scalar_tensor_tensor(v, v, 0.125, consts[:, C_SB:C_SB + 4].unsqueeze(1).broadcast_to([P, NS, 4]),
                                     ALU.mult, ALU.add)
            v = heads(dec_ss4[:], 4)
            dve.scalar_tensor_tensor(v, v, 0.125, consts[0:NS, C_NEW:C_NEW + NS].unsqueeze(2).broadcast_to([NS, NS, 4]),
                                     ALU.mult, ALU.add).then_inc(dec_s_ready, 1)
            u_new = zs_t[:, 0:2, :]
            for m in range(2):
                for half in range(2):
                    w = (2, 4, 8, 16)[2 * m + half]
                    r = slice(64 * half, 64 * half + 64)
                    last = dve.tensor_reduce(dec_a[r, m, :], dec_state[r, m, :, 16 - w:15], AX.X, ALU.add)
            link(last)
            link(dve.tensor_tensor(dec_a[:], dec_a[:], u_new, ALU.add))
            for m in range(2):
                last = dve.scalar_tensor_tensor(dec_a[:, m, :], dec_a[:, m, :], consts[:, C_INVW + m:C_INVW + m + 1],
                                                u_new[:, m, :], ALU.mult, ALU.subtract)
            last.then_inc(dec_diff, 1)
            link(dve.tensor_tensor(dec_b[:], zs_t[:, 2:4, :], zs_t[:, 4:6, :], ALU.mult))
            for m in range(2):
                link(dve.tensor_scalar(dec_b[:, m, :], dec_b[:, m, :], conv_w_t[:, m, 2:3], None, ALU.mult))
                for j in (1, 0):
                    link(dve.scalar_tensor_tensor(dec_b[:, m, :], dec_conv[:, m, :, j], conv_w_t[:, m, j:j + 1],
                                                  dec_b[:, m, :], ALU.mult, ALU.add))
            link(dve.tensor_tensor(dec_b[:], dec_b[:], zs_t[:, 6:8, :], ALU.mult))
            dve.wait_ge(dec_gate, 1)
            dve.tensor_tensor(dec_y[:, 2:4, :], dec_b[:], dec_g[:, 2:4, :], ALU.mult)
            dve.wait_ge(dec_pool, 1)
            for m in range(2):
                dve.scalar_tensor_tensor(dec_y[:, m, :], psum[:, 4, NS * m:NS * m + NS], pool_scale_t[:, m:m + 1],
                                         dec_g[:, m, :], ALU.mult, ALU.mult)
            dve.wait_ge(dec_st, 1)
            dve.tensor_reduce(dec_small[0:48, 0:1], psum[0:48, 6, 0:408], AX.X, ALU.max, negate=True).then_inc(dec_neg, 1)
            link(dve.tensor_reduce(dec_small[0:32, 4:5], psum[0:32, 7, 0:136], AX.X, ALU.max, negate=True))
            link(dve.tensor_scalar(dec_small[0:32, 7:8], sink_col[:], -1.0, None, ALU.mult))
            dve.tensor_tensor(dec_small[0:32, 4:5], dec_small[0:32, 4:5], dec_small[0:32, 7:8], ALU.min).then_inc(dec_neg, 1)
            dve.wait_ge(dec_exp, 3)
            link(dve.reciprocal(dec_small[0:48, 2:3], dec_small[0:48, 1:2]))
            dve.tensor_scalar(dec_p[:], dec_p[:], dec_small[0:48, 2:3], None, ALU.mult).then_inc(dec_pn, 1)
            link(dve.tensor_tensor(dec_small[0:32, 5:6], dec_small[0:32, 5:6], dec_small[0:32, 6:7], ALU.add))
            link(dve.reciprocal(dec_small[0:32, 5:6], dec_small[0:32, 5:6]))
            dve.tensor_scalar(dec_ps[:], dec_ps[:], dec_small[0:32, 5:6], None, ALU.mult).then_inc(dec_pn, 1)
            dve.wait_ge(dec_pt_done, 1)
            dve.tensor_copy(dec_pt[:], psum[:, 6, 0:144].rearrange("p (c x) -> p c x", c=3))
            dve.tensor_copy(dec_pt4[:], psum[0:24, 6, 144:192])
            dve.tensor_copy(dec_pst[:], psum[:, 7, 0:32])
            dve.tensor_copy(dec_pst4[:], psum[0:NS, 7, 32:64]).then_inc(dec_pt_ready, 1)
            dve.wait_ge(dec_o_done, 1)
            for half in range(2):
                r = slice(64 * half, 64 * half + 64)
                o6 = psum[r, 0, 0:48].rearrange("p (s j x) -> p x j s", j=3, x=2)[:, half]
                dve.tensor_tensor(dec_y[r, 4:7, :], o6, dec_g[r, 4:7, :], ALU.mult)
                o4 = psum[r, 1, 0:32].rearrange("p (s j x) -> p x j s", j=2, x=2)[:, half]
                last = dve.tensor_tensor(dec_y[r, 7:9, :], o4, dec_g[r, 7:9, :], ALU.mult)
            last.then_inc(dec_y_full, 1)
            dve.wait_ge(dec_y_ready, 1)
            dve.tensor_tensor(ys_lo[:], dec_y[:], ys_hi[:].bitcast(F32), ALU.subtract).then_inc(
                dec_y_ready, 1)
            dve.wait_ge(dec_mm, 1)
            for n in range(2):
                c = slice(512 * n, 512 * n + 512)
                last = dve.tensor_tensor(dec_r[:, c], psum[0:NS, 2 + n, :], mod_gate[0:NS, c], ALU.mult)
            link(last)
            dve.tensor_tensor(dec_r[:], dec_r[:], dec_x[:], ALU.add).then_inc(dec_res, 1)
            dve.wait_ge(dec_sq_ready, 1)
            dve.tensor_scalar(dec_small[0:NS, 9:10], dec_small[0:NS, 8:9], 1.0 / D, EPS, ALU.mult, ALU.add).then_inc(dec_var, 1)
            dve.wait_ge(dec_std, 1)
            link(dve.reciprocal(dec_small[0:NS, 11:12], dec_small[0:NS, 10:11]))
            dve.scalar_tensor_tensor(dec_r[:], dec_r[:], dec_small[0:NS, 11:12], dec_fg[:], ALU.mult, ALU.mult).then_inc(
                dec_out, 1)


Z_PARTS = (("pu", 256), ("pg", 256), ("dq", 384), ("dk", 384), ("dv", 384), ("dg", 384), ("ch", 256), ("cb", 256),
           ("cc", 256), ("cg", 256), ("sq", 256), ("sk", 128), ("sv", 128), ("sg", 256))
TILE_ORDER = ("pu", "ch", "cc", "cb", "pg", "cg", "dg", "sg", "dv", "sv", "dq", "sq", "dk", "sk")


def kernel(**inputs):
    import numpy as _np
    import concourse.bacc as _bacc
    from concourse import mybir as _mybir
    from concourse.bass_utils import run_bass_kernel_spmd as _run

    x = {k: _np.asarray(v) for k, v in inputs.items()}
    starts, at = {}, 0
    for n, w in Z_PARTS:
        starts[n] = at
        at += w
    widths = dict(Z_PARTS)
    w_in = _np.concatenate([x["w_in"][0][:, starts[n]:starts[n] + widths[n]] for n in TILE_ORDER], axis=1)
    w_tiles = w_in.reshape(KD, P, NT, P).transpose(2, 1, 0, 3)
    c = _np.concatenate([x["c_sample"], x["c_prompt"]], axis=0)
    pool_w = _np.zeros((P, 2, P), _np.float32)
    for g in range(4):
        r = slice(64 * (g % 2), 64 * (g % 2) + 64)
        pool_w[r, g // 2, r] = x["w_pool"][0, g]
    w_out = x["w_out"][0]
    w_out = _np.concatenate([w_out[0:256], w_out[640:896], w_out[256:640], w_out[896:1152]], axis=0)
    arrays = {
        "x_prompt": x["x_prompt"][0],
        "x_sample": x["x_sample"][:, 0],
        "c_t": c.reshape(NS + 1, KD, P).transpose(2, 1, 0),
        "w_ada": x["w_ada"][0],
        "b_ada": _np.broadcast_to(x["b_ada"], (NS + 1, 3 * D)),
        "norm_g": x["norm_g"][0].reshape(KD, P).T,
        "w_tiles": w_tiles,
        "const": constants(),
        "pool_w": pool_w,
        "pool_scale": x["pool_scale"][0].reshape(2, P).T,
        "conv_w": x["conv_w"][0].reshape(3, 2, P).transpose(2, 1, 0),
        "sink": _np.broadcast_to(x["swa_sink"], (P, NHS)),
        "sink_rows": _np.tile(x["swa_sink"][0], NS)[:, None],
        "w_out": w_out.reshape(Y, P, D).transpose(1, 0, 2),
        "final_g": _np.broadcast_to(x["final_g"], (P, D)),
        "dil_kc": x["cache_dil_k"][0].reshape(NS, 2048, NHD * 64),
        "dil_vc": x["cache_dil_v"][0].reshape(NS, 2048, NHD * 64),
        "swa_kc": x["cache_swa_k"][0].reshape(NS, P, P),
        "swa_vc": x["cache_swa_v"][0].reshape(NS, P, P),
        "pool_state": x["state_pool"][0].transpose(2, 0, 1).reshape(2, P, NS, 15).transpose(1, 0, 2, 3),
        "conv_state": x["state_conv"][0].transpose(2, 0, 1).reshape(2, P, NS, 2).transpose(1, 0, 2, 3),
        "pool_rows": x["state_pool"][0],
        "conv_rows": x["state_conv"][0],
    }
    outs = [("y_prompt", (T, D)), ("y_sample", (NS, D)), ("pool_p", (15, 256)), ("pool_s", (NS, 15, 256)),
            ("dil_k_p", (T, 384)), ("dil_v_p", (T, 384)), ("dil_k_s", (NS, 384)), ("dil_v_s", (NS, 384)),
            ("conv_p", (2, 256)), ("conv_s", (NS, 2, 256)), ("swa_k_p", (P, P)), ("swa_v_p", (P, P)),
            ("swa_k_s", (NS, P)), ("swa_v_s", (NS, P))]
    nc = _bacc.Bacc("TRN2", target_bir_lowering=False, num_devices=1)
    args = []
    for name, a in arrays.items():
        arrays[name] = a = _np.ascontiguousarray(a)
        args.append(nc.dram_tensor(name, a.shape, _mybir.dt.from_np(a.dtype), kind="ExternalInput").ap())
    for name, shape in outs:
        args.append(nc.dram_tensor(name, shape, _mybir.dt.float32, kind="ExternalOutput").ap())
    build_program(nc, *args)
    r = _run(nc, [arrays], core_ids=[0]).results[0]
    o = {name: r[name] for name, _ in outs}
    return (o["y_prompt"][None], o["y_sample"][:, None], o["pool_p"][None, None], o["pool_s"][None],
            o["dil_k_p"].reshape(1, 1, T, NHD, 64), o["dil_v_p"].reshape(1, 1, T, NHD, 64),
            o["dil_k_s"].reshape(1, NS, 1, NHD, 64), o["dil_v_s"].reshape(1, NS, 1, NHD, 64),
            o["conv_p"][None, None], o["conv_s"][None],
            o["swa_k_p"].reshape(1, 1, P, 2, 64), o["swa_v_p"].reshape(1, 1, P, 2, 64),
            o["swa_k_s"].reshape(1, NS, 1, 2, 64), o["swa_v_s"].reshape(1, NS, 1, 2, 64))
```

```python
import math
from contextlib import ExitStack

import numpy as np

import concourse.bass as bass
from concourse import mybir
from concourse.alu_op_type import AluOpType as ALU

F32 = mybir.dt.float32
F32R = mybir.dt.float32r
ACT = mybir.ActivationFunctionType
AX = mybir.AxisListType

P = 128
D = 1024
KD = D // P
T = 2048
NS = 8
TT = T + NS
GROUP = 416
GROUPS = [(g * GROUP, min(TT, (g + 1) * GROUP)) for g in range(5)]
NT = 30
PLAIN0, GATE0, V0, K0, Q0 = 0, 8, 17, 21, 25
Y = 9
EPS = 1e-6
BIG = 1.0e30
NHD, NHS = 6, 4
SLOPE_D = [2.0 ** (-8.0 * (h + 1) / NHD) for h in range(NHD)]
SLOPE_S = [2.0 ** (-8.0 * (h + 1) / NHS) for h in range(NHS)]
DILATIONS = (1, 4, 16)
CH = 256
HALO = 16

C_ID, C_OFF, C_SELP, C_SLD, C_SLS, C_INVW, C_RCF, C_DB, C_SB, C_NEW, C_EPS, C_M6, C_S6, C_M4, C_S4, C_END = np.cumsum(
    [0, 128, 256, 128, 6, 4, 2, 32, 18, 4, 8, 1, 6, 8, 4, 8]).tolist()


def constants():
    c = np.zeros((P, C_END), np.float32)
    p = np.arange(P)
    c[:, C_ID:C_ID + P] = np.eye(P)
    off = p[:, None] - np.arange(256)[None, :] + 128.0
    c[:, C_OFF:C_OFF + 256] = np.where((off >= 0) & (off <= 128), off, BIG)
    c[NS, C_SELP:C_SELP + P] = 1.0
    c[:, C_SLD:C_SLD + 6] = np.array(SLOPE_D)
    c[:, C_SLS:C_SLS + 4] = np.array(SLOPE_S)
    for t in range(2):
        for half in range(2):
            w = (2, 4, 8, 16)[2 * t + half]
            rows = slice(64 * half, 64 * half + 64)
            c[rows, C_INVW + t] = 1.0 / w
            c[rows, C_RCF + 16 * t:C_RCF + 16 * t + 16] = 1.0 / np.minimum(np.arange(16) + 1, w)
    for i, d in enumerate(DILATIONS):
        for h in range(NHD):
            c[:, C_DB + 6 * i + h] = -np.float32(SLOPE_D[h]) * d * (128 - p)
    for h in range(NHS):
        c[:, C_SB + h] = -np.float32(SLOPE_S[h]) * (128 - p)
    c[:, C_NEW:C_NEW + NS] = np.where(p[:, None] % NS == np.arange(NS)[None], 0.0, -BIG)
    c[:, C_EPS] = EPS
    for n, m, r, p0 in ((NHD, C_M6, C_S6, 0), (NHS, C_M4, C_S4, 64)):
        rows = slice(p0, p0 + NS * n)
        c[rows, m:m + n] = ((p[rows, None] - p0) % n == np.arange(n)[None])
        c[rows, r:r + NS] = ((p[rows, None] - p0) // n == np.arange(NS)[None])
    return c


def build_program(nc, x_prompt, x_sample, c_t, w_ada, b_ada, norm_g, w_tiles, const, pool_w, pool_scale,
                  conv_w, sink, sink_rows, w_out, final_g, dil_kc, dil_vc, swa_kc, swa_vc, pool_state,
                  conv_state, pool_rows, conv_rows,
                  y_prompt, y_sample, pool_p, pool_s, dil_k_p, dil_v_p, dil_k_s, dil_v_s,
                  conv_p, conv_s, swa_k_p, swa_v_p, swa_k_s, swa_v_s):
    with ExitStack() as ctx:
        base = (nc.sbuf_base + 63) // 64 * 64
        arena_bytes = nc.sbuf_usable_end - base - 64
        ctx.enter_context(nc.sbuf_tensor("arena", [P, arena_bytes // 4], F32, align_bytes=64))

        class Plan:
            def __init__(self, at):
                self.at = at

            def put(self, name, shape, dtype=F32):
                size = int(np.prod(shape[1:])) * 4
                t = nc.alloc_sbuf_tensor_at(name, shape, dtype, offset=self.at)
                self.at = (self.at + size + 31) // 32 * 32
                assert self.at <= base + arena_bytes, name
                return t

        def sem(name):
            return ctx.enter_context(nc.semaphore(name))

        def scratch(name, shape, dtype=F32):
            return nc.dram_tensor(name, shape, dtype, kind="Internal").ap()

        plain_dram = scratch("plain_dram", [8, P, T])
        gate_dram = scratch("gate_dram", [Y, P, T])
        qk_dram = scratch("qk_dram", [9, 2, 2, 64, T])
        yac_dram = scratch("yac_dram", [4, P, T])
        swa_v_dram = scratch("swa_v_dram", [T, P])
        mix_dram = scratch("mix_dram", [3, T, 3, 132])
        swa_mix_dram = scratch("swa_mix_dram", [T, 2, 132])
        spare_dram = scratch("spare_dram", [4, P, NS])
        zs_dram = scratch("zs_dram", [NS, 19 * P])

        keep = Plan(base)
        consts = keep.put("consts", [P, C_END])
        mod_gate = keep.put("mod_gate", [NS + 1, D])
        zs_t = keep.put("zs_t", [P, NT, NS])
        mod_scale = keep.put("mod_scale", [P, KD, NS + 1])
        mod_shift = keep.put("mod_shift", [P, KD, NS + 1])
        c_sb = keep.put("c_sb", [P, KD, NS + 1])
        c_silu = keep.put("c_silu", [P, KD, NS + 1])
        g_t = keep.put("g_t", [P, KD])
        small = keep.put("small", [P, 64])
        pool_scale_t = keep.put("pool_scale_t", [P, 2])
        conv_w_t = keep.put("conv_w_t", [P, 2, 3])
        pool_w_sb = keep.put("pool_w_sb", [P, 2, P])
        tail_u = keep.put("tail_u", [P, 2, 15])
        tail_z = keep.put("tail_z", [P, 2, 2])
        zc_s = keep.put("zc_s", [NS, 256])
        neg_sink = keep.put("neg_sink", [P, NHS])
        b_gate_at = keep.at
        b_gate = keep.put("b_gate", [NS + 1, D])
        ident = consts[:, C_ID:C_ID + P]
        eps = consts[:, C_EPS:C_EPS + 1]

        h_at = keep.at
        h_bytes = KD * TT * 4
        w_at = h_at + 2 * h_bytes
        slot_at = w_at + 6 * D * 4
        SLOT = TT * 4
        assert slot_at + 5 * SLOT <= base + arena_bytes

        h_hi = Plan(h_at).put("h_hi", [P, KD, TT], F32R)
        h_lo = Plan(h_at + h_bytes).put("h_lo", [P, KD, TT], F32R)
        h_f32 = Plan(h_at + h_bytes).put("h_f32", [P, KD, TT])
        wp = Plan(w_at)
        w_raw = [wp.put(f"w_raw{b}", [P, KD, P]) for b in range(2)]
        w_hi = [wp.put(f"w_hi{b}", [P, KD, P], F32R) for b in range(2)]
        w_lo = [wp.put(f"w_lo{b}", [P, KD, P], F32R) for b in range(2)]
        main = [Plan(slot_at + (1 - b) * SLOT).put(f"main{b}", [P, TT]) for b in range(2)]
        main_hi = [Plan(slot_at + (1 - b) * SLOT).put(f"main_hi{b}", [P, TT], F32R) for b in range(2)]
        main_lo = [Plan(slot_at + (3 - b) * SLOT).put(f"main_lo{b}", [P, TT], F32R) for b in range(2)]
        k_nat = Plan(slot_at + 4 * SLOT).put("k_nat", [P, TT])
        ada_w = Plan(h_at).put("ada_w", [P, 4, KD, 512])
        xp_ = Plan(slot_at)
        x_in = [xp_.put(f"x_in{i}", [P, D]) for i in range(4)]
        junk = Plan(slot_at + 2 * SLOT).put("junk", [P, D])
        b_mod = Plan(slot_at + 3 * SLOT).put("b_mod", [NS + 1, 2 * D])
        mod_sb = Plan(slot_at + 4 * SLOT).put("mod_sb", [NS + 1, 2 * D])
        gate_w = [Plan(slot_at + (2 + b) * SLOT).put(f"gate_w{b}", [P, KD, 256]) for b in range(2)]
        cp = Plan(slot_at + 2 * SLOT)
        u_in = cp.put("u_in", [P, 2, HALO + CH])
        sum_a = cp.put("sum_a", [P, 2, HALO + CH])
        sum_b = cp.put("sum_b", [P, 2, HALO + CH])
        diff = cp.put("diff", [P, 2, CH])
        ch_in = cp.put("ch_in", [P, 2, 2 + CH])
        cc_in = cp.put("cc_in", [P, 2, 2 + CH])
        cb_in = cp.put("cb_in", [P, 2, CH])
        gate_in = cp.put("gate_in", [P, 4, CH])
        yac = cp.put("yac", [P, 4, CH])
        assert cp.at <= slot_at + 5 * SLOT
        kv_nat = [Plan(b_gate_at + 2048 * b).put(f"kv_nat{b}", [P, 4, P]) for b in range(2)]
        ap_ = Plan(h_at)
        q_st, kh_st, kl_st = ([[ap_.put(f"{n}0{h}", [P, T], F32R) for h in range(2)]] for n in ("q_st", "kh_st", "kl_st"))
        v_at = ap_.at
        v_dil = [ap_.put(f"v_dil{c}", [P, 16, P]) for c in range(3)]
        logits_at = ap_.at
        xs_ = [ap_.put(f"logits{b}", [P, 2, 256]) for b in range(2)]
        probs = [ap_.put(f"probs{b}", [P, 2, 256]) for b in range(4)]
        probs_t = [ap_.put(f"probs_t{b}", [P, 4, P]) for b in range(2)]
        o_t = ap_.put("o_t", [P, 4, P])
        logits_end = ap_.at
        ap_.put("dec_ps_place", [P, 136])
        swa_at = ap_.at
        q_st.append([ap_.put(f"q_st1{h}", [P, T], F32R) for h in range(2)])
        kh_st.append([ap_.put("kh_st1", [P, T], F32R)] * 2)
        kl_st.append([ap_.put("kl_st1", [P, T], F32R)] * 2)
        v_swa = ap_.put("v_swa", [P, 16, 64])
        assert ap_.at <= w_at
        ZN_TILES = list(range(0, 6)) + list(range(V0, NT))
        ZN = {"pu": (0, 256), "ch": (256, 512), "cc": (512, 768), "dv": (768, 1152), "sv": (1152, 1280),
              "dk": (1280, 1664), "sk": (1664, 1792), "dq": (1792, 2176), "sq": (2176, 2432)}
        zp = Plan(w_at)
        zn = zp.put("zn", [NS, len(ZN_TILES) * P])
        tail_rows = zp.put("tail_rows", [15, 512])
        assert zp.at <= w_at + 3 * 4096
        op = Plan(swa_at)
        wo_hi = op.put("wo_hi", [P, Y, D], F32R)
        assert op.at <= w_at
        bp = Plan(w_at)
        wo_lo = bp.put("wo_lo", [P, Y, D], F32R)
        raw_at = bp.at
        wo_raw = [bp.put(f"wo_raw{b}", [P, D]) for b in range(2)]
        attention_at = bp.at
        bias_swa = bp.put("bias_swa", [P, 2, 256])
        dec_at = bp.at
        assert slot_at + 2 * SLOT <= attention_at
        bp = Plan(slot_at + 3 * SLOT)
        table_at = bp.at
        bias_dil = bp.put("bias_dil", [P, 3, 2, 256])
        o_st = [bp.put(f"o_st{b}", [P, 4, 132]) for b in range(4)]
        table_end = bp.at
        sink_now = bp.put("sink_now", [P, 2])
        op = Plan(h_at)
        x_res = [op.put(f"x_res{b}", [P, D]) for b in range(2)]
        gates = [op.put(f"gates{b}", [P, 5, P]) for b in range(2)]
        y_t = [op.put(f"y_t{b}", [P, Y, P]) for b in range(2)]
        final_g_sb = op.put("final_g_sb", [P, D])
        assert op.at <= h_at + 6 * T * 4
        resid = [op.put(f"resid{b}", [P, D]) for b in range(2)]
        gate_all = op.put("gate_all", [P, D])
        y_hi = [op.put(f"y_hi{b}", [P, Y, P], F32R) for b in range(2)]
        y_lo = [op.put(f"y_lo{b}", [P, Y, P], F32R) for b in range(2)]
        mp = Plan(v_at + 16 * P * 4)
        mix_in = [mp.put(f"mix_in{b}", [P, 3, 3, 132]) for b in range(2)]
        swa_in = [mp.put(f"swa_in{b}", [P, 2, 132]) for b in range(2)]
        o_mix = mp.put("o_mix", [P, 640])
        o_part = mp.put("o_part", [P, 384])
        fac = mp.put("fac", [P, 64])
        assert op.at <= v_at + 16 * P * 4 and mp.at <= logits_at
        op = Plan(logits_at)
        y_out = [op.put(f"y_out{b}", [P, D]) for b in range(2)]
        junk_o = op.put("junk_o", [P, D])
        fin = op.put("fin", [P, 8])
        ys_hi = op.put("ys_hi", [P, Y, NS], F32R)
        ys_lo = op.put("ys_lo", [P, Y, NS], F32R)
        assert op.at <= swa_at

        psum = ctx.enter_context(nc.psum_tensor("psum", [P, 8, 512], F32))

        const_loaded = sem("const_loaded")
        small_loaded = sem("small_loaded")
        x_loaded = [sem(f"x_loaded{i}") for i in range(4)]
        xs_loaded = sem("xs_loaded")
        ada_loaded = sem("ada_loaded")
        gate_loaded = [sem(f"gate_loaded{i}") for i in range(2)]
        c_ready = sem("c_ready")
        sumsq = sem("sumsq")
        rstd_ready = sem("rstd_ready")
        h_pool_ready = sem("h_pool_ready")
        xn_ready = sem("xn_ready")
        xt_ready = sem("xt_ready")
        xt_copied = [sem(f"xt_copied{i}") for i in range(2)]
        dve_link = sem("dve_link")
        mod_mm = sem("mod_mm")
        mod_added = sem("mod_added")
        mod_t = sem("mod_t")
        mod_done = sem("mod_done")
        h_aff = sem("h_aff")
        h_hi_ready = sem("h_hi_ready")
        h_ready = sem("h_ready")
        w_loaded = [sem(f"w_loaded{b}") for b in range(2)]
        w_hi_ready = sem("w_hi_ready")
        w_ready = sem("w_ready")
        group_done = sem("group_done")
        bank_free = [sem(f"bank_free{g}") for g in range(5)]
        act_evac = sem("act_evac")
        main_stored = [sem(f"main_stored{b}") for b in range(2)]
        lo_stored = [sem(f"lo_stored{b}") for b in range(2)]
        gate_mm = sem("gate_mm")
        gate_added = sem("gate_added")
        chunk_loaded = sem("chunk_loaded")
        diff_ready = sem("diff_ready")
        pool_mm = sem("pool_mm")
        yac_ready = sem("yac_ready")
        yac_stored = sem("yac_stored")
        tail_t = sem("tail_t")
        tail_copied = sem("tail_copied")
        kv_t = sem("kv_t")
        nat_copied = sem("nat_copied")
        nat_stored = [sem(f"nat_stored{b}") for b in range(2)]
        out_stored = sem("out_stored")
        piece_loaded = [sem(f"piece_loaded{j}") for j in range(4)]
        vd_loaded = [sem(f"vd_loaded{c}") for c in range(3)]
        swa_loaded = sem("swa_loaded")
        s_done = sem("s_done")
        x_ready = sem("x_ready")
        bias_ready = sem("bias_ready")
        p_ready = sem("p_ready")
        pt_done = sem("pt_done")
        pt_copied = sem("pt_copied")
        pv_done = sem("pv_done")
        ot_copied = sem("ot_copied")
        o_turned = sem("o_turned")
        o_copied = sem("o_copied")
        mix_stored = [sem(f"mix_stored{b}") for b in range(4)]
        wo_loaded = [sem(f"wo_loaded{b}") for b in range(2)]
        wo_hi_ready = sem("wo_hi_ready")
        wo_split = sem("wo_split")
        fg_loaded = sem("fg_loaded")
        tile_in = [sem(f"tile_in{b}") for b in range(2)]
        gates_in = [sem(f"gates_in{b}") for b in range(2)]
        x_again = [sem(f"x_again{b}") for b in range(2)]
        gate_bc = sem("gate_bc")
        arg_ready = sem("arg_ready")
        exp_ready = sem("exp_ready")
        mixed = sem("mixed")
        mix_t = sem("mix_t")
        yt_ready = sem("yt_ready")
        yh_ready = sem("yh_ready")
        y_split = sem("y_split")
        out_mm = sem("out_mm")
        res_gated = sem("res_gated")
        res_ready = sem("res_ready")
        sq_ready = sem("sq_ready")
        y_ready = sem("y_ready")
        y_stored = [sem(f"y_stored{b}") for b in range(2)]
        out_link = sem("out_link")
        sink_negated = sem("sink_negated")
        unit_open = sem("unit_open")
        store_open = sem("store_open")
        zs_t_done = sem("zs_t_done")
        zs_copied = sem("zs_copied")
        zc_ready = sem("zc_ready")
        zs_stored = sem("zs_stored")
        dec_loaded = sem("dec_loaded")
        dec_k_loaded = [sem(f"dec_k_loaded{b}") for b in range(2)]
        dec_link = sem("dec_link")
        dec_s_ready = sem("dec_s_ready")
        dec_st = sem("dec_st")
        dec_neg = sem("dec_neg")
        dec_exp = sem("dec_exp")
        dec_pn = sem("dec_pn")
        dec_pt_done = sem("dec_pt_done")
        dec_pt_ready = sem("dec_pt_ready")
        dec_v_loaded = [sem(f"dec_v_loaded{c}") for c in range(3)]
        dec_sv_loaded = [sem(f"dec_sv_loaded{b}") for b in range(2)]
        dec_pv = sem("dec_pv")
        dec_tail_loaded = sem("dec_tail_loaded")
        dec_o_done = sem("dec_o_done")
        dec_masked = sem("dec_masked")
        dec_diff = sem("dec_diff")
        dec_sel = sem("dec_sel")
        dec_gate = sem("dec_gate")
        dec_y_full = sem("dec_y_full")
        dec_y_ready = sem("dec_y_ready")
        dec_mm = sem("dec_mm")
        dec_res = sem("dec_res")
        dec_sq_ready = sem("dec_sq_ready")
        dec_out = sem("dec_out")
        rec_ready = sem("rec_ready")
        dec_std = sem("dec_std")
        fstd_ready = sem("fstd_ready")
        std_ready = sem("std_ready")
        gate_bc_read = sem("gate_bc_read")

        POOL_FROM = 1448

        def walk(eng, body):
            for t in (0, 1):
                body(t, t // 2, t, "plain")
            with eng.Fori(0, 3) as i:
                for b in range(2):
                    body(2 + 2 * i + b, 1 + i, 2 + b, "plain")
            with eng.Fori(0, 2) as i:
                for b in range(2):
                    body(8 + 2 * i + b, 4 + i, 8 + b, "gate")
            for t in range(12, K0):
                body(t, t // 2, t, "gate" if t < V0 else "plain")
            for t in range(K0, NT):
                body(t, t // 2, t, "k" if t < Q0 else "q")

        TURNS = [(t, g) for t in range(V0, Q0) for g in (range(4) if t < Q0 - 1 else (3,))]
        SWA_V = K0 - 1

        def turns(t):
            return [(n, g) for n, (u, g) in enumerate(TURNS) if u == t]

        def nat_stores(n):
            return 16 * sum(2 if TURNS[m] == (SWA_V, 3) else 1 for m in range(n % 2, n, 2))

        def main_free(eng, ts):
            if V0 <= ts - 2 < K0:
                eng.wait_ge(kv_t, turns(ts - 2)[-1][0] + 1)
            else:
                eng.wait_ge(main_stored[ts % 2], 16 * main_stores(ts))

        def main_stores(ts):
            return sum(0 if V0 <= t < K0 else 1 if t < K0 else 2 for t in range(ts % 2, ts, 2))

        CHUNK0 = 12
        NCH = T // CH

        UNITS = 2 * 64 + 48

        def attention_qk(eng, kind, p, c0, c1, done):
            qt = 4 + p if kind == 0 else 7 + p
            for h in range(2):
                eng.dma_start(q_st[kind][h][:, c0:c1].bitcast(F32),
                              qk_dram[qt, h, :, :, c0:c1].rearrange("a r t -> (a r) t")).then_inc(done, 16)
                if kind and h:
                    continue
                k = qk_dram[3, p] if kind else qk_dram[p, h]
                for part, st in ((0, kh_st), (1, kl_st)):
                    for half in (slice(0, 64), slice(64, 128)):
                        eng.dma_start(st[kind][h][half, c0:c1].bitcast(F32), k[part, :, c0:c1]).then_inc(done, 16)

        def load_dil(eng, p):
            v = dil_v_p[:, P * p:P * p + P]
            for j in range(4):
                attention_qk(eng, 0, p, 512 * j, 512 * j + 512, piece_loaded[j])
                eng.dma_start(v_dil[0][:, 4 * j:4 * j + 4, :],
                              v[512 * j:512 * j + 512].rearrange("(b q) c -> q b c", q=P)).then_inc(piece_loaded[j], 16)
            for r in range(4):
                eng.dma_start(v_dil[1][:, 4 * r:4 * r + 4, :],
                              v.rearrange("(b q r) c -> r q b c", q=P, r=4)[r]).then_inc(vd_loaded[1], 16)
            eng.dma_start(v_dil[2][:], v.rearrange("(q r) c -> q r c", r=16)).then_inc(vd_loaded[2], 16)

        def load_swa(eng, p):
            attention_qk(eng, 1, p, 0, T, swa_loaded)
            eng.dma_start(v_swa[:], swa_v_dram[:, 64 * p:64 * p + 64].rearrange("(b q) c -> q b c", q=P)).then_inc(
                swa_loaded, 16)

        PIECE_DMAS, SWA_DMAS = 11, 7

        ZS_STORES = 11
        DEC_LOADS = 2 + 6 + 1 + 1 + 2 + 1
        DEC_TAIL_LOADS = 3 + 1 + 4
        ROW_LINKS = 3
        ROW_GROUPS, ROW_STEPS = (4, 5, 7, 8), (36, 38, 46, 50)

        class Unit:
            def __init__(self, kind, c, i):
                self.kind, self.c, self.i = kind, c, i
                d = 1 if kind else DILATIONS[c]
                self.r, self.b = (0, i) if d == 1 else (i // 4, i % 4) if d == 4 else (i, 0)
                self.d = d
                self.full = self.b > 0
                self.own = P if self.full or (d == 16 and self.r % 2) else 0

            def view(self, t):
                return t[:].rearrange("p (t r) -> p r t", r=self.d)

            def q(self, h):
                return self.view(q_st[self.kind][h])[:, self.r, P * self.b:P * self.b + P]

            def keys(self, stack, h):
                v = self.view(stack[self.kind][h])
                if self.d == 16:
                    r0 = self.r - self.r % 2
                    return v[:, r0:r0 + 2, :]
                c0 = P * (self.b - 1) if self.full else 0
                return v[:, self.r, c0:c0 + 256]

            def v(self, h, back):
                if self.kind:
                    return v_swa[:, self.i - back, :]
                return v_dil[self.c][:, self.i - back, 64 * h:64 * h + 64]

            def bias(self, h):
                t = bias_swa[:, h, :] if self.kind else bias_dil[:, self.c, h, :]
                return t if self.full else t[:, P:256]

            def cols(self):
                return slice(0, 256) if self.full else slice(self.own, self.own + P)

            def halves(self):
                return ((0, 1), (P, 0)) if self.full else ((self.own, 0),)

        units = [Unit(0, c, i) for c in range(3) for i in range(16)] + [Unit(1, 0, i) for i in range(16)]

        last_units = [u for c in (2, 1, 0) for u in units[16 * c:16 * c + 16]]

        def rounds(eng, body):
            with eng.Fori(0, 2) as i:
                body(i, units)
            body(2, last_units)

        TURN_LAG, COPY_LAG, PV_LAG, OUT_LAG = 3, 4, 5, 10
        S_BANK, PT_BANK, OT_BANK, ON_BANK, DEC_BANK = 0, 2, 4, 6, 7

        def cache_rows(cache, b, c):
            d = DILATIONS[c]
            rows = cache[b] if isinstance(b, int) else cache[bass.ds(b, 1)].rearrange("a t e -> (a t) e")
            return rows[2048 - P * d:2048, :].rearrange("(p r) e -> r p e", r=d)[0]

        def out_load(eng, j, b):
            rows = bass.ds(P * j, P)
            eng.dma_start(mix_in[b][:], mix_dram[:, rows, :, :].rearrange("c q j w -> q c j w")).then_inc(tile_in[b], 16)
            eng.dma_start(swa_in[b][:], swa_mix_dram[rows, :, :]).then_inc(tile_in[b], 16)

        def gates_load(eng, j, b):
            rows = bass.ds(P * j, P)
            eng.dma_start(gates[b][:], gate_dram[4:Y, :, rows].rearrange("m p t -> p m t")).then_inc(gates_in[b], 16)
            eng.dma_start(y_t[b][:, 0:4, :], yac_dram[:, :, rows].rearrange("m p t -> p m t")).then_inc(gates_in[b], 16)

        def res_load(eng, j, b):
            eng.dma_start(x_res[b][:], x_prompt[bass.ds(P * j, P), :]).then_inc(x_again[b], 16)

        def out_walk(eng, step):
            step(0, 0, 0, True)
            step(1, 0, 1, True)
            with eng.Fori(1, 8) as i:
                for b in range(2):
                    step(2 * i + b, i, b, False)

        dp = Plan(w_at)
        dec_q = dp.put("dec_q", [P, NS, 384])
        dec_sq = dp.put("dec_sq", [P, NS * 256])
        dec_sk = dp.put("dec_sk", [P, NS * 2, 64])
        dec_k = [dp.put(f"dec_k{b}", [P, 3, 384]) for b in range(2)]
        dec_prod = dp.put("dec_prod", [P, 3 * 384])
        dec_qn = dp.put("dec_qn", [24, 384])
        dec_kn = dp.put("dec_kn", [24, 384])
        dec_sqn = dp.put("dec_sqn", [NS, 256])
        dec_skn = dp.put("dec_skn", [NS, 2, 2, 64])
        assert dp.at <= attention_at, (dp.at, attention_at)
        dec_p = bp.put("dec_p", [48, 408])
        dp = Plan(dec_at)
        dec_s = dp.put("dec_s", [P, 3, 48])
        dec_s4 = dp.put("dec_s4", [24, 48])
        dec_ss = dp.put("dec_ss", [P, 32])
        dec_ss4 = dp.put("dec_ss4", [NS, 32])
        dec_red = dp.put("dec_red", [P, 3, 6])
        dec_own = dp.put("dec_own", [24, 6])
        dec_sown = dp.put("dec_sown", [NS, 4])
        dec_pt4 = dp.put("dec_pt4", [24, 48])
        dec_pst4 = dp.put("dec_pst4", [NS, 32])
        sink_col = dp.put("sink_col", [32, 1])
        dec_small = dp.put("dec_small", [P, 16])
        stats = [dp.put(f"stats{b}", [P, 4, 4]) for b in range(4)]
        assert dp.at <= table_at and bp.at <= base + arena_bytes
        dec_ps = Plan(logits_end).put("dec_ps", [32, 136])
        dp = Plan(raw_at)
        dec_pz = dp.put("dec_pz", [P, 3, NS * 54])
        dec_psz = dp.put("dec_psz", [P, NS * 36])
        assert dp.at <= attention_at
        dp = Plan(b_gate_at)
        dec_v = [dp.put(f"dec_v{c}", [P, 384]) for c in range(2)] + [Plan(ap_.at).put("dec_v2", [P, 384])]
        dec_sv = [dp.put(f"dec_sv{b}", [P, P]) for b in range(2)]
        assert dp.at <= b_gate_at + 4096 and ap_.at + 1536 <= w_at
        dp = Plan(table_at)
        dec_vn = dp.put("dec_vn", [24, 384])
        dec_svn = dp.put("dec_svn", [NS, P])
        dec_m6 = dp.put("dec_m6", [48, 6, 64])
        dec_m4 = dp.put("dec_m4", [96, 4, 64])[64:96]
        dec_state = dp.put("dec_state", [P, 2, NS, 15])
        dec_conv = dp.put("dec_conv", [P, 2, NS, 2])
        dec_g = dp.put("dec_g", [P, Y, NS])
        dec_y = dp.put("dec_y", [P, Y, NS])
        dec_a = dp.put("dec_a", [P, 2, NS])
        dec_b = dp.put("dec_b", [P, 2, NS])
        dec_x = dp.put("dec_x", [NS, D])
        dec_fg = dp.put("dec_fg", [NS, D])
        assert dp.at <= table_end, (dp.at, table_end)
        dec_r = Plan(raw_at).put("dec_r", [NS, D])
        dec_junk = Plan(raw_at + 4096).put("dec_junk", [NS, D])
        block = ctx.enter_context(nc.Block())
        wv = w_ada.rearrange("(k p) e -> p k e", p=P)

        def bank(b, n=512):
            return psum[:, b, 0:n]

        @block.sync
        def _(sp):
            for dst, src in ((consts[:], const), (c_sb[:], c_t)):
                sp.dma_start(dst, src).then_inc(const_loaded, 16)

            def x_round(j, first):
                for i in range(4):
                    if not first:
                        sp.wait_ge(xt_ready, 4 * j - 3 + i)
                    sp.dma_start(x_in[i][:], x_prompt[bass.ds(512 * j + P * i, P), :]).then_inc(x_loaded[i], 16)

            def ada_load(j):
                sp.dma_start(ada_w[:, bass.ds(j, 1), :, :].rearrange("p a k e -> p (a k) e"),
                             wv[:, :, bass.ds(512 * j, 512)]).then_inc(ada_loaded, 16)

            x_round(0, True)
            for dst, src in ((b_mod[:], b_ada[:, 0:2 * D]), (g_t[:], norm_g), (b_gate[:], b_ada[:, 2 * D:]),
                             (pool_scale_t[:], pool_scale), (conv_w_t[:], conv_w), (pool_w_sb[:], pool_w),
                             (neg_sink[:], sink)):
                sp.dma_start(dst, src).then_inc(small_loaded, 16)
            ada_load(0)
            with sp.Fori(1, 4) as j:
                x_round(j, False)
                sp.wait_ge(ada_loaded, 16 * j)
                ada_load(j)
            sp.wait_ge(xt_ready, 13)
            sp.dma_start(x_in[0][0:NS, :], x_sample).then_inc(xs_loaded, 16)

            sp.wait_ge(sumsq, 17)
            sp.wait_ge(mod_added, 4)
            sp.wait_ge(mod_mm, 4)
            for q in range(2):
                sp.dma_start(gate_w[q][:], wv[:, :, 2 * D + 256 * q:2 * D + 256 * q + 256]).then_inc(gate_loaded[q], 16)

            def nat_store(n, g, t):
                sp.wait_ge(nat_copied, n + 1)
                rows = slice(4 * P * g, 4 * P * g + 4 * P)
                b = n % 2
                m = t - V0 if t < K0 else t - K0
                if t in (SWA_V, Q0 - 1):
                    if t == SWA_V:
                        sp.dma_start(swa_v_dram[rows].rearrange("(x q) c -> q x c", q=P), kv_nat[b][:]).then_inc(
                            nat_stored[b], 16)
                    if g == 3:
                        sp.dma_start(swa_v_p if t == SWA_V else swa_k_p, kv_nat[b][:, 3, :]).then_inc(nat_stored[b], 16)
                else:
                    dst = (dil_v_p if t < K0 else dil_k_p)[rows, P * m:P * m + P]
                    sp.dma_start(dst.rearrange("(x q) c -> q x c", q=P), kv_nat[b][:]).then_inc(nat_stored[b], 16)

            def store(t, half, ts, kind):
                b = ts % 2
                one = lambda a, i: a[bass.ds(i, 1), :, :].rearrange("a p t -> p (a t)")
                for n, g in turns(ts - 1) if ts >= 12 else ():
                    nat_store(n, g, ts - 1)
                sp.wait_ge(bank_free[4], t + 1)
                if V0 <= ts < K0:
                    pass
                elif kind == "plain":
                    sp.dma_start(one(plain_dram, t), main[b][:, 0:T]).then_inc(main_stored[b], 16)
                elif kind == "gate":
                    sp.dma_start(one(gate_dram, t - GATE0), main[b][:, 0:T]).then_inc(main_stored[b], 16)
                else:
                    for h in range(2):
                        r = slice(64 * h, 64 * h + 64)
                        sp.dma_start(qk_dram[t - K0, h, 0], main_hi[b][r, 0:T].bitcast(F32)).then_inc(main_stored[b], 16)
                        sp.dma_start(qk_dram[t - K0, h, 1], main_lo[b][r, 0:T].bitcast(F32)).then_inc(lo_stored[b], 16)
                if 0 <= ts - CHUNK0 < NCH:
                    n = ts - CHUNK0
                    sp.wait_ge(yac_ready, n + 1)
                    sp.dma_start(yac_dram[:, :, CH * n:CH * n + CH].rearrange("m p t -> p m t"), yac[:]).then_inc(
                        yac_stored, 16)
                if ts == 1:
                    for q in range(2):
                        sp.wait_ge(gate_mm, q + 1)
                        sp.dma_start(gate_w[q][:], wv[:, :, 2 * D + 512 + 256 * q:2 * D + 768 + 256 * q]).then_inc(
                            gate_loaded[q], 16)

            walk(sp, store)

            for b in range(2):
                sp.wait_ge(main_stored[b], 16 * (main_stores(NT + b) - 2))
                sp.wait_ge(lo_stored[b], 32 * (3 + b))
            for b in range(2):
                sp.wait_ge(nat_stored[b], nat_stores(12 + b))
            sp.wait_ge(group_done, 5 * NT)
            load_dil(sp, 0)
            for b in range(2):
                sp.wait_ge(main_stored[b], 16 * main_stores(NT + b))
                sp.wait_ge(lo_stored[b], 32 * (4 + b))
            sp.wait_ge(nat_stored[0], nat_stores(len(TURNS) + len(TURNS) % 2))
            sp.wait_ge(nat_stored[1], nat_stores(len(TURNS) + 1 - len(TURNS) % 2))
            sp.wait_ge(zs_copied, 6)
            sp.wait_ge(zc_ready, 1)
            zcol = lambda n: zn[:, ZN[n][0]:ZN[n][1]]
            sp.dma_start(zs_dram, zn[:]).then_inc(zs_stored, 16)
            for dst, src in ((dil_k_s, zcol("dk")), (dil_v_s, zcol("dv")), (swa_k_s, zcol("sk")), (swa_v_s, zcol("sv")),
                             (pool_s[:, 14, :], zcol("pu")), (pool_s[:, 0:14, :], pool_rows[:, 1:15, :]),
                             (conv_s[:, 1, :], zc_s[:]), (conv_s[:, 0, :], conv_rows[:, 1, :]),
                             (pool_p, tail_rows[:, 0:256]), (conv_p, tail_rows[0:2, 256:512])):
                sp.dma_start(dst, src).then_inc(zs_stored, 16)

            zrow = lambda n: zs_dram[:, ZN[n][0]:ZN[n][1]]
            sp.wait_ge(zs_stored, 16 * ZS_STORES)
            sp.dma_start(dec_q[:], zrow("dq").partition_broadcast(P)).then_inc(dec_loaded, 16)
            sp.dma_start(dec_sq[:].rearrange("p (s e) -> p s e", s=NS), zrow("sq").partition_broadcast(P)).then_inc(
                dec_loaded, 16)
            for n in range(3):
                sp.dma_start(dec_qn[NS * n:NS * n + NS, :], zrow("dq")).then_inc(dec_loaded, 16)
                sp.dma_start(dec_kn[NS * n:NS * n + NS, :], zrow("dk")).then_inc(dec_loaded, 16)
            sp.dma_start(dec_sk[:].rearrange("p (s g) e -> p s (g e)", s=NS), swa_kc.rearrange("s p e -> p s e")).then_inc(
                dec_loaded, 16)
            sp.dma_start(dec_sqn[:], zrow("sq")).then_inc(dec_loaded, 16)
            for x in range(2):
                sp.dma_start(dec_skn[:, :, x, :], zrow("sk").rearrange("s (g e) -> s g e", g=2)).then_inc(dec_loaded, 16)
            sp.dma_start(sink_col[:], sink_rows).then_inc(dec_loaded, 16)
            load_swa(sp, 0)
            for load, p, used in ((load_dil, 1, 48), (load_swa, 1, 64), (load_dil, 2, 64 + 48)):
                sp.wait_ge(pv_done, used)
                load(sp, p)

            sp.wait_ge(dec_s_ready, 2)
            for k in range(Y):
                if k >= 2:
                    sp.wait_ge(wo_split, k - 1)
                sp.dma_start(wo_raw[k % 2][:], w_out[:, k, :]).then_inc(wo_loaded[k % 2], 16)
            for b in range(NS):
                for c in range(3):
                    if b:
                        sp.wait_ge(dec_pv, 4 * (b - 1) + c + 1)
                    sp.dma_start(dec_v[c][:], cache_rows(dil_vc, b, c)).then_inc(dec_v_loaded[c], 16)
                if b >= 2:
                    sp.wait_ge(dec_pv, 4 * (b - 1))
                sp.dma_start(dec_sv[b % 2][:], swa_vc[b]).then_inc(dec_sv_loaded[b % 2], 16)
            for b in range(4):
                sp.wait_ge(mix_stored[b], 16 * (4 + 4 + 2 + (b == 0) + 1))
            for b in range(2):
                out_load(sp, b, b)
            sp.wait_ge(s_done, UNITS)
            for b in range(2):
                gates_load(sp, b, b)
            for b in range(2):
                res_load(sp, b, b)
            sp.dma_start(final_g_sb[:], final_g).then_inc(fg_loaded, 16)
            for b in range(4):
                sp.wait_ge(mix_stored[b], 16 * (UNITS // 16 + 1))
            for n in range(3):
                sp.dma_start(dec_vn[NS * n:NS * n + NS, :], zrow("dv")).then_inc(dec_tail_loaded, 16)
            sp.dma_start(dec_svn[:], zrow("sv")).then_inc(dec_tail_loaded, 16)
            sp.dma_start(dec_state[:], pool_state).then_inc(dec_tail_loaded, 16)
            sp.dma_start(dec_conv[:], conv_state).then_inc(dec_tail_loaded, 16)
            sp.dma_start(dec_x[:], x_sample).then_inc(dec_tail_loaded, 16)
            sp.dma_start(dec_fg[:], final_g[0:NS, :]).then_inc(dec_tail_loaded, 16)

            def out_store(j, b):
                sp.wait_ge(y_ready, j + 1)
                sp.dma_start(y_prompt[bass.ds(P * j, P), :], y_out[b][:]).then_inc(y_stored[b], 16)

            def out_step(j, b, mix=True, res=True, store=True):
                sp.wait_ge(y_split, j - 1)
                gates_load(sp, j, b)
                if mix:
                    sp.wait_ge(mixed, j)
                    out_load(sp, j + 1, 1 - b)
                if res:
                    sp.wait_ge(res_ready, j - 2)
                    res_load(sp, j - 1, 1 - b)
                if store:
                    out_store(j - 4, b)

            sp.wait_ge(mixed, 1)
            out_load(sp, 2, 0)
            out_step(2, 0, res=False, store=False)
            out_step(3, 1, store=False)
            with sp.Fori(2, 7) as i:
                for b in range(2):
                    out_step(2 * i + b, b)
            out_step(14, 0)
            out_step(15, 1, mix=False)
            sp.wait_ge(res_ready, 14)
            res_load(sp, 15, 1)
            for j in range(12, 16):
                out_store(j, j % 2)
            for b in range(2):
                sp.wait_ge(y_stored[b], 16 * 8)
            sp.wait_ge(dec_out, 1)
            sp.dma_start(y_sample, dec_r[:]).then_inc(out_stored, 16)
            sp.wait_ge(out_stored, 16)

        @block.gpsimd
        def _(pool):
            for b in range(2):
                pool.dma_start(w_raw[b][:], w_tiles[b]).then_inc(w_loaded[b], 16)

            for k in range(KD):
                pool.wait_ge(h_aff, k + 2)
                nc.gpsimd.tensor_tensor(h_lo[:, k, POOL_FROM:TT], h_f32[:, k, POOL_FROM:TT],
                                        h_hi[:, k, POOL_FROM:TT].bitcast(F32), ALU.subtract).then_inc(h_pool_ready, 1)

            def load(t, half, ts, kind):
                b = ts % 2
                if ts < NT - 2:
                    pool.wait_ge(w_ready, t + 1)
                    pool.dma_start(w_raw[b][:], w_tiles[bass.ds(t + 2, 1), :, :, :].rearrange(
                        "a p k c -> p (a k) c")).then_inc(w_loaded[b], 16)
                n = ts - CHUNK0
                if 0 <= n < NCH:
                    chunk_load(n)

            def chunk_load(n):
                c0 = CH * n
                if n == 0:
                    for b in range(2):
                        pool.wait_ge(main_stored[b], 16 * 6)
                else:
                    pool.wait_ge(yac_ready, n)
                h = HALO if n else 0
                h2 = 2 if n else 0
                def rows(a, c, left, dst):
                    pool.dma_start(dst, a[:, :, c - left:c + CH].rearrange("m p t -> p m t")).then_inc(chunk_loaded, 16)
                rows(plain_dram[0:2], c0, h, u_in[:, :, HALO - h:])
                rows(plain_dram[2:4], c0, h2, ch_in[:, :, 2 - h2:])
                rows(plain_dram[4:6], c0, h2, cc_in[:, :, 2 - h2:])
                rows(plain_dram[6:8], c0, 0, cb_in[:])
                rows(gate_dram[0:4], c0, 0, gate_in[:])

            walk(pool, load)

            def mixes(i, us):
                for g in range(len(us) // 4):
                    u = us[4 * g]
                    pool.wait_ge(o_copied, 16 * i + g + 1)
                    if u.kind:
                        dst = swa_mix_dram[:, bass.ds(i, 1), :].rearrange("t a w -> t (a w)")
                    else:
                        dst = mix_dram[u.c, :, bass.ds(i, 1), :].rearrange("t a w -> t (a w)")
                    if u.d == 1:
                        dst = dst[P * u.b:P * u.b + 512].rearrange("(b q) w -> q b w", q=P)
                    elif u.d == 4:
                        dst = dst.rearrange("(b q r) w -> r q b w", q=P, r=4)[u.r]
                    else:
                        dst = dst.rearrange("(q r) w -> q r w", r=16)[:, u.r:u.r + 4, :]
                    pool.sem_inc(store_open, 1)
                    pool.dma_start(dst, o_st[g % 4][:]).then_inc(mix_stored[g % 4], 16)
                    if len(us) == len(units) and g in ROW_GROUPS:
                        x = ROW_GROUPS.index(g)
                        if x == 0:
                            pool.wait_ge(dec_loaded, 16 * DEC_LOADS)
                        if x >= 2:
                            pool.wait_ge(dec_link, ROW_LINKS * (NS // 2 * i + x - 2) + 1)
                            pool.sem_inc(store_open, 1)
                        for c in range(3):
                            pool.dma_start(dec_k[x % 2][:, c, :], cache_rows(dil_kc, NS // 2 * i + x, c)).then_inc(
                                dec_k_loaded[x % 2], 16)

            for b in range(4):
                pool.dma_start(spare_dram[b], zs_t[:, 0, :]).then_inc(mix_stored[b], 16)
            rounds(pool, mixes)

            def residual(j, half, b, first):
                pool.wait_ge(x_again[b], 16 * (half + 1))
                pool.wait_ge(res_gated, j + 1)
                nc.gpsimd.tensor_tensor(resid[b][:], resid[b][:], x_res[b][:], ALU.add).then_inc(res_ready, 1)

            out_walk(pool, residual)

        @block.tensor
        def _(pe):
            def x_tile(j, i, first):
                pe.wait_ge(xn_ready, 4 * j + i + 1)
                if not (first and i < 2):
                    pe.wait_ge(xt_copied[i % 2], 2 * j + i // 2)
                for k in range(KD):
                    m = pe.transpose(psum[:, 2 * (i % 2) + k // 4, (k % 4) * P:(k % 4 + 1) * P],
                                     x_in[i][:, k * P:(k + 1) * P], ident)
                m.then_inc(xt_ready, 1)

            def mod_chunk(j, first):
                if first:
                    pe.wait_ge(c_ready, 1)
                else:
                    pe.wait_ge(mod_added, j)
                pe.wait_ge(ada_loaded, 16 * (j + 1))
                for k in range(KD):
                    m = pe.matmul(psum[0:NS + 1, 4, :], c_silu[:, k, :],
                                  ada_w[:, bass.ds(j, 1), k, :].rearrange("p a e -> p (a e)"),
                                  start=(k == 0), stop=(k == KD - 1))
                m.then_inc(mod_mm, 1)

            pe.wait_ge(const_loaded, 16 * 2)
            for i in range(4):
                x_tile(0, i, True)
            mod_chunk(0, True)
            with pe.Fori(1, 4) as j:
                for i in range(4):
                    x_tile(j, i, False)
                mod_chunk(j, False)
            pe.wait_ge(small_loaded, 16 * 7)
            pe.wait_ge(xn_ready, 17)
            pe.wait_ge(xt_copied[0], 8)
            for k in range(KD):
                m = pe.transpose(psum[:, 0, NS * k:NS * k + NS], x_in[0][0:NS, k * P:(k + 1) * P], ident[0:NS, 0:NS])
            m.then_inc(xt_ready, 1)
            pe.wait_ge(mod_added, 4)
            for e in range(2 * KD):
                m = pe.transpose(psum[:, 5, (NS + 1) * e:(NS + 1) * (e + 1)], mod_sb[:, e * P:(e + 1) * P],
                                 ident[0:NS + 1, 0:NS + 1])
            m.then_inc(mod_t, 1)

            def three(out, hi, lo, mhi, mlo, start, stop):
                pe.matmul(out, hi, mhi, start=start, stop=False)
                pe.matmul(out, hi, mlo, start=False, stop=False)
                return pe.matmul(out, lo, mhi, start=False, stop=stop)

            def gate_columns(q):
                b = q % 2
                pe.wait_ge(gate_loaded[b], 16 * (q // 2 + 1))
                if q:
                    pe.wait_ge(gate_added, q)
                for k in range(KD):
                    m = pe.matmul(psum[0:NS + 1, 5, 0:256], c_silu[:, k, :], gate_w[b][:, k, :],
                                  start=(k == 0), stop=(k == KD - 1))
                m.then_inc(gate_mm, 1)

            def pool_matmul(n):
                pe.wait_ge(diff_ready, n + 1)
                for m in range(2):
                    mm = pe.matmul(psum[:, 5, CH * m:CH * m + CH], pool_w_sb[:, m, :], diff[:, m, :],
                                   start=True, stop=True)
                mm.then_inc(pool_mm, 1)

            def turn(t):
                pe.wait_ge(bank_free[4], t + 1)
                for n, g in turns(t):
                    if n >= 2:
                        pe.wait_ge(nat_copied, n - 1)
                    src = main[t % 2] if t < K0 else k_nat
                    for x in range(4):
                        c = P * (4 * g + x)
                        m = pe.transpose(psum[:, 6 + n % 2, P * x:P * x + P], src[:, c:c + P], ident)
                    m.then_inc(kv_t, 1)

            def project(t, b, ts, chunk=None):
                pe.wait_ge(w_ready, t + 1)
                if ts == 0:
                    for k in range(KD):
                        pe.wait_ge(h_ready, k + 1)
                        pe.wait_ge(h_pool_ready, k + 1)
                        for g, (c0, c1) in enumerate(GROUPS):
                            m = three(bank(g, c1 - c0), w_hi[b][:, k, :], w_lo[b][:, k, :],
                                      h_hi[:, k, c0:c1], h_lo[:, k, c0:c1], k == 0, k == KD - 1)
                            if k == KD - 1:
                                m.then_inc(group_done, 1)
                    return
                for g, (c0, c1) in enumerate(GROUPS):
                    pe.wait_ge(bank_free[g], t)
                    for k in range(KD):
                        m = three(bank(g, c1 - c0), w_hi[b][:, k, :], w_lo[b][:, k, :],
                                  h_hi[:, k, c0:c1], h_lo[:, k, c0:c1], k == 0, k == KD - 1)
                    m.then_inc(group_done, 1)
                    if g == 0 and V0 < ts <= Q0:
                        turn(ts - 1)
                    if g == 2 and chunk is not None:
                        pool_matmul(chunk)

            project(0, 0, 0)
            project(1, 1, 1)
            for q in range(4):
                gate_columns(q)
            with pe.Fori(1, 6) as i:
                for b in range(2):
                    project(2 * i + b, b, 2)
            project(12, 0, 12)
            with pe.Fori(0, 2) as i:
                for b in range(2):
                    project(CHUNK0 + 1 + 2 * i + b, 1 - b, 13, chunk=2 * i + b)
            for t in range(V0, Q0 + 1):
                project(t, t % 2, t, chunk=t - CHUNK0 - 1 if t <= CHUNK0 + NCH else None)
            with pe.Fori(13, 15) as i:
                for b in range(2):
                    project(2 * i + b, b, Q0 + 1)

            pe.wait_ge(tail_copied, 1)
            for m in range(2):
                pe.transpose(psum[0:15, 5, P * m:P * m + P], tail_u[:, m, :], ident)
                last = pe.transpose(psum[0:2, 5, 256 + P * m:256 + P * m + P], tail_z[:, m, :], ident)
            last.then_inc(tail_t, 1)

            pe.wait_ge(bank_free[4], NT)
            for x in range(0, len(ZN_TILES), 4):
                if x >= 8:
                    pe.wait_ge(zs_copied, x // 4 - 1)
                for y, t in enumerate(ZN_TILES[x:x + 4]):
                    m = pe.transpose(psum[0:NS, 6 + x // 4 % 2, P * y:P * y + P], zs_t[:, t, :], ident)
                m.then_inc(zs_t_done, 1)

            for g in range(4):
                pe.wait_ge(bank_free[g], NT)

            def scores(base, n, u, i):
                if u.kind and u.i == 0:
                    pe.wait_ge(swa_loaded, 16 * SWA_DMAS * (i + 1))
                if n == 0 and u.c:
                    for j in range(4):
                        pe.wait_ge(piece_loaded[j], 16 * PIECE_DMAS * (i + 1))
                if not u.kind and u.c == 0 and u.i % 4 == 0:
                    pe.wait_ge(piece_loaded[u.i // 4], 16 * PIECE_DMAS * (i + 1))
                if n >= 2:
                    pe.wait_ge(x_ready, base + n - 1)
                for h in range(2):
                    out = psum[:, S_BANK + n % 2, 256 * h:256 * h + 256]
                    pe.matmul(out, u.q(h), u.keys(kh_st, h), start=True, stop=False)
                    m = pe.matmul(out, u.q(h), u.keys(kl_st, h), start=False, stop=True)
                m.then_inc(s_done, 1)

            def turn_probs(base, n, u):
                pe.wait_ge(p_ready, base + n + 1)
                if n >= 2:
                    pe.wait_ge(pt_copied, base + n - 1)
                for h in range(2):
                    for c, _ in u.halves():
                        k = 2 * h + (c // P if u.full else 0)
                        m = pe.transpose(psum[:, PT_BANK + n % 2, P * k:P * k + P], probs[n % 4][:, h, c:c + P], ident)
                m.then_inc(pt_done, 1)

            def weigh_values(i, base, gbase, n, u):
                g = n // 4
                if n == 0:
                    pe.wait_ge(zs_copied, 6)
                if not u.kind and u.c and u.i == 0:
                    pe.wait_ge(vd_loaded[u.c], 16 * (4 if u.c == 1 else 1) * (i + 1))
                pe.wait_ge(pt_copied, base + n + 1)
                if n % 4 == 0 and g >= 2:
                    pe.wait_ge(ot_copied, gbase + g - 1)
                for h in range(2):
                    hs = u.halves()
                    for x, (c, back) in enumerate(hs):
                        k = 2 * h + x
                        m = pe.matmul(psum[64 * h:64 * h + 64, OT_BANK + g % 2, P * (n % 4):P * (n % 4) + P],
                                      u.v(h, back), probs_t[n % 2][:, k, :], start=(x == 0), stop=(x == len(hs) - 1))
                m.then_inc(pv_done, 1)

            def turn_out(gbase, g):
                pe.wait_ge(ot_copied, gbase + g + 1)
                if g:
                    pe.wait_ge(o_copied, gbase + g)
                for x in range(4):
                    m = pe.transpose(psum[:, ON_BANK, P * x:P * x + P], o_t[:, x, :], ident)
                m.then_inc(o_turned, 1)

            def decode(s):
                if s == 4:
                    pe.wait_ge(dec_s_ready, 2)
                    for c in range(3):
                        pe.transpose(psum[0:48, DEC_BANK, P * c:P * c + P], dec_s[:, c, :], ident)
                    pe.transpose(psum[0:48, DEC_BANK, 384:408], dec_s4[:], ident[0:24, 0:24]).then_inc(dec_st, 1)
                if s == 12:
                    pe.wait_ge(dec_exp, 1)
                    pe.transpose(psum[0:32, DEC_BANK, 0:P], dec_ss[:], ident)
                    pe.transpose(psum[0:32, DEC_BANK, P:136], dec_ss4[:], ident[0:NS, 0:NS]).then_inc(dec_st, 1)
                if s == 22:
                    pe.wait_ge(dec_pn, 1)
                    pe.wait_ge(dec_exp, 2)
                    for c in range(3):
                        pe.transpose(psum[:, DEC_BANK, 48 * c:48 * c + 48], dec_p[:, P * c:P * c + P], ident[0:48, 0:48])
                    pe.transpose(psum[0:24, DEC_BANK, 144:192], dec_p[:, 384:408], ident[0:48, 0:48]).then_inc(
                        dec_pt_done, 1)
                if s == 30:
                    pe.wait_ge(dec_pt_ready, 1)
                    pe.wait_ge(dec_pn, 2)
                    pe.transpose(psum[:, DEC_BANK, 0:32], dec_ps[:, 0:P], ident[0:32, 0:32])
                    pe.transpose(psum[0:NS, DEC_BANK, 32:64], dec_ps[:, P:136], ident[0:32, 0:32]).then_inc(
                        dec_pt_done, 1)
                if 36 <= s < 36 + 2 * NS and s % 2 == 0:
                    b = (s - 36) // 2
                    if b == 0:
                        pe.wait_ge(dec_pt_ready, 2)
                    for c in range(3):
                        pe.wait_ge(dec_v_loaded[c], 16 * (b + 1))
                        pe.matmul(psum[0:48, DEC_BANK, 0:384], dec_pz[:, c, 48 * b:48 * b + 48], dec_v[c][:],
                                  start=(b == 0 and c == 0), stop=False).then_inc(dec_pv, 1)
                    pe.wait_ge(dec_sv_loaded[b % 2], 16 * (b // 2 + 1))
                    pe.matmul(psum[64:96, DEC_BANK, 384:512], dec_psz[:, 32 * b:32 * b + 32], dec_sv[b % 2][:],
                              start=(b == 0), stop=False).then_inc(dec_pv, 1)

            def attend(i, us):
                base, gbase, n = 64 * i, 16 * i, len(us)
                for s in range(n + OUT_LAG + 1 - 4):
                    if len(us) < len(units):
                        decode(s)
                    if s < n:
                        scores(base, s, us[s], i)
                    if TURN_LAG <= s < n + TURN_LAG:
                        turn_probs(base, s - TURN_LAG, us[s - TURN_LAG])
                    if PV_LAG <= s < n + PV_LAG:
                        weigh_values(i, base, gbase, s - PV_LAG, us[s - PV_LAG])
                    if s >= OUT_LAG and (s - OUT_LAG) % 4 == 0:
                        turn_out(gbase, (s - OUT_LAG) // 4)

            rounds(pe, attend)

            pe.wait_ge(o_copied, UNITS // 4)
            for n in range(2):
                m = pe.matmul(bank(n), consts[0:NS + 1, C_SELP:C_SELP + P], mod_gate[:, 512 * n:512 * n + 512],
                              start=True, stop=True)
            m.then_inc(gate_bc, 1)

            def turn_mix(j):
                pe.wait_ge(mixed, j + 1)
                for m in range(5):
                    mm = pe.transpose(psum[:, 4 + m // 4, (m % 4) * P:(m % 4 + 1) * P], o_mix[:, m * P:m * P + P], ident)
                mm.then_inc(mix_t, 1)

            def out_half(b, n):
                for k in range(Y):
                    c = slice(512 * n, 512 * n + 512)
                    m = three(bank(2 * b + n), y_hi[b][:, k, :], y_lo[b][:, k, :], wo_hi[:, k, c], wo_lo[:, k, c],
                              k == 0, k == Y - 1)
                return m

            def out_step(j, b, turn, first):
                pe.wait_ge(y_split, j + 1)
                if not first:
                    pe.wait_ge(res_gated, j - 1)
                out_half(b, 0)
                if turn:
                    turn_mix(j + 1)
                out_half(b, 1).then_inc(out_mm, 1)

            turn_mix(0)
            pe.wait_ge(wo_split, Y)
            pe.wait_ge(gate_bc_read, 1)
            out_step(0, 0, True, True)
            pe.wait_ge(dec_tail_loaded, 16 * DEC_TAIL_LOADS)
            pe.matmul(psum[0:48, DEC_BANK, 0:384], dec_pt4[:], dec_vn[:], start=False, stop=True)
            pe.matmul(psum[64:96, DEC_BANK, 384:512], dec_pst4[:], dec_svn[:], start=False, stop=True).then_inc(
                dec_o_done, 1)
            out_step(1, 1, True, True)
            pe.wait_ge(dec_diff, 1)
            for m in range(2):
                pe.matmul(psum[:, 6, NS * m:NS * m + NS], pool_w_sb[:, m, :], dec_a[:, m, :], start=True, stop=True)
            pe.wait_ge(dec_masked, 1)
            for m in range(5):
                src, sel = ((dec_m6, consts[0:48, C_S6:C_S6 + NS]) if m < 3 else (dec_m4, consts[64:96, C_S4:C_S4 + NS]))
                x = 2 * m if m < 3 else 2 * (m - 3)
                mm = pe.matmul(psum[:, 6, NS * (2 + m):NS * (3 + m)], src[:, x:x + 2, :].rearrange("p h e -> p (h e)"), sel,
                               start=True, stop=True)
            mm.then_inc(dec_sel, 1)
            with pe.Fori(1, 7) as i:
                for b in range(2):
                    out_step(2 * i + b, b, True, False)
            out_step(14, 0, True, False)
            pe.wait_ge(dec_y_ready, 2)
            for n in range(2):
                for k in range(Y):
                    c = slice(512 * n, 512 * n + 512)
                    m = three(psum[0:NS, 6 + n, :], ys_hi[:, k, :], ys_lo[:, k, :], wo_hi[:, k, c], wo_lo[:, k, c], k == 0, k == Y - 1)
            m.then_inc(dec_mm, 1)
            out_step(15, 1, False, False)

        @block.scalar
        def _(act):
            act.wait_ge(const_loaded, 16 * 2)
            nc.scalar.activation(c_silu[:], c_sb[:], ACT.Silu).then_inc(c_ready, 1)

            def x_round(j, first):
                for i in range(4):
                    act.wait_ge(x_loaded[i], 16 * (j + 1))
                    if not (first and i == 0):
                        act.wait_ge(sumsq, 4 * j + i)
                    nc.scalar.activation(junk[:], x_in[i][:], ACT.Square, accum_out=small[:, i:i + 1]).then_inc(sumsq, 1)
                    act.wait_ge(sumsq, 4 * j + i + 1)
                    nc.scalar.activation(small[:, 8 + i:9 + i], small[:, i:i + 1], ACT.Sqrt, scale=1.0 / D, bias=eps).then_inc(
                        std_ready, 1)
                    if i >= 2:
                        x = 2 * (i - 2)
                        act.wait_ge(xt_ready, 4 * j + x + 1)
                        nc.scalar.copy(h_f32[:, :, bass.ds(512 * j + P * x, P)],
                                       psum[:, 0:2, :].rearrange("p b (k t) -> p (b k) t", t=P)).then_inc(xt_copied[0], 1)

            x_round(0, True)
            with act.Fori(1, 4) as j:
                x_round(j, False)
            def split_w(t, half, ts):
                b = ts % 2
                act.wait_ge(w_loaded[b], 16 * (half + 1))
                if ts >= 2:
                    act.wait_ge(group_done, 5 * (t - 1))
                nc.scalar.copy(w_hi[b][:], w_raw[b][:]).then_inc(w_hi_ready, 1)

            act.wait_ge(xs_loaded, 16)
            act.wait_ge(sumsq, 16)
            nc.scalar.activation(junk[0:NS, :], x_in[0][0:NS, :], ACT.Square, accum_out=small[0:NS, 0:1]).then_inc(sumsq, 1)
            act.wait_ge(sumsq, 17)
            nc.scalar.activation(small[0:NS, 8:9], small[0:NS, 0:1], ACT.Sqrt, scale=1.0 / D, bias=eps[0:NS]).then_inc(
                std_ready, 1)
            split_w(0, 0, 0)
            act.wait_ge(xt_ready, 17)
            nc.scalar.copy(h_f32[:, :, T:TT], psum[:, 0, 0:NS * KD].rearrange("p (k s) -> p k s", s=NS)).then_inc(
                xt_copied[0], 1)

            act.wait_ge(mod_done, 1)
            act.wait_ge(xt_copied[1], 8)
            for k in range(KD):
                m = nc.scalar.activation(h_hi[:, k, 0:T], h_f32[:, k, 0:T], ACT.Identity, scale=mod_scale[:, k, NS:NS + 1],
                                         bias=mod_shift[:, k, NS:NS + 1])
                if k == 0:
                    act.wait_ge(h_aff, 1)
                    m = nc.scalar.copy(h_hi[:, :, T:TT], h_f32[:, :, T:TT])
                m.then_inc(h_hi_ready, 1)

            def nat(n):
                act.wait_ge(kv_t, n + 1)
                if n >= 2:
                    act.wait_ge(nat_stored[n % 2], nat_stores(n))
                nc.scalar.copy(kv_nat[n % 2][:], bank(6 + n % 2).rearrange("p (x c) -> p x c", c=P)).then_inc(nat_copied, 1)

            def evac(t, half, ts, kind):
                b = ts % 2
                if ts + 1 < NT:
                    split_w(t + 1, half + ts % 2, ts + 1)
                for n, g in turns(ts - 1) if ts >= 12 else ():
                    nat(n)
                if kind == "plain":
                    return
                if ts >= 12:
                    main_free(act, ts)
                elif ts >= 2:
                    act.wait_ge(main_stored[b], 16 * half)
                for g, (c0, c1) in enumerate(GROUPS):
                    n = min(c1, T) - c0
                    act.wait_ge(group_done, 5 * t + g + 1)
                    if kind == "gate":
                        m = nc.scalar.activation(main[b][:, c0:c0 + n], bank(g, n), ACT.Silu)
                        m.then_inc(act_evac if g == 4 else bank_free[g], 1)
                    else:
                        nc.scalar.activation(main_hi[b][:, c0:c0 + n], bank(g, n), ACT.Copy,
                                             scale=-0.125 if kind == "q" else 1.0).then_inc(act_evac, 1)

            walk(act, evac)

            def weights(k):
                act.wait_ge(wo_loaded[k % 2], 16 * (k // 2 + 1))
                nc.scalar.copy(wo_hi[:, k, :], wo_raw[k % 2][:]).then_inc(wo_hi_ready, 1)

            def decode(s):
                if s == 10:
                    act.wait_ge(dec_neg, 1)
                    nc.scalar.activation(dec_p[:], psum[0:48, DEC_BANK, 0:408], ACT.Exp, bias=dec_small[0:48, 0:1],
                                         accum_out=dec_small[0:48, 1:2]).then_inc(dec_exp, 1)
                if s == 18:
                    act.wait_ge(dec_neg, 2)
                    nc.scalar.activation(dec_small[0:32, 6:7], sink_col[:], ACT.Exp, bias=dec_small[0:32, 4:5])
                    nc.scalar.activation(dec_ps[:], psum[0:32, DEC_BANK, 0:136], ACT.Exp, bias=dec_small[0:32, 4:5],
                                         accum_out=dec_small[0:32, 5:6]).then_inc(dec_exp, 1)

            def attend(i, us):
                base, gbase, n = 64 * i, 16 * i, len(us)
                for s in range(n + OUT_LAG + 2 - 4):
                    if len(us) < len(units):
                        decode(s)
                        if s == 2:
                            act.wait_ge(pv_done, 128)
                        if s % 2 == 0 and 8 <= s <= 2 * Y + 6:
                            weights(s // 2 - 4)
                    if s < n:
                        u = us[s]
                        act.wait_ge(x_ready, base + s + 1)
                        if s >= 4:
                            act.wait_ge(pt_done, base + s - 3)
                        for h in range(2):
                            st = stats[s // 4 % 4]
                            m = nc.scalar.activation(probs[s % 4][:, h, u.cols()], xs_[s % 2][:, h, u.cols()], ACT.Exp,
                                                     scale=-1.0, bias=st[:, s % 4, 2 * h:2 * h + 1],
                                                     accum_out=st[:, s % 4, 2 * h + 1:2 * h + 2])
                        m.then_inc(p_ready, 1)
                    if s >= OUT_LAG - 1 and (s - OUT_LAG + 1) % 4 == 0 and (s - OUT_LAG + 1) // 4 < n // 4:
                        copy_ot(base, gbase, (s - OUT_LAG + 1) // 4)
                    if s >= OUT_LAG + 1 and (s - OUT_LAG - 1) % 4 == 0:
                        copy_o(i, gbase, (s - OUT_LAG - 1) // 4)

            def copy_ot(base, gbase, g):
                act.wait_ge(pv_done, base + 4 * g + 4)
                if g:
                    act.wait_ge(o_turned, gbase + g)
                nc.scalar.copy(o_t[:], bank(OT_BANK + g % 2).rearrange("p (x q) -> p x q", q=P)).then_inc(ot_copied, 1)

            def copy_o(i, gbase, g):
                act.wait_ge(mix_stored[g % 4], 16 * (4 * i + g // 4 + 1))
                nc.scalar.copy(o_st[g % 4][:, :, P:132], stats[g % 4][:])
                act.wait_ge(o_turned, gbase + g + 1)
                nc.scalar.copy(o_st[g % 4][:, :, 0:P], bank(ON_BANK).rearrange("p (x q) -> p x q", q=P)).then_inc(
                    o_copied, 1)

            rounds(act, attend)

            def out_a(j, b):
                act.wait_ge(arg_ready, j + 1)
                nc.scalar.activation(fac[:, 0:22], fac[:, 0:22], ACT.Exp).then_inc(exp_ready, 1)

            def out_b(j, b, first):
                act.wait_ge(yt_ready, j + 1)
                if not first:
                    act.wait_ge(out_mm, j - 1)
                nc.scalar.copy(y_hi[b][:], y_t[b][:]).then_inc(yh_ready, 1)

            def out_c(j, b):
                act.wait_ge(res_ready, j + 1)
                nc.scalar.activation(junk_o[:], resid[b][:], ACT.Square, accum_out=fin[:, b:b + 1]).then_inc(sq_ready, 1)
                act.wait_ge(sq_ready, j + 1)
                nc.scalar.activation(fin[:, 4 + b:5 + b], fin[:, b:b + 1], ACT.Sqrt, scale=1.0 / D, bias=eps).then_inc(
                    fstd_ready, 1)

            nc.scalar.activation(dec_g[:], zs_t[:, GATE0:V0, :], ACT.Silu).then_inc(dec_gate, 1)
            out_a(0, 0)
            for b in range(2):
                out_b(b, b, True)
                out_a(b + 1, 1 - b)
            with act.Fori(1, 7) as i:
                for b in range(2):
                    out_b(2 * i + b, b, False)
                    out_a(2 * i + b + 1, 1 - b)
                    out_c(2 * i + b - 2, b)
            act.wait_ge(dec_y_full, 1)
            nc.scalar.copy(ys_hi[:], dec_y[:]).then_inc(dec_y_ready, 1)
            out_b(14, 0, False)
            out_a(15, 1)
            out_c(12, 0)
            out_b(15, 1, False)
            out_c(13, 1)
            out_c(14, 0)
            act.wait_ge(dec_res, 1)
            nc.scalar.activation(dec_junk[:], dec_r[:], ACT.Square, accum_out=dec_small[0:NS, 8:9]).then_inc(
                dec_sq_ready, 1)
            act.wait_ge(dec_sq_ready, 1)
            nc.scalar.activation(dec_small[0:NS, 10:11], dec_small[0:NS, 8:9], ACT.Sqrt, scale=1.0 / D,
                                 bias=eps[0:NS]).then_inc(dec_std, 1)
            out_c(15, 1)

        @block.vector
        def _(dve):
            links = [0]

            def link(ins):
                links[0] += 1
                ins.then_inc(dve_link, 1)
                dve.wait_ge(dve_link, links[0])

            def x_round(j, first):
                def turned(i):
                    dve.wait_ge(xt_ready, 4 * j + i + 1)
                    dve.tensor_copy(h_f32[:, :, bass.ds(512 * j + P * i, P)],
                                    psum[:, 2:4, :].rearrange("p b (k t) -> p (b k) t", t=P)).then_inc(xt_copied[1], 1)

                for i in range(4):
                    dve.wait_ge(std_ready, 4 * j + i + 1)
                    dve.reciprocal(small[:, 12 + i:13 + i], small[:, 8 + i:9 + i]).then_inc(rstd_ready, 1)
                    dve.wait_ge(rstd_ready, 4 * j + i + 1)
                    dve.tensor_scalar(x_in[i][:], x_in[i][:], small[:, 12 + i:13 + i], None, ALU.mult).then_inc(
                        xn_ready, 1)
                    if i == 2:
                        if not first:
                            mod_add(j - 1)
                        turned(1)
                turned(3)

            def mod_add(j):
                dve.wait_ge(mod_mm, j + 1)
                dve.tensor_tensor(mod_sb[:, bass.ds(512 * j, 512)], psum[0:NS + 1, 4, :],
                                  b_mod[:, bass.ds(512 * j, 512)], ALU.add).then_inc(mod_added, 1)

            dve.wait_ge(const_loaded, 16 * 2)
            x_round(0, True)
            dve.wait_ge(small_loaded, 16 * 7)
            with dve.Fori(1, 4) as j:
                x_round(j, False)
            def split_w(t):
                b = t[1] % 2
                dve.wait_ge(w_hi_ready, t[0] + 1)
                dve.tensor_tensor(w_lo[b][:], w_raw[b][:], w_hi[b][:].bitcast(F32), ALU.subtract).then_inc(w_ready, 1)

            dve.wait_ge(std_ready, 17)
            link(dve.reciprocal(small[0:NS, 12:13], small[0:NS, 8:9]))
            dve.tensor_scalar(x_in[0][0:NS, :], x_in[0][0:NS, :], small[0:NS, 12:13], None, ALU.mult).then_inc(xn_ready, 1)
            split_w((0, 0))
            mod_add(3)
            dve.wait_ge(mod_t, 1)
            mod_ps = psum[:, 5, 0:2 * KD * (NS + 1)].rearrange("p (e n) -> p e n", n=NS + 1)
            dve.tensor_copy(mod_shift[:], mod_ps[:, 0:KD, :])
            dve.scalar_tensor_tensor(mod_scale[:], mod_ps[:, KD:2 * KD, :], 1.0,
                                     g_t[:].unsqueeze(2).broadcast_to([P, KD, NS + 1]), ALU.add, ALU.mult).then_inc(mod_done, 1)
            dve.wait_ge(mod_done, 1)
            dve.wait_ge(xt_copied[0], 9)
            dve.wait_ge(xt_copied[1], 8)
            dve_s = h_f32[:, :, T:TT]
            link(dve.tensor_tensor(dve_s, dve_s, mod_scale[:, :, 0:NS], ALU.mult))
            dve.tensor_tensor(dve_s, dve_s, mod_shift[:, :, 0:NS], ALU.add).then_inc(h_aff, 1)

            for k in range(KD):
                dve.wait_ge(h_hi_ready, k + 1)
                dve.tensor_scalar(h_f32[:, k, 0:T], h_f32[:, k, 0:T], mod_scale[:, k, NS:NS + 1],
                                  mod_shift[:, k, NS:NS + 1], ALU.mult, ALU.add).then_inc(h_aff, 1)
                dve.wait_ge(h_aff, k + 2)
                dve.tensor_tensor(h_lo[:, k, 0:POOL_FROM], h_f32[:, k, 0:POOL_FROM], h_hi[:, k, 0:POOL_FROM].bitcast(F32),
                                  ALU.subtract).then_inc(h_ready, 1)

            def chunk(n):
                if n == 0:
                    for t_, w in ((u_in, HALO), (ch_in, 2), (cc_in, 2)):
                        link(dve.memset(t_[:, :, 0:w], 0.0))
                dve.wait_ge(chunk_loaded, 80 * (n + 1))
                W = HALO + CH
                link(dve.tensor_tensor(sum_a[:, :, 1:W], u_in[:, :, 1:W], u_in[:, :, 0:W - 1], ALU.add))
                link(dve.tensor_tensor(sum_b[:, :, 3:W], sum_a[:, :, 3:W], sum_a[:, :, 1:W - 2], ALU.add))
                link(dve.tensor_tensor(sum_a[:, 1, 7:W], sum_b[:, 1, 7:W], sum_b[:, 1, 3:W - 4], ALU.add))
                link(dve.tensor_tensor(sum_b[:, 1, 15:W], sum_a[:, 1, 15:W], sum_a[:, 1, 7:W - 8], ALU.add))
                for m in range(2):
                    for half, s in ((0, sum_a), (1, sum_b)):
                        r = slice(64 * half, 64 * half + 64)
                        last = dve.scalar_tensor_tensor(diff[r, m, :], s[r, m, HALO:W], 1.0 / (2, 4, 8, 16)[2 * m + half],
                                                        u_in[r, m, HALO:W], ALU.mult, ALU.subtract)
                if n == 0:
                    link(last)
                    for half, s in ((0, sum_a), (1, sum_b)):
                        r = slice(64 * half, 64 * half + 64)
                        rc = consts[r, C_RCF:C_RCF + 32].rearrange("p (m t) -> p m t", m=2)
                        link(dve.tensor_tensor(s[r, :, 0:16], s[r, :, HALO:HALO + 16], rc, ALU.mult))
                        last = dve.tensor_tensor(diff[r, :, 0:16], s[r, :, 0:16], u_in[r, :, HALO:HALO + 16], ALU.subtract)
                last.then_inc(diff_ready, 1)
                link(dve.tensor_tensor(ch_in[:], ch_in[:], cc_in[:], ALU.mult))
                for m in range(2):
                    for j in range(3):
                        z = ch_in[:, m, j:j + CH]
                        wj = conv_w_t[:, m, j:j + 1]
                        acc = cc_in[:, m, 0:CH]
                        if j == 0:
                            ins = dve.tensor_scalar(acc, z, wj, None, ALU.mult)
                        else:
                            ins = dve.scalar_tensor_tensor(acc, z, wj, acc, ALU.mult, ALU.add)
                        link(ins)
                link(dve.tensor_tensor(cc_in[:, :, 0:CH], cc_in[:, :, 0:CH], cb_in[:], ALU.mult))
                if n:
                    dve.wait_ge(yac_stored, 16 * n)
                dve.tensor_tensor(yac[:, 2:4, :], cc_in[:, :, 0:CH], gate_in[:, 2:4, :], ALU.mult)
                if n == NCH - 1:
                    dve.tensor_copy(tail_u[:], u_in[:, :, HALO + CH - 15:HALO + CH])
                    dve.tensor_copy(tail_z[:], ch_in[:, :, CH:CH + 2]).then_inc(tail_copied, 1)
                dve.wait_ge(pool_mm, n + 1)
                for m in range(2):
                    last = dve.scalar_tensor_tensor(yac[:, m, :], psum[:, 5, CH * m:CH * m + CH], pool_scale_t[:, m:m + 1],
                                                    gate_in[:, m, :], ALU.mult, ALU.mult)
                last.then_inc(yac_ready, 1)

            def evac(t, half, ts, kind):
                b = ts % 2
                if ts + 1 < NT:
                    split_w((t + 1, ts + 1))
                if kind == "plain" and ts >= 12:
                    main_free(dve, ts)
                elif kind == "plain" and ts >= 2:
                    dve.wait_ge(main_stored[b], 16 * half)
                if ts == K0:
                    dve.wait_ge(yac_stored, 16 * NCH)
                if ts >= K0 + 2:
                    dve.wait_ge(lo_stored[b], 32 * ((ts - K0) // 2))
                if K0 < ts < Q0:
                    dve.wait_ge(kv_t, turns(ts - 1)[-1][0] + 1)
                for g, (c0, c1) in enumerate(GROUPS):
                    n = min(c1, T) - c0
                    if kind == "plain":
                        dve.wait_ge(group_done, 5 * t + g + 1)
                        last = dve.tensor_copy(main[b][:, c0:c0 + n], bank(g, n))
                    elif kind == "gate":
                        if g < 4:
                            continue
                        dve.wait_ge(act_evac, t - GATE0 + 1)
                    else:
                        dve.wait_ge(act_evac, V0 - GATE0 + 5 * (ts - K0) + g + 1)
                        last = dve.scalar_tensor_tensor(main_lo[b][:, c0:c0 + n], bank(g, n),
                                                        -0.125 if kind == "q" else 1.0,
                                                        main_hi[b][:, c0:c0 + n].bitcast(F32), ALU.mult, ALU.subtract)
                        if kind == "k":
                            last = dve.tensor_copy(k_nat[:, c0:c0 + n], bank(g, n))
                    if g == 4:
                        dve.tensor_copy(zs_t[:, bass.ds(t, 1), :].rearrange("p a s -> p (a s)"),
                                        psum[:, g, n:n + NS]).then_inc(bank_free[g], 1)
                    else:
                        last.then_inc(bank_free[g], 1)
                if 0 <= ts - CHUNK0 < NCH:
                    chunk(ts - CHUNK0)
                if ts == 1:
                    for q in range(4):
                        dve.wait_ge(gate_mm, q + 1)
                        dve.tensor_tensor(mod_gate[:, 256 * q:256 * q + 256], psum[0:NS + 1, 5, 0:256],
                                          b_gate[:, 256 * q:256 * q + 256], ALU.add).then_inc(gate_added, 1)

            walk(dve, evac)

            for x in range(0, len(ZN_TILES), 4):
                dve.wait_ge(zs_t_done, x // 4 + 1)
                n = P * min(4, len(ZN_TILES) - x)
                dve.tensor_copy(zn[:, P * x:P * x + n], psum[0:NS, 6 + x // 4 % 2, 0:n]).then_inc(zs_copied, 1)
            dve.wait_ge(tail_t, 1)
            dve.tensor_copy(tail_rows[:, 0:256], psum[0:15, 5, 0:256])
            dve.tensor_copy(tail_rows[0:2, 256:512], psum[0:2, 5, 256:512]).then_inc(zs_copied, 1)
            dve.wait_ge(zs_copied, 6)
            dve.tensor_tensor(zc_s[:], zn[:, 256:512], zn[:, 512:768], ALU.mult).then_inc(zc_ready, 1)

            dve.wait_ge(lo_stored[0], 32 * 4)
            dve.wait_ge(kv_t, len(TURNS))
            dve.tensor_scalar(neg_sink[:], neg_sink[:], -1.0, None, ALU.mult).then_inc(sink_negated, 1)
            dve.wait_ge(sink_negated, 1)

            heads = lambda ap, n: ap.rearrange("p (s h) -> p s h", h=n)

            def window_logits(half):
                prod = dec_prod[:, 0:1024]
                part = slice(16 * half, 16 * half + 16)
                link(dve.tensor_tensor(prod.rearrange("p (y x e) -> p y x e", x=2, e=64),
                                       dec_sq[:, 1024 * half:1024 * half + 1024].rearrange("p (y x e) -> p y x e", x=2, e=64),
                                       dec_sk[:, 8 * half:8 * half + 8, :].unsqueeze(2).broadcast_to([P, 8, 2, 64]), ALU.mult))
                link(dve.tensor_reduce(dec_ss[:, part], prod.rearrange("p (x e) -> p x e", e=64), AX.X, ALU.add))
                v = heads(dec_ss[:, part], 4)
                dve.scalar_tensor_tensor(v, v, 0.125, consts[:, C_SB:C_SB + 4].unsqueeze(1).broadcast_to([P, NS // 2, 4]),
                                         ALU.mult, ALU.add)

            def new_logits():
                for own, full, q, k, rows, n in ((dec_own, dec_s4, dec_qn[:], dec_kn[:], 24, NHD),
                                                 (dec_sown, dec_ss4, dec_sqn[:],
                                                  dec_skn[:].rearrange("s g x e -> s (g x e)"), NS, NHS)):
                    pr = dec_prod[0:rows, 0:64 * n]
                    link(dve.tensor_tensor(pr, q, k, ALU.mult))
                    link(dve.tensor_reduce(own[:], pr.rearrange("p (x e) -> p x e", e=64), AX.X, ALU.add))
                    last = dve.scalar_tensor_tensor(
                        heads(full[:], n), own[:].unsqueeze(1).broadcast_to([rows, NS, n]), 0.125,
                        consts[0:rows, C_NEW:C_NEW + NS].unsqueeze(2).broadcast_to([rows, NS, n]), ALU.mult, ALU.add)
                last.then_inc(dec_s_ready, 1)

            def row_logits(i, x):
                n = NS // 2 * i + x
                dve.wait_ge(dec_loaded, 16 * DEC_LOADS)
                dve.wait_ge(dec_k_loaded[x % 2], 48 * (2 * i + x // 2 + 1))
                prod = dec_prod[:].rearrange("p (c e) -> p c e", c=3)
                dve.tensor_tensor(prod, dec_k[x % 2][:], dec_q[:, bass.ds(n, 1), :].broadcast_to([P, 3, 384]),
                                  ALU.mult).then_inc(dec_link, 1)
                dve.wait_ge(dec_link, ROW_LINKS * n + 1)
                dve.tensor_reduce(dec_red[:], prod.rearrange("p c (h e) -> p c h e", e=64), AX.X, ALU.add).then_inc(
                    dec_link, 1)
                dve.wait_ge(dec_link, ROW_LINKS * n + 2)
                dve.scalar_tensor_tensor(dec_s[:, :, bass.ds(6 * n, 6)], dec_red[:], 0.125,
                                         consts[:, C_DB:C_DB + 18].rearrange("p (c h) -> p c h", c=3),
                                         ALU.mult, ALU.add).then_inc(dec_link, 1)

            def decode(s):
                if s == 0:
                    dve.wait_ge(dec_link, ROW_LINKS * NS)
                    dve.sem_inc(dec_s_ready, 1)
                    dve.wait_ge(lo_stored[1], 32 * 5)
                if s < 2:
                    window_logits(s)
                if s == 2:
                    new_logits()
                if s == 8:
                    dve.wait_ge(dec_st, 1)
                    dve.tensor_reduce(dec_small[0:48, 0:1], psum[0:48, DEC_BANK, 0:408], AX.X, ALU.max,
                                      negate=True).then_inc(dec_neg, 1)
                if s == 13:
                    dve.wait_ge(dec_exp, 1)
                    link(dve.reciprocal(dec_small[0:48, 2:3], dec_small[0:48, 1:2]))
                    dve.tensor_scalar(dec_p[:], dec_p[:], dec_small[0:48, 2:3], None, ALU.mult).then_inc(dec_pn, 1)
                if s == 16:
                    dve.wait_ge(dec_st, 2)
                    link(dve.tensor_reduce(dec_small[0:32, 4:5], psum[0:32, DEC_BANK, 0:136], AX.X, ALU.max, negate=True))
                    link(dve.tensor_scalar(dec_small[0:32, 7:8], sink_col[:], -1.0, None, ALU.mult))
                    dve.tensor_tensor(dec_small[0:32, 4:5], dec_small[0:32, 4:5], dec_small[0:32, 7:8], ALU.min).then_inc(
                        dec_neg, 1)
                if s == 21:
                    dve.wait_ge(dec_exp, 2)
                    link(dve.tensor_tensor(dec_small[0:32, 5:6], dec_small[0:32, 5:6], dec_small[0:32, 6:7], ALU.add))
                    link(dve.reciprocal(dec_small[0:32, 5:6], dec_small[0:32, 5:6]))
                    dve.tensor_scalar(dec_ps[:], dec_ps[:], dec_small[0:32, 5:6], None, ALU.mult).then_inc(dec_pn, 1)
                if s == 27:
                    dve.wait_ge(wo_split, Y)
                    dve.memset(dec_psz[:], 0.0)
                    link(dve.memset(dec_pz[:], 0.0))
                own = lambda ap, n: ap.rearrange("p (s x) -> p s x", s=NS)[:, :, 0:n]
                if s == 28:
                    dve.wait_ge(dec_pt_done, 1)
                    for c in range(3):
                        dve.tensor_copy(own(dec_pz[:, c, :], 6), heads(psum[:, DEC_BANK, 48 * c:48 * c + 48], 6))
                    dve.tensor_copy(dec_pt4[:], psum[0:24, DEC_BANK, 144:192]).then_inc(dec_pt_ready, 1)
                if s == 32:
                    dve.wait_ge(dec_pt_done, 2)
                    dve.tensor_copy(own(dec_psz[:], 4), heads(psum[:, DEC_BANK, 0:32], 4))
                    dve.tensor_copy(dec_pst4[:], psum[0:NS, DEC_BANK, 32:64]).then_inc(dec_pt_ready, 1)

            def pair_tables(i, kind):
                off = consts[:, C_OFF:C_OFF + 256]
                for h in range(2):
                    if kind and h == 0:
                        dve.wait_ge(lo_stored[1], 32 * 5)
                    if kind == 0:
                        slope = consts[:, bass.ds(C_SLD + 2 * i + h, 1)]
                        for c, d in enumerate(DILATIONS):
                            last = dve.tensor_scalar(bias_dil[:, c, h, :], off, slope, float(d), ALU.mult, ALU.mult)
                    else:
                        slope = consts[:, bass.ds(C_SLS + 2 * i + h, 1)]
                        last = dve.tensor_scalar(bias_swa[:, h, :], off, slope, None, ALU.mult)
                if kind:
                    last = dve.tensor_copy(sink_now[:], neg_sink[:, bass.ds(2 * i, 2)])
                last.then_inc(bias_ready, 1)
                dve.wait_ge(bias_ready, 2 * i + kind + 1)

            def weights(k):
                dve.wait_ge(wo_hi_ready, k + 1)
                dve.tensor_tensor(wo_lo[:, k, :], wo_raw[k % 2][:], wo_hi[:, k, :].bitcast(F32), ALU.subtract).then_inc(
                    wo_split, 1)

            def attend(i, us):
                base, gbase, n = 64 * i, 16 * i, len(us)
                for s in range(n + COPY_LAG):
                    if len(us) < len(units):
                        if s % 2 == 0 and 10 <= s <= 2 * Y + 8:
                            weights(s // 2 - 5)
                        decode(s)
                    elif s in ROW_STEPS:
                        row_logits(i, ROW_STEPS.index(s))
                    if s >= COPY_LAG:
                        m = s - COPY_LAG
                        u = us[m]
                        dve.wait_ge(pt_done, base + m + 1)
                        if m >= 2:
                            dve.wait_ge(pv_done, base + m - 1)
                        src = bank(PT_BANK + m % 2).rearrange("p (k q) -> p k q", q=P)
                        dst = probs_t[m % 2]
                        if u.full:
                            dve.tensor_copy(dst[:], src).then_inc(pt_copied, 1)
                        else:
                            dve.tensor_copy(dst[:, 0:4:2, :], src[:, 0:4:2, :]).then_inc(pt_copied, 1)
                    if s < n:
                        u = us[s]
                        g = s // 4
                        if s == 0 or u.kind and u.i == 0:
                            pair_tables(i, u.kind)
                        dve.wait_ge(s_done, base + s + 1)
                        if s >= 2:
                            dve.wait_ge(p_ready, base + s - 1)
                        dve.sem_inc(unit_open, 1)
                        for h in range(2):
                            c = u.cols()
                            m = dve.tensor_tensor_reduce(
                                out=xs_[s % 2][:, h, c], in0=psum[:, S_BANK + s % 2, 256 * h + c.start:256 * h + c.stop],
                                in1=u.bias(h), scale=1.0, scalar=sink_now[:, h:h + 1] if u.kind else 3.0e38,
                                op0=ALU.add, op1=ALU.min,
                                accum_out=stats[g % 4][:, s % 4, 2 * h:2 * h + 1])
                        m.then_inc(x_ready, 1)

            rounds(dve, attend)

            LINKS = 10

            def combine(j, half, b, first):
                n = [0]

                def olink(ins):
                    n[0] += 1
                    ins.then_inc(out_link, 1)
                    dve.wait_ge(out_link, LINKS * j + n[0])

                dve.wait_ge(tile_in[b], 32 * (half + 1))
                st = mix_in[b][:, :, :, P:132].rearrange("p c j (h s) -> p c j h s", s=2)
                ss = swa_in[b][:, :, P:132].rearrange("p j (h s) -> p j h s", s=2)
                v6 = lambda a: fac[:, a:a + 6].rearrange("p (j h) -> p j h", h=2)
                v4 = lambda a: fac[:, a:a + 4].rearrange("p (j h) -> p j h", h=2)
                olink(dve.tensor_tensor(v6(24), st[:, 0, :, :, 0], st[:, 1, :, :, 0], ALU.min))
                olink(dve.tensor_tensor(v6(24), v6(24), st[:, 2, :, :, 0], ALU.min))
                for c in range(3):
                    dve.tensor_tensor(v6(6 * c), v6(24), st[:, c, :, :, 0], ALU.subtract)
                sinks = neg_sink[:].rearrange("p (j h) -> p j h", h=2)
                dve.tensor_tensor(v4(18), ss[:, :, :, 0], sinks, ALU.subtract).then_inc(arg_ready, 1)
                dve.wait_ge(exp_ready, j + 1)
                for c in range(3):
                    last = dve.tensor_tensor(v6(30 + 6 * c), v6(6 * c), st[:, c, :, :, 1], ALU.mult)
                olink(last)
                olink(dve.tensor_tensor(v6(48), v6(30), v6(36), ALU.add))
                dve.tensor_tensor(v6(48), v6(48), v6(42), ALU.add)
                olink(dve.tensor_tensor(v4(54), v4(18), ss[:, :, :, 1], ALU.add))
                olink(dve.reciprocal(fac[:, 48:58], fac[:, 48:58]))
                olink(dve.tensor_tensor(fac[:, 0:18].rearrange("p (c x) -> p c x", c=3),
                                        fac[:, 0:18].rearrange("p (c x) -> p c x", c=3),
                                        fac[:, 48:54].unsqueeze(1).broadcast_to([P, 3, 6]), ALU.mult))
                if not (first and b == 0):
                    dve.wait_ge(mix_t, j)
                src = lambda c: mix_in[b][:, c, :, 0:P].rearrange("p j (h e) -> p j h e", e=64)
                f = lambda a: fac[:, a:a + 6].rearrange("p (j h) -> p j h", h=2).unsqueeze(3).broadcast_to([P, 3, 2, 64])
                om = o_mix[:, 0:384].rearrange("p (j h e) -> p j h e", h=2, e=64)
                op_ = o_part[:].rearrange("p (j h e) -> p j h e", h=2, e=64)
                dve.tensor_tensor(om, src(0), f(0), ALU.mult)
                dve.tensor_tensor(o_mix[:, 384:640].rearrange("p (j h e) -> p j h e", h=2, e=64),
                                  swa_in[b][:, :, 0:P].rearrange("p j (h e) -> p j h e", e=64),
                                  fac[:, 54:58].rearrange("p (j h) -> p j h", h=2).unsqueeze(3).broadcast_to([P, 2, 2, 64]),
                                  ALU.mult)
                olink(dve.tensor_tensor(op_, src(1), f(6), ALU.mult))
                olink(dve.tensor_tensor(o_mix[:, 0:384], o_mix[:, 0:384], o_part[:], ALU.add))
                olink(dve.tensor_tensor(op_, src(2), f(12), ALU.mult))
                dve.tensor_tensor(o_mix[:, 0:384], o_mix[:, 0:384], o_part[:], ALU.add).then_inc(mixed, 1)
                assert n[0] == LINKS, n[0]

            def gate_mix(j, half, b):
                dve.wait_ge(gates_in[b], 32 * (half + 1))
                dve.wait_ge(mix_t, j + 1)
                dve.tensor_tensor(y_t[b][:, 4:8, :], bank(4).rearrange("p (m t) -> p m t", t=P), gates[b][:, 0:4, :], ALU.mult)
                dve.tensor_tensor(y_t[b][:, 8, :], bank(5, P), gates[b][:, 4, :], ALU.mult).then_inc(yt_ready, 1)

            def split_y(j, b):
                dve.wait_ge(yh_ready, j + 1)
                dve.tensor_tensor(y_lo[b][:], y_t[b][:], y_hi[b][:].bitcast(F32), ALU.subtract).then_inc(y_split, 1)

            def gate_out(j, b):
                dve.wait_ge(out_mm, j + 1)
                dve.tensor_tensor(resid[b][:], psum[:, 2 * b:2 * b + 2, :].rearrange("p a c -> p (a c)"), gate_all[:],
                                  ALU.mult).then_inc(res_gated, 1)

            def final_norm(j, half, b, first):
                dve.wait_ge(fstd_ready, j + 1)
                dve.reciprocal(fin[:, 2 + b:3 + b], fin[:, 4 + b:5 + b]).then_inc(rec_ready, 1)
                dve.wait_ge(rec_ready, j + 1)
                if not first:
                    dve.wait_ge(y_stored[b], 16 * half)
                dve.scalar_tensor_tensor(y_out[b][:], resid[b][:], fin[:, 2 + b:3 + b], final_g_sb[:], ALU.mult, ALU.mult).then_inc(
                    y_ready, 1)

            def decode_branches():
                dve.wait_ge(dec_tail_loaded, 16 * DEC_TAIL_LOADS)
                u_new = zs_t[:, 0:2, :]
                for m in range(2):
                    for half in range(2):
                        w = (2, 4, 8, 16)[2 * m + half]
                        r = slice(64 * half, 64 * half + 64)
                        last = dve.tensor_reduce(dec_a[r, m, :], dec_state[r, m, :, 16 - w:15], AX.X, ALU.add)
                link(last)
                link(dve.tensor_tensor(dec_a[:], dec_a[:], u_new, ALU.add))
                for m in range(2):
                    last = dve.scalar_tensor_tensor(dec_a[:, m, :], dec_a[:, m, :], consts[:, C_INVW + m:C_INVW + m + 1],
                                                    u_new[:, m, :], ALU.mult, ALU.subtract)
                last.then_inc(dec_diff, 1)
                link(dve.tensor_tensor(dec_b[:], zs_t[:, 2:4, :], zs_t[:, 4:6, :], ALU.mult))
                for m in range(2):
                    link(dve.tensor_scalar(dec_b[:, m, :], dec_b[:, m, :], conv_w_t[:, m, 2:3], None, ALU.mult))
                    for j in (1, 0):
                        link(dve.scalar_tensor_tensor(dec_b[:, m, :], dec_conv[:, m, :, j], conv_w_t[:, m, j:j + 1],
                                                      dec_b[:, m, :], ALU.mult, ALU.add))
                link(dve.tensor_tensor(dec_b[:], dec_b[:], zs_t[:, 6:8, :], ALU.mult))
                dve.wait_ge(dec_gate, 1)
                dve.tensor_tensor(dec_y[:, 2:4, :], dec_b[:], dec_g[:, 2:4, :], ALU.mult)

            def decode_own():
                dve.wait_ge(dec_o_done, 1)
                dve.tensor_tensor(dec_m6[:], psum[0:48, DEC_BANK, 0:384].rearrange("p (h e) -> p h e", e=64),
                                  consts[0:48, C_M6:C_M6 + 6].unsqueeze(2).broadcast_to([48, 6, 64]), ALU.mult)
                dve.tensor_tensor(
                    dec_m4.rearrange("p (g x) e -> p g x e", x=2),
                    psum[64:96, DEC_BANK, 384:512].rearrange("p (g e) -> p g e", e=64).unsqueeze(2).broadcast_to([32, 2, 2, 64]),
                    consts[64:96, C_M4:C_M4 + 4].rearrange("p (g x) -> p g x", x=2).unsqueeze(3).broadcast_to([32, 2, 2, 64]),
                    ALU.mult).then_inc(dec_masked, 1)

            def decode_rows():
                dve.wait_ge(dec_sel, 1)
                for m in range(2):
                    dve.scalar_tensor_tensor(dec_y[:, m, :], psum[:, 6, NS * m:NS * m + NS], pool_scale_t[:, m:m + 1],
                                             dec_g[:, m, :], ALU.mult, ALU.mult)
                dve.tensor_tensor(dec_y[:, 4:9, :], psum[:, 6, 2 * NS:7 * NS].rearrange("p (m s) -> p m s", s=NS),
                                  dec_g[:, 4:9, :], ALU.mult).then_inc(dec_y_full, 1)

            def window(i, b, first=False, more=True):
                j = 2 * i + b
                if not first or i:
                    gate_out(j - 2, b)
                    if not first or j >= 3:
                        final_norm(j - 3, i - 2 + b, 1 - b, first and j < 5)
                gate_mix(j, i, b)
                split_y(j, b)
                if more:
                    combine(j + 1, i + b, 1 - b, False)

            combine(0, 0, 0, True)
            dve.wait_ge(gate_bc, 1)
            dve.tensor_copy(gate_all[:], psum[:, 0:2, :].rearrange("p a b -> p (a b)")).then_inc(gate_bc_read, 1)
            window(0, 0, first=True)
            dve.wait_ge(fg_loaded, 16)
            decode_branches()
            window(0, 1, first=True)
            decode_own()
            window(1, 0, first=True)
            decode_rows()
            for i, b in ((1, 1), (2, 0), (2, 1)):
                window(i, b, first=True)
            with dve.Fori(3, 7) as i:
                for b in range(2):
                    window(i, b)
            dve.wait_ge(dec_y_ready, 1)
            dve.tensor_tensor(ys_lo[:], dec_y[:], ys_hi[:].bitcast(F32), ALU.subtract).then_inc(dec_y_ready, 1)
            for b in range(2):
                window(7, b, more=b == 0)
            gate_out(14, 0)
            final_norm(13, 6, 1, False)
            dve.wait_ge(dec_mm, 1)
            for n in range(2):
                c = slice(512 * n, 512 * n + 512)
                last = dve.tensor_tensor(dec_r[:, c], psum[0:NS, 6 + n, :], mod_gate[0:NS, c], ALU.mult)
            link(last)
            dve.tensor_tensor(dec_r[:], dec_r[:], dec_x[:], ALU.add).then_inc(dec_res, 1)
            dve.wait_ge(y_ready, 14)
            gate_out(15, 1)
            final_norm(14, 7, 0, False)
            final_norm(15, 7, 1, False)

            dve.wait_ge(dec_std, 1)
            link(dve.reciprocal(dec_small[0:NS, 11:12], dec_small[0:NS, 10:11]))
            dve.scalar_tensor_tensor(dec_r[:], dec_r[:], dec_small[0:NS, 11:12], dec_fg[:], ALU.mult, ALU.mult).then_inc(
                dec_out, 1)


Z_PARTS = (("pu", 256), ("pg", 256), ("dq", 384), ("dk", 384), ("dv", 384), ("dg", 384), ("ch", 256), ("cb", 256),
           ("cc", 256), ("cg", 256), ("sq", 256), ("sk", 128), ("sv", 128), ("sg", 256))
TILE_ORDER = ("pu", "ch", "cc", "cb", "pg", "cg", "dg", "sg", "dv", "sv", "dk", "sk", "dq", "sq")


def kernel(**inputs):
    import numpy as _np
    import concourse.bacc as _bacc
    from concourse import mybir as _mybir
    from concourse.bass_utils import run_bass_kernel_spmd as _run

    x = {k: _np.asarray(v) for k, v in inputs.items()}
    starts, at = {}, 0
    for n, w in Z_PARTS:
        starts[n] = at
        at += w
    widths = dict(Z_PARTS)
    w_in = _np.concatenate([x["w_in"][0][:, starts[n]:starts[n] + widths[n]] for n in TILE_ORDER], axis=1)
    w_tiles = w_in.reshape(KD, P, NT, P).transpose(2, 1, 0, 3)
    c = _np.concatenate([x["c_sample"], x["c_prompt"]], axis=0)
    pool_w = _np.zeros((P, 2, P), _np.float32)
    for g in range(4):
        r = slice(64 * (g % 2), 64 * (g % 2) + 64)
        pool_w[r, g // 2, r] = x["w_pool"][0, g]
    w_out = x["w_out"][0]
    w_out = _np.concatenate([w_out[0:256], w_out[640:896], w_out[256:640], w_out[896:1152]], axis=0)
    arrays = {
        "x_prompt": x["x_prompt"][0],
        "x_sample": x["x_sample"][:, 0],
        "c_t": c.reshape(NS + 1, KD, P).transpose(2, 1, 0),
        "w_ada": x["w_ada"][0],
        "b_ada": _np.broadcast_to(x["b_ada"], (NS + 1, 3 * D)),
        "norm_g": x["norm_g"][0].reshape(KD, P).T,
        "w_tiles": w_tiles,
        "const": constants(),
        "pool_w": pool_w,
        "pool_scale": x["pool_scale"][0].reshape(2, P).T,
        "conv_w": x["conv_w"][0].reshape(3, 2, P).transpose(2, 1, 0),
        "sink": _np.broadcast_to(x["swa_sink"], (P, NHS)),
        "sink_rows": _np.tile(x["swa_sink"][0], NS)[:, None],
        "w_out": w_out.reshape(Y, P, D).transpose(1, 0, 2),
        "final_g": _np.broadcast_to(x["final_g"], (P, D)),
        "dil_kc": x["cache_dil_k"][0].reshape(NS, 2048, NHD * 64),
        "dil_vc": x["cache_dil_v"][0].reshape(NS, 2048, NHD * 64),
        "swa_kc": x["cache_swa_k"][0].reshape(NS, P, P),
        "swa_vc": x["cache_swa_v"][0].reshape(NS, P, P),
        "pool_state": x["state_pool"][0].transpose(2, 0, 1).reshape(2, P, NS, 15).transpose(1, 0, 2, 3),
        "conv_state": x["state_conv"][0].transpose(2, 0, 1).reshape(2, P, NS, 2).transpose(1, 0, 2, 3),
        "pool_rows": x["state_pool"][0],
        "conv_rows": x["state_conv"][0],
    }
    outs = [("y_prompt", (T, D)), ("y_sample", (NS, D)), ("pool_p", (15, 256)), ("pool_s", (NS, 15, 256)),
            ("dil_k_p", (T, 384)), ("dil_v_p", (T, 384)), ("dil_k_s", (NS, 384)), ("dil_v_s", (NS, 384)),
            ("conv_p", (2, 256)), ("conv_s", (NS, 2, 256)), ("swa_k_p", (P, P)), ("swa_v_p", (P, P)),
            ("swa_k_s", (NS, P)), ("swa_v_s", (NS, P))]
    nc = _bacc.Bacc("TRN2", target_bir_lowering=False, num_devices=1)
    args = []
    for name, a in arrays.items():
        arrays[name] = a = _np.ascontiguousarray(a)
        args.append(nc.dram_tensor(name, a.shape, _mybir.dt.from_np(a.dtype), kind="ExternalInput").ap())
    for name, shape in outs:
        args.append(nc.dram_tensor(name, shape, _mybir.dt.float32, kind="ExternalOutput").ap())
    build_program(nc, *args)
    r = _run(nc, [arrays], core_ids=[0]).results[0]
    o = {name: r[name] for name, _ in outs}
    return (o["y_prompt"][None], o["y_sample"][:, None], o["pool_p"][None, None], o["pool_s"][None],
            o["dil_k_p"].reshape(1, 1, T, NHD, 64), o["dil_v_p"].reshape(1, 1, T, NHD, 64),
            o["dil_k_s"].reshape(1, NS, 1, NHD, 64), o["dil_v_s"].reshape(1, NS, 1, NHD, 64),
            o["conv_p"][None, None], o["conv_s"][None],
            o["swa_k_p"].reshape(1, 1, P, 2, 64), o["swa_v_p"].reshape(1, 1, P, 2, 64),
            o["swa_k_s"].reshape(1, NS, 1, 2, 64), o["swa_v_s"].reshape(1, NS, 1, 2, 64))
```
